# Optimizing a Trainium2 kernel written in Bass

```python
import jax, jax.numpy as jnp
from jax import lax
import numpy as np

D_MODEL = 1024
BATCH = 1
SEQ = 512
DEPTH = 1

MIX_WIDTH = D_MODEL
RET_HEADS = 4
RET_DK = MIX_WIDTH // (2 * RET_HEADS)
RET_DV = MIX_WIDTH // (2 * RET_HEADS)
RET_WIDTH = RET_HEADS * RET_DV
RET_CHUNK = 128
DIFF_HEADS = 4
DIFF_DQK = MIX_WIDTH // (4 * DIFF_HEADS)
DIFF_DV = 2 * DIFF_DQK
DIFF_WIDTH = DIFF_HEADS * DIFF_DV
Q_BLOCK = 128
IN_SPLITS = [RET_HEADS * RET_DK, RET_HEADS * RET_DK, RET_WIDTH, RET_WIDTH,
             DIFF_HEADS * 2 * DIFF_DQK, DIFF_HEADS * 2 * DIFF_DQK, DIFF_WIDTH]
IN_COLS = sum(IN_SPLITS)
IN_OFFSETS = [int(o) for o in np.cumsum(IN_SPLITS)[:-1]]

PEER_HEADS = 8
PEER_TOPK = 16
N_KEYS = 128
N_EXPERTS = N_KEYS * N_KEYS
PEER_DQ = 256
PEER_TOKEN_BLOCK = 128

RMS_EPS = 1e-6
NEG_INF = -1e30


def rmsnorm(x, g=None):
    xf = x.astype(jnp.float32)
    y = xf * lax.rsqrt(jnp.mean(xf * xf, axis=-1, keepdims=True) + RMS_EPS)
    if g is not None:
        y = y * g.astype(jnp.float32)
    return y.astype(x.dtype)

def lambda_init(layer_idx):
    return 0.8 - 0.6 * float(np.exp(-0.3 * layer_idx))

def retention(q, k, v):
    B, T, H, dk = q.shape
    dv = v.shape[-1]
    C = RET_CHUNK
    N = T // C
    log_gamma = jnp.log1p(-jnp.exp2(-5.0 - jnp.arange(H, dtype=jnp.float32)))

    def chunks(a):
        return a.astype(jnp.float32).reshape(B, N, C, H, a.shape[-1]).transpose(1, 0, 3, 2, 4)

    qc, kc, vc = chunks(q), chunks(k) * (dk ** -0.5), chunks(v)
    idx = jnp.arange(C, dtype=jnp.float32)
    rel = idx[:, None] - idx[None, :]
    intra = jnp.where(rel >= 0, jnp.exp(log_gamma[:, None, None] * jnp.maximum(rel, 0.0)), 0.0)
    cross = jnp.exp(log_gamma[:, None] * (idx + 1.0))
    kdec = jnp.exp(log_gamma[:, None] * (C - 1.0 - idx))
    cdec = jnp.exp(log_gamma * C)

    def step(S, inp):
        qi, ki, vi = inp
        o = jnp.einsum('bhij,bhjv->bhiv', jnp.einsum('bhid,bhjd->bhij', qi, ki) * intra[None], vi)
        o = o + jnp.einsum('bhid,bhdv->bhiv', qi, S) * cross[None, :, :, None]
        S = S * cdec[None, :, None, None] + jnp.einsum('bhjd,bhjv->bhdv', ki * kdec[None, :, :, None], vi)
        return S, o

    S0 = jnp.zeros((B, H, dk, dv), jnp.float32)
    _, o = lax.scan(step, S0, (qc, kc, vc))
    return o.transpose(1, 0, 3, 2, 4).reshape(B, T, H, dv)

def alibi_slopes(n_heads):
    return jnp.exp2(-8.0 * (jnp.arange(n_heads, dtype=jnp.float32) + 1.0) / n_heads)

def diff_attention(q, k, v, lam):
    B, T, H, _, d = q.shape
    dv = v.shape[-1]
    C = Q_BLOCK
    N = T // C
    qb = (q.astype(jnp.float32) * (d ** -0.5)).reshape(B, N, C, H, 2, d).transpose(1, 0, 3, 4, 2, 5)
    kt = k.astype(jnp.float32).transpose(0, 2, 3, 1, 4)
    vt = v.astype(jnp.float32).transpose(0, 2, 1, 3)
    slopes = alibi_slopes(H)
    kpos = jnp.arange(T)

    def block(args):
        qi, start = args
        qpos = start + jnp.arange(C)
        dist = (qpos[:, None] - kpos[None, :]).astype(jnp.float32)
        bias = jnp.where(dist >= 0, -slopes[:, None, None] * dist, NEG_INF)
        s = jnp.einsum('bhpid,bhpjd->bhpij', qi, kt) + bias[None, :, None]
        p = jax.nn.softmax(s, axis=-1)
        a = p[:, :, 0] - lam * p[:, :, 1]
        return jnp.einsum('bhij,bhjv->bhiv', a, vt)

    o = lax.map(block, (qb, jnp.arange(N) * C))
    return o.transpose(1, 0, 3, 2, 4).reshape(B, T, H, dv)

def peer(xn, wq, subkeys, u, v):
    B, T, D = xn.shape
    xt = xn.reshape(-1, PEER_TOKEN_BLOCK, D)
    K = PEER_TOPK

    def block(xb):
        t = xb.shape[0]
        q = (xb @ wq).reshape(t, PEER_HEADS, 2, PEER_DQ // 2)
        s = jnp.einsum('thpd,hpkd->thpk', q, subkeys).astype(jnp.float32)
        s_top, i_top = lax.top_k(s, K)
        cand = (s_top[:, :, 0, :, None] + s_top[:, :, 1, None, :]).reshape(t, PEER_HEADS, K * K)
        c_top, c_idx = lax.top_k(cand, K)
        i1 = jnp.take_along_axis(i_top[:, :, 0], c_idx // K, axis=-1)
        i2 = jnp.take_along_axis(i_top[:, :, 1], c_idx % K, axis=-1)
        e = i1 * N_KEYS + i2
        g = jax.nn.softmax(c_top, axis=-1)
        ue = jnp.take(u, e, axis=0)
        ve = jnp.take(v, e, axis=0)
        act = jax.nn.gelu(jnp.einsum('thkd,td->thk', ue, xb).astype(jnp.float32), approximate=False)
        return jnp.einsum('thk,thkd->td', (g * act).astype(xb.dtype), ve)

    return lax.map(block, xt).reshape(B, T, D)

def first_inputs(seed: int = 0) -> dict:
    key = jax.random.key(seed)
    ks = jax.random.split(key, 13)
    f = jnp.float32
    x = jax.random.normal(ks[0], (BATCH, SEQ, D_MODEL), f)
    norm_mix_g = 1.0 + 0.02 * jax.random.normal(ks[1], (DEPTH, D_MODEL), f)
    w_in = jax.random.normal(ks[2], (DEPTH, D_MODEL, IN_COLS), f) * D_MODEL ** -0.5
    diff_lambda = 0.1 * jax.random.normal(ks[3], (DEPTH, 4, DIFF_DQK), f)
    diff_subln_g = 1.0 + 0.02 * jax.random.normal(ks[4], (DEPTH, DIFF_DV), f)
    w_out = jax.random.normal(ks[5], (DEPTH, MIX_WIDTH, D_MODEL), f) * MIX_WIDTH ** -0.5
    norm_ffn_g = 1.0 + 0.02 * jax.random.normal(ks[6], (DEPTH, D_MODEL), f)
    peer_wq = jax.random.normal(ks[7], (DEPTH, D_MODEL, PEER_HEADS * PEER_DQ), f) * D_MODEL ** -0.5
    peer_subkeys = jax.random.normal(ks[8], (DEPTH, PEER_HEADS, 2, N_KEYS, PEER_DQ // 2), f) * (PEER_DQ // 2) ** -0.5
    peer_u = jax.random.normal(ks[9], (DEPTH, N_EXPERTS, D_MODEL), f) * D_MODEL ** -0.5
    peer_v = jax.random.normal(ks[10], (DEPTH, N_EXPERTS, D_MODEL), f) * PEER_TOPK ** -0.5
    final_norm_g = 1.0 + 0.02 * jax.random.normal(ks[11], (D_MODEL,), f)
    return {"x": x, "norm_mix_g": norm_mix_g, "w_in": w_in, "diff_lambda": diff_lambda,
            "diff_subln_g": diff_subln_g, "w_out": w_out, "norm_ffn_g": norm_ffn_g,
            "peer_wq": peer_wq, "peer_subkeys": peer_subkeys, "peer_u": peer_u,
            "peer_v": peer_v, "final_norm_g": final_norm_g}

def first_block(x, norm_mix_g, w_in, diff_lambda, diff_subln_g, w_out, norm_ffn_g,
              peer_wq, peer_subkeys, peer_u, peer_v, final_norm_g):
    B, T, D = x.shape
    for l in range(DEPTH):
        h = rmsnorm(x, norm_mix_g[l])
        proj = h @ w_in[l]
        rq, rk, rv, rg, dq, dk, dv = jnp.split(proj, IN_OFFSETS, axis=-1)
        ry = retention(rq.reshape(B, T, RET_HEADS, RET_DK), rk.reshape(B, T, RET_HEADS, RET_DK),
                       rv.reshape(B, T, RET_HEADS, RET_DV))
        ry = rmsnorm(ry).reshape(B, T, RET_WIDTH)
        ret_out = (jax.nn.silu(rg.astype(jnp.float32)) * ry).astype(x.dtype)
        li = lambda_init(l)
        lp = diff_lambda[l].astype(jnp.float32)
        lam = jnp.exp(jnp.sum(lp[0] * lp[1])) - jnp.exp(jnp.sum(lp[2] * lp[3])) + li
        dy = diff_attention(dq.reshape(B, T, DIFF_HEADS, 2, DIFF_DQK), dk.reshape(B, T, DIFF_HEADS, 2, DIFF_DQK),
                            dv.reshape(B, T, DIFF_HEADS, DIFF_DV), lam)
        diff_out = (rmsnorm(dy, diff_subln_g[l]) * (1.0 - li)).reshape(B, T, DIFF_WIDTH).astype(x.dtype)
        x = x + jnp.concatenate([ret_out, diff_out], axis=-1) @ w_out[l]
        x = x + peer(rmsnorm(x, norm_ffn_g[l]), peer_wq[l], peer_subkeys[l], peer_u[l], peer_v[l])
    return rmsnorm(x, final_norm_g)


CHUNK = 64
EPS = 1e-6

N_HEADS_A = 8
N_KV_A = 2
HEAD_DIM = 64
ROT_DIM = HEAD_DIM // 4
ROPE_THETA = 500000.0
N_IDX_HEADS = 8
IDX_DIM = 32
IDX_ROT_DIM = IDX_DIM // 4
TOPK_MAX = 256
WIDTH_A = N_HEADS_A * HEAD_DIM

POOL_WINDOWS = (2, 4, 8, 16)
N_POOL_GROUPS = 4
POOL_GROUP_DIM = 128
WIDTH_B = N_POOL_GROUPS * POOL_GROUP_DIM

N_BRANCHES = 2

SPLIT_SIZES = (
    WIDTH_A,
    N_KV_A * HEAD_DIM,
    N_KV_A * HEAD_DIM,
    N_IDX_HEADS * IDX_DIM,
    IDX_DIM,
    N_IDX_HEADS,
    WIDTH_A,
    WIDTH_B,
    WIDTH_B,
    N_BRANCHES * D_MODEL,
)
D_IN = int(sum(SPLIT_SIZES))
SPLIT_POINTS = [int(s) for s in np.cumsum(SPLIT_SIZES)[:-1]]


def rms_norm(t, g):
    tf = t.astype(jnp.float32)
    tf = tf * lax.rsqrt(jnp.mean(tf * tf, axis=-1, keepdims=True) + EPS)
    return (tf * g.astype(jnp.float32)).astype(t.dtype)

def rope_tables(positions, rot_dim):
    half = rot_dim // 2
    inv_freq = ROPE_THETA ** (-jnp.arange(half, dtype=jnp.float32) / half)
    ang = positions.astype(jnp.float32)[..., None] * inv_freq
    return jnp.cos(ang), jnp.sin(ang)

def apply_partial_rope(t, cos, sin):
    half = cos.shape[-1]
    tf = t.astype(jnp.float32)
    c = cos[:, :, None, :]
    s = sin[:, :, None, :]
    t1 = tf[..., :half]
    t2 = tf[..., half:2 * half]
    out = jnp.concatenate([t1 * c - t2 * s, t1 * s + t2 * c, tf[..., 2 * half:]], axis=-1)
    return out.astype(t.dtype)

def dsa_attention(q, k, v, qi, ki, wi, k_sel):
    B, S = q.shape[0], q.shape[1]
    n_blocks = S // Q_BLOCK
    rep = N_HEADS_A // N_KV_A
    key_chunk = jnp.arange(S) // CHUNK
    scale = HEAD_DIM ** -0.5

    def block(i):
        start = i * Q_BLOCK
        qb = lax.dynamic_slice_in_dim(q, start, Q_BLOCK, axis=1)
        qib = lax.dynamic_slice_in_dim(qi, start, Q_BLOCK, axis=1)
        wib = lax.dynamic_slice_in_dim(wi, start, Q_BLOCK, axis=1)
        q_chunk = (start + jnp.arange(Q_BLOCK)) // CHUNK
        allowed = key_chunk[None, :] <= q_chunk[:, None]
        logits = jnp.einsum('bqhd,bsd->bqhs', qib, ki)
        iscore = jnp.einsum('bqhs,bqh->bqs', jax.nn.relu(logits), wib).astype(jnp.float32)
        iscore = jnp.where(allowed[None], iscore, -jnp.inf)
        _, idx = lax.top_k(iscore, k_sel)
        valid = key_chunk[idx] <= q_chunk[None, :, None]
        kg = jax.vmap(lambda kb, ib: kb[ib])(k, idx)
        vg = jax.vmap(lambda vb, ib: vb[ib])(v, idx)
        qg = qb.reshape(B, Q_BLOCK, N_KV_A, rep, HEAD_DIM)
        s = jnp.einsum('bqgrd,bqkgd->bqgrk', qg, kg).astype(jnp.float32) * scale
        s = jnp.where(valid[:, :, None, None, :], s, -jnp.inf)
        p = jax.nn.softmax(s, axis=-1).astype(v.dtype)
        o = jnp.einsum('bqgrk,bqkgd->bqgrd', p, vg)
        return o.reshape(B, Q_BLOCK, N_HEADS_A * HEAD_DIM)

    out = lax.map(block, jnp.arange(n_blocks))
    return out.transpose(1, 0, 2, 3).reshape(B, S, N_HEADS_A * HEAD_DIM)

def multiscale_pool(u, pool_w, pool_scale):
    B, S = u.shape[0], u.shape[1]
    ug = u.astype(jnp.float32).reshape(B, S, N_POOL_GROUPS, POOL_GROUP_DIM)
    cs = jnp.cumsum(ug, axis=1)
    t = jnp.arange(S)
    outs = []
    for g, w in enumerate(POOL_WINDOWS):
        c = cs[:, :, g]
        lagged = jnp.pad(c, ((0, 0), (w, 0), (0, 0)))[:, :S]
        count = jnp.minimum(t + 1, w).astype(jnp.float32)[None, :, None]
        outs.append((c - lagged) / count - ug[:, :, g])
    pooled = jnp.stack(outs, axis=2).astype(u.dtype)
    mixed = jnp.einsum('bsgc,gcd->bsgd', pooled, pool_w)
    return mixed.reshape(B, S, WIDTH_B) * pool_scale

def second_inputs(seed: int = 0) -> dict:
    key = jax.random.key(seed)
    ks = jax.random.split(key, 13)
    f32 = jnp.float32
    x = jax.random.normal(ks[0], (BATCH, SEQ, D_MODEL), f32)
    offsets = jax.random.randint(ks[1], (BATCH, 1), 0, 100000, dtype=jnp.int32)
    positions = (jnp.arange(SEQ, dtype=jnp.int32)[None, :] + offsets).astype(jnp.int32)
    norm_g = 1.0 + 0.02 * jax.random.normal(ks[2], (DEPTH, D_MODEL), f32)
    w_in = jax.random.normal(ks[3], (DEPTH, D_MODEL, D_IN), f32) * D_MODEL ** -0.5
    merge_bias = 0.02 * jax.random.normal(ks[4], (DEPTH, N_BRANCHES, D_MODEL), f32)
    q_norm_g = 1.0 + 0.02 * jax.random.normal(ks[5], (DEPTH, HEAD_DIM), f32)
    k_norm_g = 1.0 + 0.02 * jax.random.normal(ks[6], (DEPTH, HEAD_DIM), f32)
    pool_w = jax.random.normal(ks[7], (DEPTH, N_POOL_GROUPS, POOL_GROUP_DIM, POOL_GROUP_DIM), f32) * POOL_GROUP_DIM ** -0.5
    pool_scale = 1.0 + 0.1 * jax.random.normal(ks[8], (DEPTH, WIDTH_B), f32)
    w_branch_a = jax.random.normal(ks[9], (DEPTH, WIDTH_A, D_MODEL), f32) * WIDTH_A ** -0.5
    w_branch_b = jax.random.normal(ks[10], (DEPTH, WIDTH_B, D_MODEL), f32) * WIDTH_B ** -0.5
    w_out = jax.random.normal(ks[11], (DEPTH, D_MODEL, D_MODEL), f32) * D_MODEL ** -0.5
    return {"x": x, "positions": positions, "norm_g": norm_g, "w_in": w_in,
            "merge_bias": merge_bias, "q_norm_g": q_norm_g, "k_norm_g": k_norm_g,
            "pool_w": pool_w, "pool_scale": pool_scale, "w_branch_a": w_branch_a,
            "w_branch_b": w_branch_b, "w_out": w_out}

def second_block(x, positions, norm_g, w_in, merge_bias, q_norm_g, k_norm_g, pool_w, pool_scale,
              w_branch_a, w_branch_b, w_out):
    B, S = x.shape[0], x.shape[1]
    k_sel = min(TOPK_MAX, S // 4)
    cos_a, sin_a = rope_tables(positions, ROT_DIM)
    cos_i, sin_i = rope_tables(positions, IDX_ROT_DIM)
    for layer in range(DEPTH):
        h = rms_norm(x, norm_g[layer])
        proj = h @ w_in[layer]
        q, k, v, qi, ki, wi, z_a, u_b, z_b, gates = jnp.split(proj, SPLIT_POINTS, axis=-1)

        q = q.reshape(B, S, N_HEADS_A, HEAD_DIM)
        k = k.reshape(B, S, N_KV_A, HEAD_DIM)
        v = v.reshape(B, S, N_KV_A, HEAD_DIM)
        q = apply_partial_rope(rms_norm(q, q_norm_g[layer]), cos_a, sin_a)
        k = apply_partial_rope(rms_norm(k, k_norm_g[layer]), cos_a, sin_a)
        qi = apply_partial_rope(qi.reshape(B, S, N_IDX_HEADS, IDX_DIM), cos_i, sin_i) * (IDX_DIM ** -0.5)
        ki = apply_partial_rope(ki[:, :, None, :], cos_i, sin_i)[:, :, 0, :]
        wi = wi * (N_IDX_HEADS ** -0.5)
        a = dsa_attention(q, k, v, qi, ki, wi, k_sel) * jax.nn.silu(z_a)

        b = multiscale_pool(u_b, pool_w[layer], pool_scale[layer]) * jax.nn.silu(z_b)

        g = jax.nn.sigmoid(gates.reshape(B, S, N_BRANCHES, D_MODEL) + merge_bias[layer])
        y = g[:, :, 0] * (a @ w_branch_a[layer]) + g[:, :, 1] * (b @ w_branch_b[layer])
        x = x + y @ w_out[layer]
    return x


def setup_inputs(seed=0):
    out = dict(first_inputs(seed))
    for name, value in second_inputs(seed + 1).items():
        if name != "x":
            out[name + "_2"] = value
    return out


def reference(
    x, norm_mix_g, w_in, diff_lambda, diff_subln_g, w_out, norm_ffn_g, peer_wq, peer_subkeys,
    peer_u, peer_v, final_norm_g, positions_2, norm_g_2, w_in_2, merge_bias_2, q_norm_g_2,
    k_norm_g_2, pool_w_2, pool_scale_2, w_branch_a_2, w_branch_b_2, w_out_2,
):
    x = first_block(
        x, norm_mix_g, w_in, diff_lambda, diff_subln_g, w_out, norm_ffn_g, peer_wq,
        peer_subkeys, peer_u, peer_v, final_norm_g,
    )
    return second_block(
        x, positions_2, norm_g_2, w_in_2, merge_bias_2, q_norm_g_2, k_norm_g_2, pool_w_2,
        pool_scale_2, w_branch_a_2, w_branch_b_2, w_out_2,
    )


_drawn_inputs = setup_inputs


def setup_inputs(seed=0):
    import zlib

    import numpy as np

    out = dict(_drawn_inputs(seed))
    spreads = {}
    factors = {'diff_lambda': 6.481,
     'diff_subln_g': 3.642,
     'norm_ffn_g': 3.312,
     'norm_g_2': 5.734,
     'merge_bias_2': 8.0,
     'q_norm_g_2': 8.0,
     'k_norm_g_2': 8.0}
    for name, (base, spread) in spreads.items():
        noise = np.random.default_rng([zlib.crc32(name.encode()), seed]).standard_normal(out[name].shape)
        drawn = base * np.exp(spread * noise) if base else spread * noise
        out[name] = __import__('jax').numpy.asarray(drawn.astype(out[name].dtype))
    for name, factor in factors.items():
        out[name] = (out[name] * factor).astype(out[name].dtype)
    return out
```

```python
from concourse import mybir
import concourse.bass as bass
import numpy as np

F32 = mybir.dt.float32
F32R = mybir.dt.float32r
BF16 = mybir.dt.bfloat16
I32 = mybir.dt.int32
U32 = mybir.dt.uint32
ALU = mybir.AluOpType
ACT = mybir.ActivationFunctionType
AX_X = mybir.AxisListType.X

P = 128
T = 512
D = 1024
TT = T // P
KT = D // P
BANK = 512
RMS_EPS = 1e-6
NEG = -1e30

RET_HEADS, RET_D = 4, 128
DIFF_HEADS, DIFF_DQK, DIFF_DV = 4, 64, 128
LAMBDA_INIT = 0.8 - 0.6 * float(np.exp(-0.3 * 0))

PEER_HEADS, PEER_TOPK, N_KEYS = 8, 16, 128
HK = PEER_HEADS * PEER_TOPK
HP = PEER_HEADS * 2

A_HEADS, KV_HEADS, HEAD_DIM = 8, 2, 64
IDX_HEADS, IDX_DIM = 8, 32
K_SEL = min(256, T // 4)
ROPE_THETA = 500000.0
POOL_WINDOWS = (2, 4, 8, 16)


class Signal:

    def __init__(self, nc, name):
        self.semaphore = nc.alloc_semaphore(name)
        self.value = 0

    def after(self, instruction, amount=1):
        instruction.then_inc(self.semaphore, amount)
        self.value += amount
        return (self, self.value)


class Lane:

    def __init__(self, nc, engine, name):
        self.engine = engine
        self.finished = Signal(nc, name + "_finished")
        self.seen = {}

    def wait(self, *marks):
        for mark in marks:
            if mark is None:
                continue
            signal, value = mark
            if self.seen.get(signal, 0) < value:
                self.engine.wait_ge(signal.semaphore, value)
                self.seen[signal] = value

    def mark(self, instruction):
        return self.finished.after(instruction)

    def latest(self):
        return (self.finished, self.finished.value) if self.finished.value else None


class Region:

    def __init__(self, nc, start):
        self.nc, self.at = nc, start

    def tensor(self, name, shape, dtype):
        size = int(np.prod(shape[1:])) * mybir.dt.size(dtype)
        made = self.nc.alloc_sbuf_tensor_at(name, list(shape), dtype, offset=self.at)
        self.at += (size + 63) // 64 * 64
        return made


class Core:

    def __init__(self, nc):
        self.nc = nc
        self.pe = Lane(nc, nc.tensor, "tensor")
        self.act = Lane(nc, nc.scalar, "scalar")
        self.dve = Lane(nc, nc.vector, "vector")
        self.pool = Lane(nc, nc.gpsimd, "gpsimd")
        self.sp = Lane(nc, nc.sync, "sync")
        self.bank = [nc.alloc_psum_tensor(f"bank{i}", [P, BANK], F32) for i in range(8)]
        self.bank_read = [None] * 8
        self.stored = []

    def load(self, name, out, in_, queue=None):
        lane = queue or self.sp
        return Signal(self.nc, name).after(lane.engine.dma_start(out, in_), 16)

    def meet(self):
        lanes = (self.pe, self.act, self.dve, self.pool)
        marks = [lane.latest() for lane in lanes]
        for lane in lanes:
            lane.wait(*marks)
        return [m for m in marks if m]


def split_pair(core, source, high, low, ready, scale=None):
    act, dve = core.act, core.dve
    act.wait(*ready)
    if scale is None:
        high_ready = act.mark(act.engine.activation(high, source, ACT.Copy))
    else:
        high_ready = act.mark(act.engine.activation(high, source, ACT.Copy, scale=scale))
    dve.wait(*ready)
    dve.wait(high_ready)
    if scale is None:
        low_ready = dve.mark(dve.engine.tensor_tensor(low, source, high.bitcast(F32), ALU.subtract))
    else:
        low_ready = dve.mark(dve.engine.scalar_tensor_tensor(
            out=low, in0=source, scalar=scale, in1=high.bitcast(F32), op0=ALU.mult, op1=ALU.subtract))
    return [high_ready, low_ready]


def three_products(engine, out, left, right, first, last):
    (lh, ll), (rh, rl) = left, right
    engine.matmul(out, lh, rh, start=first, stop=False)
    engine.matmul(out, lh, rl, start=False, stop=False)
    return engine.matmul(out, ll, rh, start=False, stop=last)


class WeightStream:

    ROWS, RAW, PAIRS = 4, 2, 3

    def __init__(self, core, region, name):
        self.core = core
        shape = [P, self.ROWS, BANK]
        self.raw = [region.tensor(f"{name}_raw{i}", shape, F32) for i in range(self.RAW)]
        self.high = [region.tensor(f"{name}_high{i}", shape, F32R) for i in range(self.PAIRS)]
        self.low = [region.tensor(f"{name}_low{i}", shape, F32R) for i in range(self.PAIRS)]
        self.arrived = [Signal(core.nc, f"{name}_arrived{i}") for i in range(self.RAW)]
        self.raw_split = [[] for _ in range(self.RAW)]
        self.pair_used = [None] * self.PAIRS
        self.queue = []
        self.loaded = 0
        self.split = 0
        self.landed = {}
        self.ready = {}

    def add(self, weights, columns):
        view = weights.rearrange("(k p) c -> p k c", p=P)[:, :, columns[0]:columns[1]]
        for k in range(0, view.shape[1], self.ROWS):
            self.queue.append((view[:, k:k + self.ROWS, :], columns[1] - columns[0]))

    def load_next(self, *free):
        n = self.loaded
        source, width = self.queue[n]
        slot = n % self.RAW
        sp = self.core.sp
        sp.wait(*self.raw_split[slot], *free)
        out = self.raw[slot][:, :, 0:width]
        self.landed[n] = self.arrived[slot].after(sp.engine.dma_start(out, source), 16)
        self.loaded += 1

    def split_next(self):
        if self.split >= len(self.queue):
            return
        n = self.split
        while self.loaded <= n:
            self.load_next()
        width = self.queue[n][1]
        slot, raw = n % self.PAIRS, n % self.RAW
        ready = [self.landed[n], self.pair_used[slot]]
        self.ready[n] = split_pair(self.core, self.raw[raw][:, :, 0:width],
                                   self.high[slot][:, :, 0:width], self.low[slot][:, :, 0:width], ready)
        self.raw_split[raw] = self.ready[n]
        self.split += 1
        if self.loaded < len(self.queue):
            self.load_next()

    def pair(self, n):
        return self.high[n % self.PAIRS], self.low[n % self.PAIRS]


def project(core, stream, chunk, n_chunks, width, data, data_ready, token_major, banks, between=None):
    pe = core.pe
    high, low = data
    marks = []
    for c in range(chunk, chunk + n_chunks):
        while stream.split < min(c + 2, len(stream.queue)):
            stream.split_next()
        weight_high, weight_low = stream.pair(c)
        pe.wait(*stream.ready[c], *data_ready)
        for tile in range(4):
            b = banks[tile]
            if c == chunk:
                pe.wait(core.bank_read[b])
            for r in range(stream.ROWS):
                k = (c - chunk) * stream.ROWS + r
                part = slice(tile * P, tile * P + P)
                first, last = k == 0, k == n_chunks * stream.ROWS - 1
                if token_major:
                    left = (high[:, k, part], low[:, k, part])
                    right = (weight_high[:, r, 0:width], weight_low[:, r, 0:width])
                    out = core.bank[b][:, 0:width]
                else:
                    left = (weight_high[:, r, part], weight_low[:, r, part])
                    right = (high[:, k, :], low[:, k, :])
                    out = core.bank[b][:, :]
                done = three_products(pe.engine, out, left, right, first, last)
            mark = pe.mark(done)
            if between is not None:
                between()
            if c == chunk + n_chunks - 1:
                marks.append(mark)
        stream.pair_used[c % stream.PAIRS] = mark
    return marks


def copy_out(core, lane, out, source, ready, **kw):
    lane.wait(*ready)
    if lane is core.act:
        return lane.mark(lane.engine.activation(out, source, kw.get("func", ACT.Copy), scale=kw.get("scale", 1.0)))
    if "scale" in kw:
        return lane.mark(lane.engine.tensor_scalar(out, source, kw["scale"], None, ALU.mult))
    return lane.mark(lane.engine.tensor_copy(out, source))


def rms_scale(core, sums, scratch, out, n, ready):
    dve, act = core.dve, core.act
    dve.wait(*ready)
    mean = dve.mark(dve.engine.tensor_scalar(scratch, sums, 1.0 / n, RMS_EPS, ALU.mult, ALU.add))
    act.wait(mean)
    root = act.mark(act.engine.activation(scratch, scratch, ACT.Sqrt))
    dve.wait(root)
    return dve.mark(dve.engine.reciprocal(out, scratch))


def token_scales(core, x, small, junk, ready):
    dve = core.dve
    sums, scratch, scale = (small[:, 4 * i:4 * i + 4] for i in range(3))
    dve.wait(*ready)
    for t in range(TT):
        dve.wait(dve.latest())
        summed = dve.mark(dve.engine.tensor_tensor_reduce(
            out=junk[:, :], in0=x[:, t, :], in1=x[:, t, :], scale=1.0, scalar=0.0, op0=ALU.mult, op1=ALU.add,
            accum_out=sums[:, t:t + 1]))
    return scale, rms_scale(core, sums, scratch, scale, D, [summed])


def normalise_and_turn(core, x, gain, high, low, small, normed, junk, ident, ready, banks):
    act, dve = core.act, core.dve
    scale, scaled = token_scales(core, x, small, junk, ready)
    rows = []
    for t in range(TT):
        lane = act if t % 2 else dve
        lane.wait(scaled)
        if lane is act:
            rows.append(act.mark(act.engine.activation(normed[:, t, :], x[:, t, :], ACT.Copy, scale=scale[:, t:t + 1])))
        else:
            rows.append(dve.mark(dve.engine.tensor_scalar(normed[:, t, :], x[:, t, :], scale[:, t:t + 1], None, ALU.mult)))
    return turn_to_pair(core, normed, high, low, KT, ident, rows, banks, gain)


def turn_to_pair(core, source, high, low, tiles, ident, ready, banks, gain=None):
    pe = core.pe
    for k in range(tiles):
        b = banks[k % len(banks)]
        pe.wait(core.bank_read[b], *ready)
        for t in range(TT):
            turned = pe.engine.transpose(core.bank[b][:, t * P:t * P + P], source[:, t, k * P:k * P + P], ident)
        turned = pe.mark(turned)
        marks = split_pair(core, core.bank[b][:, :], high[:, k, :], low[:, k, :], [turned],
                           scale=None if gain is None else gain[:, k:k + 1])
        core.bank_read[b] = marks[1]
    return marks


def constants():
    i = np.arange(P, dtype=np.float64)
    later = np.arange(T, dtype=np.float64)[None, :] - i[:, None]
    gamma = 1.0 - 2.0 ** (-5.0 - np.arange(RET_HEADS))
    decay = np.where(later[:, None, :] >= 0, gamma[None, :, None] ** np.maximum(later, 0)[:, None, :], 0.0)
    decay = decay * RET_D ** -0.5
    key = np.arange(T, dtype=np.float64)[None, :] - (T - P)
    distance = i[:, None] - key
    alibi = np.where(distance >= 0, -distance, NEG)
    chunk_end = (np.floor(i / 64) + 1)[:, None] * 64
    allowed = np.where(key < chunk_end, 0.0, NEG)
    pool_start = np.stack([1.0 / np.minimum(np.arange(16) + 1, w) for w in POOL_WINDOWS])
    freq_a = ROPE_THETA ** (-np.arange(8) / 8)
    freq_i = ROPE_THETA ** (-np.arange(4) / 4)
    return {
        "identity": np.eye(P, dtype=np.float32),
        "decay": decay.astype(np.float32).reshape(P, RET_HEADS * T),
        "alibi": alibi.astype(np.float32),
        "allowed": allowed.astype(np.float32),
        "pool_start": np.broadcast_to(pool_start.astype(np.float32).reshape(1, -1), (P, 64)).copy(),
        "frequencies": np.broadcast_to(np.concatenate([freq_a, freq_i]).astype(np.float32), (P, 12)).copy(),
        "counting": np.broadcast_to(np.arange(P, dtype=np.float32), (P, P)).copy(),
    }


def row_of(vector, n):
    return vector.rearrange("(a n) -> a n", a=1).broadcast_to([P, n])


def block_one_mixing(core, dram, keep):
    nc, pe, act, dve = core.nc, core.pe, core.act, core.dve
    region = Region(nc, keep.end)
    ident = keep.ident[:, :]
    x = keep.x

    h_high = region.tensor("h_high", [P, KT, T], F32R)
    h_low = region.tensor("h_low", [P, KT, T], F32R)
    stream = WeightStream(core, region, "mix")
    outs_at = region.at
    feature = {n: region.tensor(n, [P, 4, T], F32) for n in ("ret_q", "ret_k", "diff_q", "diff_k0", "diff_k1")}
    token = {n: region.tensor(n, [P, TT, T], F32) for n in ("ret_v", "ret_gate", "diff_v")}
    end_of_outs = region.at
    work = Region(nc, region.at)
    lambda_rows = work.tensor("lambda_rows", [P, 4, DIFF_DQK], F32)
    lambda_sums = work.tensor("lambda_sums", [P, 4], F32)
    subln = work.tensor("subln", [P, DIFF_DV], F32)
    small = work.tensor("mix_small", [P, 64], F32)
    early = Region(nc, outs_at)
    normed = early.tensor("normed_x", [P, TT, D], F32)
    junk = early.tensor("junk_x", [P, D], F32)

    x_ready = [keep.x_ready]
    stream.add(dram["w_in"], (0, 512))
    for g in range(1, 7):
        stream.add(dram["w_in"], (g * 512, g * 512 + 512))
    stream.add(dram["w_out"], (0, 512))
    stream.add(dram["w_out"], (512, 1024))
    rows_ready = core.load("lambda_rows_in", lambda_rows[:, :, :],
                           dram["diff_lambda"].rearrange("(a q) d -> a q d", a=1).broadcast_to([P, 4, DIFF_DQK]), core.act)
    subln_ready = core.load("subln_in", subln[:, :], row_of(dram["diff_subln_g"], DIFF_DV), core.act)
    stream.load_next()
    stream.load_next()
    h_ready = normalise_and_turn(core, x, keep.gains[0], h_high, h_low, small, normed, junk, ident,
                                 x_ready + [keep.consts_ready], range(8))

    dve.wait(rows_ready)
    for n in range(2):
        dve.wait(dve.latest())
        summed = dve.mark(dve.engine.tensor_tensor_reduce(
            out=lambda_rows[:, 2 * n, :], in0=lambda_rows[:, 2 * n, :], in1=lambda_rows[:, 2 * n + 1, :], scale=1.0,
            scalar=0.0, op0=ALU.mult, op1=ALU.add, accum_out=lambda_sums[:, n:n + 1]))
    act.wait(summed)
    powers = act.mark(act.engine.activation(lambda_sums[:, 2:4], lambda_sums[:, 0:2], ACT.Exp))
    lam = lambda_sums[:, 0:1]
    dve.wait(powers)
    difference = dve.mark(dve.engine.tensor_tensor(lam, lambda_sums[:, 2:3], lambda_sums[:, 3:4], ALU.subtract))
    dve.wait(difference)
    lam_ready = dve.mark(dve.engine.tensor_scalar(lam, lam, LAMBDA_INIT, None, ALU.add))
    dve.wait(subln_ready)
    dve.mark(dve.engine.tensor_scalar(subln[:, :], subln[:, :], 1.0 - LAMBDA_INIT, None, ALU.mult))

    core.meet()
    zero_half = dve.mark(dve.engine.memset(feature["diff_k0"][64:128, :, :], 0.0))
    dve.mark(dve.engine.memset(feature["diff_k1"][0:64, :, :], 0.0))

    results = {}
    plan = [("ret_q", False), ("ret_k", False), ("ret_v", True), ("ret_gate", True),
            ("diff_q", False), ("diff_k", False), ("diff_v", True)]
    for g, (name, token_major) in enumerate(plan):
        banks = [(g % 2) * 4 + i for i in range(4)]
        summed = project(core, stream, 2 * g, 2, BANK, (h_high, h_low), h_ready, token_major, banks)
        marks = []
        for i, b in enumerate(banks):
            source = core.bank[b][:, :]
            if name == "diff_k":
                marks.append(copy_out(core, dve, feature["diff_k0"][0:64, i, :], source[0:64, :], [summed[i]]))
                marks.append(copy_out(core, act, feature["diff_k1"][64:128, i, :], source[64:128, :], [summed[i], marks[-1]]))
            elif name == "diff_q":
                marks.append(copy_out(core, act, feature[name][:, i, :], source, [summed[i]], scale=DIFF_DQK ** -0.5))
            elif name == "ret_gate":
                marks.append(copy_out(core, act, token[name][:, i, :], source, [summed[i]], func=ACT.Silu))
            else:
                out = token[name] if token_major else feature[name]
                marks.append(copy_out(core, act if i % 2 else dve, out[:, i, :], source, [summed[i]]))
            core.bank_read[b] = marks[-1]
        results[name] = marks

    hand_over = core.meet()
    heads = Region(nc, keep.end)
    mix = heads.tensor("mix", [P, TT, D], F32)
    weights = [heads.tensor(f"ret_weights{i}", [P, 4, T], F32) for i in range(1)] + \
              [heads.tensor(f"diff_scores{i}", [P, 2, T], F32) for i in range(2)]
    assert heads.at <= keep.end + 2 * KT * T * 4

    weighed, ret_weights = None, weights[0]
    for h in range(RET_HEADS):
        for j in range(TT):
            n = (TT - j) * P
            b = j
            pe.wait(core.bank_read[b])
            scored = pe.mark(pe.engine.matmul(core.bank[b][:, 0:n], feature["ret_k"][:, h, j * P:j * P + P],
                                              feature["ret_q"][:, h, j * P:T], start=True, stop=True))
            dve.wait(scored, weighed)
            core.bank_read[b] = dve.mark(dve.engine.tensor_tensor(
                ret_weights[:, j, 0:n], core.bank[b][:, 0:n], keep.decay[:, h * T:h * T + n], ALU.mult))
        b = 4 + h
        pe.wait(core.bank_read[b], core.bank_read[3])
        for t in range(TT):
            for j in range(t + 1):
                step = pe.engine.matmul(core.bank[b][:, t * P:t * P + P], ret_weights[:, j, (t - j) * P:(t - j) * P + P],
                                        token["ret_v"][:, j, h * P:h * P + P], start=(j == 0), stop=(j == t))
        weighed = pe.mark(step)
        core.bank_read[b] = copy_out(core, act, mix[:, :, h * P:h * P + P],
                                     core.bank[b][:, :].rearrange("p (t v) -> p t v", t=TT), [weighed])
    mixed_ret = core.bank_read[7]

    items = [(h, t) for h in range(DIFF_HEADS) for t in range(TT)]
    shrink = small[:, 32:64]
    averaged, scores_read = [None, None], [None, None]
    softmaxed = {}

    def score(i):
        h, t = items[i]
        n = (t + 1) * P
        for half, key in enumerate(("diff_k0", "diff_k1")):
            b = 2 * (i % 2) + half
            pe.wait(core.bank_read[b])
            scored = pe.mark(pe.engine.matmul(core.bank[b][:, 0:n], feature["diff_q"][:, h, t * P:t * P + P],
                                              feature[key][:, h, 0:n], start=True, stop=True))
            s = weights[1 + i % 2][:, half, 0:n]
            dve.wait(scored, averaged[i % 2])
            core.bank_read[b] = dve.mark(dve.engine.scalar_tensor_tensor(
                out=s, in0=keep.alibi[:, T - P - t * P:T], scalar=2.0 ** (-8.0 * (h + 1) / DIFF_HEADS),
                in1=core.bank[b][:, 0:n], op0=ALU.mult, op1=ALU.add))
        base = 8 * (i % 2)
        top, total, share = (shrink[:, base + 2 * m:base + 2 * m + 2] for m in range(3))
        s = weights[1 + i % 2]
        dve.wait(core.bank_read[b])
        highest = dve.mark(dve.engine.tensor_reduce(top, s[:, :, 0:n], AX_X, ALU.max))
        dve.wait(highest)
        negated = dve.mark(dve.engine.tensor_scalar(top, top, -1.0, None, ALU.mult))
        act.wait(negated)
        for half in range(2):
            powered = act.mark(act.engine.activation(s[:, half, 0:n], s[:, half, 0:n], ACT.Exp,
                                                     bias=top[:, half:half + 1], accum_out=total[:, half:half + 1]))
        dve.wait(powered)
        inverse = dve.mark(dve.engine.reciprocal(share, total))
        dve.wait(inverse, lam_ready)
        weighted = dve.mark(dve.engine.tensor_scalar(share[:, 1:2], share[:, 1:2], lam, None, ALU.mult))
        dve.wait(weighted)
        second = dve.mark(dve.engine.tensor_scalar(s[:, 1, 0:n], s[:, 1, 0:n], share[:, 1:2], None, ALU.mult))
        dve.wait(second)
        softmaxed[i] = dve.mark(dve.engine.scalar_tensor_tensor(
            out=s[:, 0, 0:n], in0=s[:, 0, 0:n], scalar=share[:, 0:1], in1=s[:, 1, 0:n], op0=ALU.mult, op1=ALU.subtract))

    turned_weights = weights[0]
    head_out = {}

    def weigh(i):
        h, t = items[i]
        b = 4 + i % 2
        pe.wait(softmaxed[i], core.bank_read[b])
        for j in range(t + 1):
            turned = pe.engine.transpose(core.bank[b][:, j * P:j * P + P], weights[1 + i % 2][:, 0, j * P:j * P + P], ident)
        averaged[i % 2] = turned = pe.mark(turned)
        n = (t + 1) * P
        slot = turned_weights[:, i % 4, 0:n]
        copied = copy_out(core, act, slot, core.bank[b][:, 0:n], [turned, weighed, head_out.get(i - 4)])
        core.bank_read[b] = copied
        out_bank = 6 + h % 2
        pe.wait(copied)
        if t == 0:
            pe.wait(core.bank_read[out_bank])
        for j in range(t + 1):
            step = pe.engine.matmul(core.bank[out_bank][:, t * P:t * P + P], turned_weights[:, i % 4, j * P:j * P + P],
                                    token["diff_v"][:, j, h * P:h * P + P], start=(j == 0), stop=(j == t))
        head_out[i] = pe.mark(step)
        if t == TT - 1:
            core.bank_read[out_bank] = copy_out(
                core, act, mix[:, :, BANK + h * P:BANK + h * P + P],
                core.bank[out_bank][:, :].rearrange("p (t v) -> p t v", t=TT), [head_out[i]])

    for i in range(len(items) + 1):
        if i < len(items):
            score(i)
        if i:
            weigh(i - 1)

    sums, scratch, scale = (keep.head_scale[:, 32 * m:32 * m + 32] for m in range(3))
    junk = Region(nc, keep.end + 2 * KT * T * 4 - 512).tensor("junk_head", [P, P], F32)
    dve.wait(mixed_ret, act.latest(), head_out[len(items) - 1])
    for t in range(TT):
        for h in range(8):
            head = mix[:, t, h * P:h * P + P]
            dve.wait(dve.latest())
            summed = dve.mark(dve.engine.tensor_tensor_reduce(
                out=junk[:, :], in0=head, in1=head, scale=1.0, scalar=0.0, op0=ALU.mult, op1=ALU.add,
                accum_out=sums[:, 8 * t + h:8 * t + h + 1]))
    scaled = rms_scale(core, sums, scratch, scale, P, [summed])
    dve.wait(scaled)
    for t in range(TT):
        for h in range(8):
            head = mix[:, t, h * P:h * P + P]
            factor = token["ret_gate"][:, t, h * P:h * P + P] if h < RET_HEADS else subln[:, :]
            normed_heads = dve.mark(dve.engine.scalar_tensor_tensor(
                out=head, in0=head, scalar=scale[:, 8 * t + h:8 * t + h + 1], in1=factor, op0=ALU.mult, op1=ALU.mult))

    late = Region(nc, outs_at)
    mix_high = late.tensor("mix_high", [P, KT, T], F32R)
    mix_low = late.tensor("mix_low", [P, KT, T], F32R)
    assert late.at <= end_of_outs
    hand_over = core.meet()
    mix_ready = turn_to_pair(core, mix, mix_high, mix_low, KT, ident, [normed_heads], range(4, 8))
    for g in range(2):
        banks = [g * 4 + i for i in range(4)]
        summed = project(core, stream, 14 + 2 * g, 2, BANK, (mix_high, mix_low), mix_ready, True, banks)
        for t, b in enumerate(banks):
            dve.wait(summed[t])
            part = x[:, t, g * BANK:g * BANK + BANK]
            core.bank_read[b] = keep.x_written = dve.mark(dve.engine.tensor_tensor(part, part, core.bank[b][:, :], ALU.add))


class Kept:

    def __init__(self, core, dram):
        nc = core.nc
        region = Region(nc, (nc.sbuf_base + 63) // 64 * 64)
        self.x = region.tensor("x", [P, TT, D], F32)
        self.ident = region.tensor("ident", [P, P], F32)
        self.gains = [region.tensor(f"gain{i}", [P, KT], F32) for i in range(3)]
        self.head_scale = region.tensor("head_scale", [P, 96], F32)
        self.rows_at = region.at
        self.decay = region.tensor("decay_sb", [P, RET_HEADS * T], F32)
        self.alibi = region.tensor("alibi_sb", [P, T], F32)
        self.end = region.at
        arrived = Signal(nc, "tables_arrived")
        act = core.act
        arrived.after(act.engine.dma_start(self.ident[:, :], dram["identity"]), 16)
        for tile, name in zip(self.gains, ("norm_mix_g", "norm_ffn_g", "norm_g_2")):
            arrived.after(act.engine.dma_start(tile[:, :], dram[name]), 16)
        arrived.after(act.engine.dma_start(self.decay[:, :], dram["decay"]), 16)
        self.consts_ready = arrived.after(act.engine.dma_start(self.alibi[:, :], dram["alibi"]), 16)
        self.x_ready = core.load("x_arrived", self.x[:, :, :], dram["x"].rearrange("(t p) d -> p t d", p=P))
        self.x_written = None


EARLY_BANKS = (0, 1, 2, 3)
GATE_BANKS = (4, 5, 6, 7)
GATE_CHUNK = 128
BATCH = 4
GROUP = 4


def peer_scores(core, dram, keep, xn_high, xn_low, region, scores):
    pe, act, dve = core.pe, core.act, core.dve
    small = region.tensor("ffn_small", [P, 16], F32)
    subkeys = region.tensor("subkeys", [P, HP, N_KEYS], F32)
    query = region.tensor("query", [P, HP, T], F32)
    normed = Region(core.nc, region.at - HP * T * 4).tensor("normed_ffn", [P, TT, D], F32)
    junk = Region(core.nc, region.at - HP * T * 4 + TT * D * 4).tensor("junk_ffn", [P, D], F32)
    stream = WeightStream(core, region, "wq")
    subkeys_ready = core.load("subkeys_arrived", subkeys[:, :, :], dram["subkeys"])
    for g in range(4):
        stream.add(dram["peer_wq"], (g * 512, g * 512 + 512))
    stream.load_next()
    stream.load_next()
    xn_ready = normalise_and_turn(core, keep.x, keep.gains[1], xn_high, xn_low, small, normed, junk,
                                  keep.ident[:, :], [keep.x_written], range(8))
    core.meet()
    query_ready = []
    for g in range(4):
        banks = [(g % 2) * 4 + i for i in range(4)]
        summed = project(core, stream, 2 * g, 2, BANK, (xn_high, xn_low), xn_ready, False, banks)
        for i, b in enumerate(banks):
            lane = act if i % 2 else dve
            core.bank_read[b] = copy_out(core, lane, query[:, 4 * g + i, :], core.bank[b][:, :], [summed[i]])
            query_ready.append(core.bank_read[b])
    marks = []
    for t in range(TT):
        for g in range(4):
            b = (4 * t + g) % 8
            pe.wait(core.bank_read[b], subkeys_ready, *query_ready[4 * g:4 * g + 4])
            for i in range(4):
                scored = pe.engine.matmul(core.bank[b][:, i * P:i * P + P], query[:, 4 * g + i, t * P:t * P + P],
                                          subkeys[:, 4 * g + i, :], start=True, stop=True)
            lane = act if g % 2 else dve
            core.bank_read[b] = copy_out(core, lane, scores[:, t, 4 * g:4 * g + 4, :],
                                         core.bank[b][:, :].rearrange("p (a k) -> p a k", a=4), [pe.mark(scored)])
            marks.append(core.bank_read[b])
    return marks


def top_sixteen(core, pairs):
    dve = core.dve
    v = dve.engine
    first = [dve.mark(v.max(top[:, 0:8], values)) for values, work, top, places in pairs]
    for n, (values, work, top, places) in enumerate(pairs):
        dve.wait(first[n])
        dve.mark(v.max_index(places[:, 0:8], top[:, 0:8], values))
    rest = [dve.mark(v.match_replace(work, top[:, 0:8], values, -3e38)) for values, work, top, places in pairs]
    for n, (values, work, top, places) in enumerate(pairs):
        dve.wait(rest[n])
        first[n] = dve.mark(v.max(top[:, 8:16], work))
    for n, (values, work, top, places) in enumerate(pairs):
        dve.wait(first[n])
        done = dve.mark(v.max_index(places[:, 8:16], top[:, 8:16], work))
    return done


def choose_experts(core, dram, keep, scores, scores_ready, chosen, region):
    pe, act, dve = core.pe, core.act, core.dve
    work = [region.tensor(f"top_work{i}", [P, 2 * N_KEYS], F32) for i in range(2)]
    cand = [region.tensor(f"candidates{i}", [P, PEER_TOPK, PEER_TOPK], F32) for i in range(2)]
    top = region.tensor("top", [P, HP, PEER_TOPK], F32)
    places = region.tensor("places", [P, HP, PEER_TOPK], U32)
    keys = region.tensor("top_keys", [P, HP, PEER_TOPK], F32)
    best = region.tensor("best", [P, PEER_HEADS, PEER_TOPK], F32)
    best_at = region.tensor("best_at", [P, PEER_HEADS, PEER_TOPK], U32)
    digit = region.tensor("digit", [P, 2, PEER_HEADS, PEER_TOPK], U32)
    digit_value = region.tensor("digit_value", [P, 2, PEER_HEADS, PEER_TOPK], F32)
    match = region.tensor("match", [P, PEER_HEADS * PEER_TOPK, PEER_TOPK], F32)
    picked = region.tensor("picked", [P, 3, HK], F32)
    total = region.tensor("gate_total", [P, 2, PEER_HEADS], F32)
    v = dve.engine
    turned = None
    dve.wait(*scores_ready)
    yield
    for t in range(TT):
        for hp in range(0, HP, 2):
            done = top_sixteen(core, [(scores[:, t, hp + i, :], work[i][:, 0:N_KEYS], top[:, hp + i, :], places[:, hp + i, :])
                                      for i in range(2)])
            yield
        dve.wait(done)
        keys_ready = dve.mark(v.tensor_copy(keys[:, :, :], places[:, :, :]))
        for h in range(0, PEER_HEADS, 2):
            rows = []
            for i in range(2):
                a = top[:, 2 * (h + i), :].unsqueeze(2).broadcast_to([P, PEER_TOPK, PEER_TOPK])
                b = top[:, 2 * (h + i) + 1, :].unsqueeze(1).broadcast_to([P, PEER_TOPK, PEER_TOPK])
                summed = dve.mark(v.tensor_tensor(cand[i][:, :, :], a, b, ALU.add))
                rows.append((cand[i][:, :, :].rearrange("p a b -> p (a b)"), work[i][:, :], best[:, h + i, :], best_at[:, h + i, :]))
            dve.wait(summed)
            done = top_sixteen(core, rows)
            yield
        gate = picked[:, 2, :].rearrange("p (h k) -> p h k", h=PEER_HEADS)
        dve.wait(done, turned)
        shifted = dve.mark(v.tensor_tensor(gate, best[:, :, :], best[:, :, 0:1].broadcast_to([P, PEER_HEADS, PEER_TOPK]), ALU.subtract))
        act.wait(shifted)
        powered = act.mark(act.engine.activation(picked[:, 2, :], picked[:, 2, :], ACT.Exp))
        dve.mark(v.tensor_scalar(digit[:, 0, :, :], best_at[:, :, :], 4, None, ALU.logical_shift_right))
        split = dve.mark(v.tensor_scalar(digit[:, 1, :, :], best_at[:, :, :], 15, None, ALU.bitwise_and))
        dve.wait(split)
        digits = dve.mark(v.tensor_copy(digit_value[:, :, :, :], digit[:, :, :, :]))
        dve.wait(powered)
        summed = dve.mark(v.tensor_reduce(total[:, 0, :], gate, AX_X, ALU.add))
        dve.wait(summed)
        inverse = dve.mark(v.reciprocal(total[:, 1, :], total[:, 0, :]))
        dve.wait(inverse, digits, keys_ready)
        gated = dve.mark(v.tensor_tensor(gate, gate, total[:, 1, :].unsqueeze(2).broadcast_to([P, PEER_HEADS, PEER_TOPK]), ALU.mult))
        yield
        for half in range(2):
            wide = [P, HK, PEER_TOPK]
            ranks = keep.counting[:, 0:PEER_TOPK].unsqueeze(1).broadcast_to(wide)
            chosen_rank = digit_value[:, half, :, :].rearrange("p h k -> p (h k)").unsqueeze(2).broadcast_to(wide)
            compared = dve.mark(v.tensor_tensor(match[:, :, :], chosen_rank, ranks, ALU.is_equal))
            dve.wait(compared)
            yield
            for h in range(PEER_HEADS):
                part = match[:, h * PEER_TOPK:(h + 1) * PEER_TOPK, :]
                of_rank = keys[:, 2 * h + half, :].unsqueeze(1).broadcast_to([P, PEER_TOPK, PEER_TOPK])
                marked = dve.mark(v.tensor_tensor(part, part, of_rank, ALU.mult))
            dve.wait(marked)
            yield
            picked_ready = dve.mark(v.tensor_reduce(picked[:, half, :], match[:, :, :], AX_X, ALU.add))
            dve.wait(picked_ready)
        b = GATE_BANKS[t % 4]
        pe.wait(picked_ready, gated, core.bank_read[b])
        for i in range(3):
            step = pe.engine.transpose(core.bank[b][:, i * P:i * P + P], picked[:, i, :], keep.ident[:, :])
        turned = pe.mark(step)
        for i in range(3):
            moved = copy_out(core, act, chosen[i][:, t * P:t * P + P], core.bank[b][:, i * P:i * P + P], [turned])
        core.bank_read[b] = moved
        yield
    keep.chosen_ready = moved


def build_gates(core, dram, keep, chosen, region):
    pe, act, dve = core.pe, core.act, core.dve
    key1, key2, gate = chosen
    stages = region.tensor("gate_stage", [P, N_KEYS, GATE_CHUNK], F32)
    parts = [region.tensor(f"gate_part{i}", [P, T], F32) for i in range(3)]
    part16 = region.tensor("gate_part16", [P, T], BF16)
    ring = 2
    hot1 = [region.tensor(f"hot1_{i}", [P, BATCH, P], BF16) for i in range(ring)]
    hot2 = [region.tensor(f"hot2_{i}", [P, BATCH, 3, P], BF16) for i in range(ring)]
    stored_signal = Signal(core.nc, "gates_stored")
    v = dve.engine
    counting = keep.counting16[:, :]
    dve.wait(keep.chosen_ready)
    rest = gate
    for i in range(3):
        rounded = dve.mark(v.tensor_copy(part16[:, :], rest[:, :]))
        dve.wait(rounded)
        kept = dve.mark(v.tensor_copy(parts[i][:, :], part16[:, :]))
        dve.wait(kept)
        if i < 2:
            left = dve.mark(v.tensor_tensor(gate[:, :], rest[:, :], parts[i][:, :], ALU.subtract))
            dve.wait(left)
    yield
    batches = T // BATCH
    per_chunk = GATE_CHUNK // BATCH
    used = [None] * ring
    hot_ready = {}
    stored = None

    def make_hot(n):
        dve.wait(used[n % ring])
        for i in range(BATCH):
            t = n * BATCH + i
            v.tensor_scalar(hot1[n % ring][:, i, :], counting, key1[:, t:t + 1], None, ALU.is_equal)
            for part in range(3):
                step = v.tensor_scalar(hot2[n % ring][:, i, part, :], counting, key2[:, t:t + 1],
                                       parts[part][:, t:t + 1], ALU.is_equal, ALU.mult)
        hot_ready[n] = dve.mark(step)

    make_hot(0)
    yield
    for n in range(batches):
        if n + 1 < batches:
            make_hot(n + 1)
        b = GATE_BANKS[n % 4]
        pe.wait(hot_ready[n], core.bank_read[b])
        for i in range(BATCH):
            for part in range(3):
                step = pe.engine.matmul(core.bank[b][:, i * P:i * P + P], hot1[n % ring][:, i, :],
                                        hot2[n % ring][:, i, part, :], start=(part == 0), stop=(part == 2))
        used[n % ring] = built = pe.mark(step)
        act.wait(built, stored if n % per_chunk == 0 else None)
        at = (n % per_chunk) * BATCH
        core.bank_read[b] = act.mark(act.engine.activation(
            stages[:, :, at:at + BATCH], core.bank[b][:, :].rearrange("p (t k) -> p k t", t=BATCH), ACT.Copy))
        if n % per_chunk == per_chunk - 1:
            pool = core.pool
            pool.wait(core.bank_read[b])
            stored = stored_signal.after(pool.engine.dma_start(
                dram["gates"][n // per_chunk], stages[:, :, :]), 16)
            keep.gates_stored = stored
        yield


def hidden_units(core, dram, keep, xn_high, xn_low, xn_ready, region, background):
    pe, act, dve, sp = core.pe, core.act, core.dve, core.sp
    RAW, PAIR, OUT = 3, 2, 3
    raw = [region.tensor(f"u_raw{i}", [P, KT, P], F32) for i in range(RAW)]
    high = [region.tensor(f"u_high{i}", [P, KT, P], F32R) for i in range(PAIR)]
    low = [region.tensor(f"u_low{i}", [P, KT, P], F32R) for i in range(PAIR)]
    out = [region.tensor(f"hidden{i}", [P, T], F32) for i in range(OUT)]
    arrived = [Signal(core.nc, f"u_arrived{i}") for i in range(RAW)]
    stored = [Signal(core.nc, f"hidden_stored{i}") for i in range(OUT)]
    stored_at = [None] * OUT
    split_of, landed = {}, {}
    product_of = {}

    def load(j):
        sp.wait(*split_of.get(j - RAW, []))
        landed[j] = arrived[j % RAW].after(sp.engine.dma_start(raw[j % RAW][:, :, :], dram["peer_u"][j]), 16)

    def split(j):
        split_of[j] = split_pair(core, raw[j % RAW][:, :, :], high[j % PAIR][:, :, :], low[j % PAIR][:, :, :],
                                 [landed[j], product_of.get(j - PAIR)])

    for j in range(RAW):
        load(j)
    split(0)
    for j in range(N_KEYS):
        if j + 1 < N_KEYS:
            split(j + 1)
        b = EARLY_BANKS[j % 4]
        pe.wait(*split_of[j], core.bank_read[b], *xn_ready)
        for k in range(KT):
            step = three_products(pe.engine, core.bank[b][:, :], (high[j % PAIR][:, k, :], low[j % PAIR][:, k, :]),
                                  (xn_high[:, k, :], xn_low[:, k, :]), k == 0, k == KT - 1)
        product_of[j] = pe.mark(step)
        for _ in range(keep.pace(j)):
            next(background, None)
        if j + RAW < N_KEYS:
            load(j + RAW)
        act.wait(product_of[j], stored_at[j % OUT])
        core.bank_read[b] = act.mark(act.engine.activation(out[j % OUT][:, :], core.bank[b][:, :], ACT.Gelu))
        sp.wait(core.bank_read[b])
        stored_at[j % OUT] = stored[j % OUT].after(sp.engine.dma_start(dram["hidden"][j], out[j % OUT][:, :]), 16)
        if (j + 1) % GROUP == 0:
            keep.hidden_stored[j // GROUP] = [stored_at[m % OUT] for m in range(max(0, j - OUT + 1), j + 1)]
    for _ in background:
        pass


def combine(core, dram, keep, region):
    pe, act, dve, sp, pool = core.pe, core.act, core.dve, core.sp, core.pool
    gate = [region.tensor(f"gate_in{i}", [P, TT, GROUP, P], F32) for i in range(2)]
    hidden = [region.tensor(f"hidden_in{i}", [P, GROUP, T], F32) for i in range(2)]
    value = [region.tensor(f"v_raw{i}", [P, GROUP, BANK], F32) for i in range(2)]
    value_pair = [[region.tensor(f"v_{n}{i}", [P, GROUP, BANK], F32R) for n in ("high", "low")] for i in range(3)]
    weight_pair = [[region.tensor(f"w_{n}{i}", [P, GROUP, T], F32R) for n in ("high", "low")] for i in range(2)]
    arrived = {n: [Signal(core.nc, f"{n}_arrived{i}") for i in range(2)] for n in ("gate", "hid", "v")}
    groups = N_KEYS // GROUP
    v_rows = dram["peer_v"]
    split_of, landed, half_done, multiplied, weight_ready = {}, {}, {}, {}, {}

    def load_weights(g):
        s = g % 2
        sp.wait(keep.gates_stored, *keep.hidden_stored[g], *weight_ready.get(g - 2, []))
        for c in range(TT):
            mark = arrived["gate"][s].after(sp.engine.dma_start(
                gate[s][:, c, :, :], dram["gates"][c][:, g * GROUP:(g + 1) * GROUP, :]), 16)
        landed["w", g] = [mark, arrived["hid"][s].after(sp.engine.dma_start(
            hidden[s][:, :, :], dram["hidden"][g * GROUP:(g + 1) * GROUP].rearrange("j p t -> p j t")), 16)]

    def load_values(n):
        g, half = n // 2, n % 2
        s = n % 2
        act_queue = sp
        act_queue.wait(*split_of.get(n - 2, []))
        landed["v", n] = arrived["v"][s].after(act_queue.engine.dma_start(
            value[s][:, :, :], v_rows[:, g * GROUP:(g + 1) * GROUP, half * BANK:(half + 1) * BANK]), 16)

    def prepare_values(n):
        split_of[n] = split_pair(core, value[n % 2][:, :, :], value_pair[n % 3][0][:, :, :], value_pair[n % 3][1][:, :, :],
                                 [landed["v", n], half_done.get(n - 3)])

    def prepare_weights(g):
        s = g % 2
        product = hidden[s][:, :, :].rearrange("p j (c t) -> p j c t", c=TT)
        dve.wait(*landed["w", g])
        for j in range(GROUP):
            step = dve.engine.tensor_tensor(product[:, j, :, :], product[:, j, :, :], gate[s][:, :, j, :], ALU.mult)
        multiplied[g] = dve.mark(step)
        weight_ready[g] = split_pair(core, hidden[s][:, :, :], weight_pair[s][0][:, :, :], weight_pair[s][1][:, :, :],
                                     [multiplied[g], half_done.get(2 * (g - 2) + 1)])

    load_weights(0)
    load_values(0)
    load_values(1)
    load_weights(1)
    prepare_weights(0)
    prepare_values(0)
    for n in range(2 * groups):
        g, half = n // 2, n % 2
        if n + 1 < 2 * groups:
            prepare_values(n + 1)
        if n + 2 < 2 * groups:
            load_values(n + 2)
        if half == 1 and g + 1 < groups:
            prepare_weights(g + 1)
            if g + 2 < groups:
                load_weights(g + 2)
        value_high, value_low = value_pair[n % 3]
        weight_high, weight_low = weight_pair[g % 2]
        pe.wait(*split_of[n], *weight_ready[g])
        for t in range(TT):
            b = 4 * half + t
            pe.wait(core.bank_read[b])
            for j in range(GROUP):
                part = slice(t * P, t * P + P)
                step = three_products(pe.engine, core.bank[b][:, :], (weight_high[:, j, part], weight_low[:, j, part]),
                                      (value_high[:, j, :], value_low[:, j, :]), j == 0, j == GROUP - 1)
            half_done[n] = pe.mark(step)
            out = keep.x[:, t, half * BANK:(half + 1) * BANK]
            dve.wait(half_done[n])
            core.bank_read[b] = keep.x_written = dve.mark(dve.engine.tensor_tensor(out, out, core.bank[b][:, :], ALU.add))


def peer(core, dram, keep):
    nc = core.nc
    core.sp.wait(*core.meet())
    region = Region(nc, keep.rows_at)
    xn_high = region.tensor("xn_high", [P, KT, T], F32R)
    xn_low = region.tensor("xn_low", [P, KT, T], F32R)
    keep.counting = region.tensor("counting_sb", [P, P], F32)
    keep.counting16 = region.tensor("counting16", [P, P], BF16)
    chosen = [region.tensor(n, [P, T], F32) for n in ("key1", "key2", "gate")]
    scores_at = region.at
    scores = region.tensor("scores", [P, TT, HP, N_KEYS], F32)
    after_scores = region.at
    counting_ready = core.load("counting_arrived", keep.counting[:, :], dram["counting"], core.act)
    scores_ready = peer_scores(core, dram, keep, xn_high, xn_low, Region(nc, after_scores), scores)
    core.dve.wait(counting_ready)
    core.dve.mark(core.dve.engine.tensor_copy(keep.counting16[:, :], keep.counting[:, :]))
    released = core.meet()
    core.sp.wait(*released)

    def background():
        yield from choose_experts(core, dram, keep, scores, scores_ready, chosen, Region(nc, after_scores))
        core.act.wait(*[m for m in (core.dve.latest(), core.pe.latest()) if m])
        core.dve.wait(core.act.latest(), core.pe.latest())
        yield from build_gates(core, dram, keep, chosen, Region(nc, scores_at))

    keep.hidden_stored = {}
    top = 229344 // 64 * 64
    hidden_region = Region(nc, top - 34 * 1024)
    hidden_units(core, dram, keep, xn_high, xn_low, [], hidden_region, background())
    released = core.meet()
    core.sp.wait(*released)
    combine(core, dram, keep, Region(nc, keep.rows_at))


TWO_PI = 2.0 * float(np.pi)
TURN = (6.28125, float(np.float32(1.9350051879882812e-03)), 0.0)
TURN = (TURN[0], TURN[1], TWO_PI - TURN[0] - TURN[1])
ROUND = 1.5 * 2.0 ** 23
PI_BELOW = 3.1415925
FREQS = 12


def rotary_tables(core, dram, region):
    act, dve = core.act, core.dve
    v = dve.engine
    position = region.tensor("position", [P, TT], I32)
    position_value = region.tensor("position_value", [P, TT], F32)
    frequency = region.tensor("frequency", [P, FREQS], F32)
    angle = region.tensor("angle", [P, TT, FREQS], F32)
    turns = region.tensor("turns", [P, TT, FREQS], F32)
    tables = [region.tensor(n, [P, TT, FREQS], F32) for n in ("cosine", "sine")]
    loaded = [core.load("position_arrived", position[:, :], dram["positions"], act),
              core.load("frequency_arrived", frequency[:, :], dram["frequencies"], act)]
    dve.wait(*loaded)
    dve.wait(dve.mark(v.tensor_copy(position_value[:, :], position[:, :])))
    shape = [P, TT, FREQS]
    dve.wait(dve.mark(v.tensor_tensor(angle[:, :, :], position_value[:, :].unsqueeze(2).broadcast_to(shape),
                                      frequency[:, :].unsqueeze(1).broadcast_to(shape), ALU.mult)))
    ready = []
    for table, quarter in zip(tables, (0.25, 0.0)):
        dve.wait(dve.mark(v.tensor_scalar(turns[:, :, :], angle[:, :, :], 1.0 / TWO_PI, quarter, ALU.mult, ALU.add)))
        dve.wait(dve.mark(v.tensor_scalar(turns[:, :, :], turns[:, :, :], ROUND, None, ALU.add)))
        dve.wait(dve.mark(v.tensor_scalar(turns[:, :, :], turns[:, :, :], ROUND, None, ALU.subtract)))
        source = angle
        for part in TURN:
            dve.wait(dve.mark(v.scalar_tensor_tensor(out=table[:, :, :], in0=turns[:, :, :], scalar=-part,
                                                     in1=source[:, :, :], op0=ALU.mult, op1=ALU.add)))
            source = table
        dve.wait(dve.mark(v.tensor_scalar(table[:, :, :], table[:, :, :], quarter * TWO_PI, PI_BELOW, ALU.add, ALU.min)))
        reduced = dve.mark(v.tensor_scalar(table[:, :, :], table[:, :, :], -PI_BELOW, None, ALU.max))
        dve.wait(reduced)
        act.wait(reduced)
        ready.append(act.mark(act.engine.activation(table[:, :, :], table[:, :, :], ACT.Sin)))
    return tables, ready


def rotate(core, tensor, heads, width, pairs, cosine, sine, at, scratch):
    dve = core.dve
    v = dve.engine
    view = tensor.rearrange("p t (h d) -> p t h d", h=heads)
    one, two = view[:, :, :, 0:pairs], view[:, :, :, pairs:2 * pairs]
    shape = [P, TT, heads, pairs]
    c = cosine[:, :, at:at + pairs].unsqueeze(2).broadcast_to(shape)
    s = sine[:, :, at:at + pairs].unsqueeze(2).broadcast_to(shape)
    size = TT * heads * pairs
    parts = [scratch[:, i, 0:size].rearrange("p (t h d) -> p t h d", t=TT, h=heads) for i in range(4)]
    for out, a, b in ((parts[0], one, c), (parts[1], two, s), (parts[2], one, s), (parts[3], two, c)):
        product = dve.mark(v.tensor_tensor(out, a, b, ALU.mult))
    dve.wait(product)
    dve.mark(v.tensor_tensor(one, parts[0], parts[1], ALU.subtract))
    done = dve.mark(v.tensor_tensor(two, parts[2], parts[3], ALU.add))
    dve.wait(done)
    return done


def norm_heads(core, tensor, heads, gain, square, small, ready):
    dve = core.dve
    v = dve.engine
    view = tensor.rearrange("p t (h d) -> p t h d", h=heads)
    squared = square[:, 0:TT * heads * HEAD_DIM].rearrange("p (t h d) -> p t h d", t=TT, h=heads)
    sums, scratch, scale = (small[:, i, 0:TT * heads] for i in range(3))
    dve.wait(*ready)
    dve.wait(dve.mark(v.tensor_tensor(squared, view, view, ALU.mult)))
    summed = dve.mark(v.tensor_reduce(sums, square[:, 0:TT * heads * HEAD_DIM].rearrange("p (a d) -> p a d", d=HEAD_DIM),
                                      AX_X, ALU.add))
    scaled = rms_scale(core, sums, scratch, scale, HEAD_DIM, [summed])
    dve.wait(scaled)
    shape = [P, TT, heads, HEAD_DIM]
    dve.wait(dve.mark(v.tensor_tensor(view, view, scale.rearrange("p (t h) -> p t h", t=TT).unsqueeze(3).broadcast_to(shape), ALU.mult)))
    for t in range(TT):
        done = dve.mark(v.tensor_tensor(view[:, t, :, :], view[:, t, :, :],
                                        gain.unsqueeze(1).broadcast_to([P, heads, HEAD_DIM]), ALU.mult))
    dve.wait(done)
    return done


def select_keys(core, keep, index_q, index_k, weight, weight_ready, bias, scores, relus, top, index_ready):
    pe, act, dve = core.pe, core.act, core.dve
    v = dve.engine
    allowed = keep.allowed
    assert K_SEL >= P
    dve.mark(v.tensor_copy(bias[:, 0, 0:P], allowed[:, T - P:T]))
    used = [None] * 2
    item = 0
    for t in range(1, TT):
        n = (t + 1) * P
        low = allowed[:, T - P - t * P:T]
        total = scores[t % 2][:, 0:n]
        for h in range(IDX_HEADS):
            b = 4 + item % 4
            pe.wait(core.bank_read[b], *index_ready)
            scored = pe.mark(pe.engine.matmul(core.bank[b][:, 0:n], index_q[:, h // 4, t * P:t * P + P],
                                              index_k[:, h % 4, 0:n], start=True, stop=True))
            relu = relus[item % 2][:, 0:n]
            act.wait(scored, used[item % 2])
            core.bank_read[b] = act.mark(act.engine.activation(relu, core.bank[b][:, 0:n], ACT.Relu))
            dve.wait(core.bank_read[b], weight_ready, dve.latest())
            used[item % 2] = dve.mark(v.scalar_tensor_tensor(
                out=total, in0=relu, scalar=weight[:, t, h:h + 1], in1=low if h == 0 else total,
                op0=ALU.mult, op1=ALU.add))
            item += 1
            yield
        other = scores[2][:, 0:n]
        now = total
        for r in range(K_SEL // 8):
            dve.wait(dve.latest())
            found = dve.mark(v.max(top[:, 8 * (r % 2):8 * (r % 2) + 8], now))
            dve.wait(found)
            v_out = other if now is total else total
            dve.mark(v.match_replace(v_out, top[:, 8 * (r % 2):8 * (r % 2) + 8], now, -3e38))
            now = v_out
            if r % 3 == 2:
                yield
        dve.wait(dve.latest())
        dve.wait(dve.mark(v.tensor_scalar(now, now, -2e38, NEG, ALU.is_gt, ALU.mult)))
        keep.bias_ready = dve.mark(v.tensor_tensor(bias[:, t, 0:n], now, low, ALU.add))
        yield


def block_two(core, dram, keep):
    nc, pe, act, dve, sp = core.nc, core.pe, core.act, core.dve, core.sp
    v = dve.engine
    released = core.meet()
    sp.wait(*released)
    act.wait(*released)
    x = keep.x
    ident = keep.ident[:, :]
    region = Region(nc, keep.rows_at)
    h_high = region.tensor("h2_high", [P, KT, T], F32R)
    h_low = region.tensor("h2_low", [P, KT, T], F32R)
    stream = WeightStream(core, region, "two")
    small = region.tensor("small_two", [P, 4, 64], F32)
    keep.allowed = region.tensor("allowed_sb", [P, T], F32)
    pool_start = region.tensor("pool_start_sb", [P, 64], F32)
    pool_scale = region.tensor("pool_scale_sb", [P, 4], F32)
    merge_bias = region.tensor("merge_bias_sb", [P, 16], F32)
    head_gain = region.tensor("head_gain", [P, 2, HEAD_DIM], F32)
    tables = [core.load(n + "_arrived", tile, dram[n], act) for n, tile in (
        ("allowed", keep.allowed[:, :]), ("pool_start", pool_start[:, :]), ("pool_scale", pool_scale[:, :]),
        ("merge_bias", merge_bias[:, :]))]
    tables.append(core.load("q_gain_arrived", head_gain[:, 0, :], row_of(dram["q_norm_g"], HEAD_DIM), act))
    tables.append(core.load("k_gain_arrived", head_gain[:, 1, :], row_of(dram["k_norm_g"], HEAD_DIM), act))
    (cosine, sine), rotary_ready = rotary_tables(core, dram, region)
    outs_at = region.at
    z_a = region.tensor("z_a", [P, TT, T], F32)
    pooled = region.tensor("pooled", [P, 4, T], F32)
    mixed = region.tensor("z_b", [P, 4, T], F32)
    kvi = region.tensor("k_v_qi", [P, TT, T], F32)
    kiw = region.tensor("ki_wi", [P, TT, 40], F32)
    q_turned = region.tensor("q_turned", [P, 4, T], F32)
    keys = region.tensor("keys", [P, 4, T], F32)
    bias = region.tensor("bias", [P, TT, T], F32)
    index_q = region.tensor("index_q", [P, 2, T], F32)
    shared_at = region.at
    q = region.tensor("q", [P, TT, T], F32)
    index_k = region.tensor("index_k", [P, 4, T], F32)
    index_scores = Region(nc, region.at)
    after_index = region.at
    pool_buffer = [None, None]
    early = Region(nc, outs_at)
    normed = early.tensor("normed_two", [P, TT, D], F32)
    junk = early.tensor("junk_two", [P, D], F32)
    final_gain = early.tensor("final_gain", [P, D], F32)
    final_ready = core.load("final_gain_arrived", final_gain[:, :], row_of(dram["final_norm_g"], D), act)

    w = dram["w_in_2"]
    for columns in ((512, 1024), (1024, 1064), (0, 512), (1064, 1576), (1576, 2088), (2088, 2600)):
        stream.add(w, columns)
    for half in range(2):
        for branch in range(2):
            stream.add(w, (2600 + 1024 * branch + 512 * half, 2600 + 1024 * branch + 512 * half + 512))
        stream.add(dram["w_branch_a"], (half * 512, half * 512 + 512))
        stream.add(dram["w_branch_b"], (half * 512, half * 512 + 512))
    for half in range(2):
        stream.add(dram["w_out_2"], (half * 512, half * 512 + 512))
    stream.load_next()
    stream.load_next()

    dve.wait(final_ready)
    scale, scaled = token_scales(core, x, keep.head_scale, junk, [keep.x_written])
    dve.wait(scaled)
    for t in range(TT):
        kept = dve.mark(v.scalar_tensor_tensor(out=x[:, t, :], in0=x[:, t, :], scalar=scale[:, t:t + 1],
                                               in1=final_gain[:, :], op0=ALU.mult, op1=ALU.mult))
    h_ready = normalise_and_turn(core, x, keep.gains[2], h_high, h_low, keep.head_scale, normed, junk, ident, [kept], range(8))
    core.meet()
    dve.wait(*tables)
    gains_ready = dve.mark(v.tensor_scalar(head_gain[:, 0, :], head_gain[:, 0, :], HEAD_DIM ** -0.5, None, ALU.mult))
    dve.mark(v.memset(keys[:, :, :], 0.0))
    cleared = dve.mark(v.memset(index_k[:, :, :], 0.0))

    work = Region(nc, outs_at)
    square = work.tensor("square", [P, TT * T], F32)
    rotary_work = work.tensor("rotary_work", [P, 4, 256], F32)
    keys_twice = work.tensor("keys_twice", [P, TT, 4, HEAD_DIM], F32)
    index_k_four = work.tensor("index_k_four", [P, TT, 4, IDX_DIM], F32)
    assert work.at <= outs_at + 3 * 8192

    def gather(tensor, chunk, n_chunks, width, first_bank):
        banks = [first_bank + i for i in range(4)]
        summed = project(core, stream, chunk, n_chunks, width, (h_high, h_low), h_ready, True, banks)
        marks = []
        for t, b in enumerate(banks):
            core.bank_read[b] = copy_out(core, act, tensor[:, t, 0:width], core.bank[b][:, 0:width], [summed[t]])
            marks.append(core.bank_read[b])
        return marks

    def turn_out(sources, evacuate, ready):
        b = turn_out.bank = 4 + (turn_out.bank + 1) % 4
        pe.wait(core.bank_read[b], *ready)
        for t in range(TT):
            step = pe.engine.transpose(core.bank[b][:, t * P:t * P + P], sources(t), ident)
        core.bank_read[b] = evacuate(core.bank[b], pe.mark(step))
        return core.bank_read[b]
    turn_out.bank = 3

    kvi_ready = gather(kvi, 0, 2, BANK, 0)
    kiw_ready = gather(kiw, 2, 2, 40, 4)
    q_ready = gather(q, 4, 2, BANK, 0)

    dve.wait(*rotary_ready)
    norm_heads(core, kvi[:, :, 0:128], KV_HEADS, head_gain[:, 1, :], square, small, kvi_ready)
    keys_rotated = rotate(core, kvi[:, :, 0:128], KV_HEADS, HEAD_DIM, 8, cosine, sine, 0, rotary_work)
    rotate(core, kvi[:, :, 256:512], IDX_HEADS, IDX_DIM, 4, cosine, sine, 8, rotary_work)
    dve.wait(*kiw_ready)
    index_rotated = rotate(core, kiw[:, :, 0:IDX_DIM], 1, IDX_DIM, 4, cosine, sine, 8, rotary_work)
    weight = kiw[:, :, IDX_DIM:IDX_DIM + IDX_HEADS]
    weight_ready = dve.mark(v.tensor_scalar(weight, weight, IDX_DIM ** -0.5 * IDX_HEADS ** -0.5, None, ALU.mult))
    act.wait(keys_rotated, index_rotated)
    for g in range(KV_HEADS):
        for again in range(2):
            twice = act.mark(act.engine.activation(keys_twice[:, :, 2 * g + again, :], kvi[:, :, g * 64:g * 64 + 64], ACT.Copy))
    for again in range(4):
        four = act.mark(act.engine.activation(index_k_four[:, :, again, :], kiw[:, :, 0:IDX_DIM], ACT.Copy))

    def spread_index(bank, turned):
        act.wait(turned, cleared)
        for j in range(4):
            rows = slice(32 * j, 32 * j + 32)
            step = act.mark(act.engine.activation(index_k[rows, j, :], bank[rows, :], ACT.Copy))
        return step

    index_ready = [turn_out(lambda t: index_k_four[:, t, :, :].rearrange("p a d -> p (a d)"), spread_index, [four])]
    for c in range(2):
        index_ready.append(turn_out(lambda t: kvi[:, t, 256 + c * P:256 + c * P + P],
                                    lambda bank, turned: copy_out(core, act, index_q[:, c, :], bank[:, :], [turned]),
                                    [index_rotated]))
    keys_ready = []
    for g in range(KV_HEADS):
        def spread_keys(bank, turned):
            act.wait(turned, cleared)
            for half in range(2):
                rows = slice(64 * half, 64 * half + 64)
                step = act.mark(act.engine.activation(keys[rows, 2 * g + half, :], bank[rows, :], ACT.Copy))
            return step
        keys_ready.append(turn_out(lambda t: keys_twice[:, t, 2 * g:2 * g + 2, :].rearrange("p a d -> p (a d)"),
                                   spread_keys, [twice]))
    norm_heads(core, q[:, :, :], A_HEADS, head_gain[:, 0, :], square, small, q_ready + [gains_ready])
    q_rotated = rotate(core, q[:, :, :], A_HEADS, HEAD_DIM, 8, cosine, sine, 0, rotary_work)
    q_turned_ready = []
    for c in range(4):
        q_turned_ready.append(turn_out(lambda t: q[:, t, c * P:c * P + P],
                                       lambda bank, turned: copy_out(core, act, q_turned[:, c, :], bank[:, :], [turned]),
                                       [q_rotated]))

    core.meet()
    buffers = Region(nc, shared_at)
    relus = [buffers.tensor(f"relu{i}", [P, T], F32) for i in range(2)]
    extra = Region(nc, after_index)
    index_total = [extra.tensor("index_total0", [P, T], F32), buffers.tensor("index_total1", [P, T], F32),
                   buffers.tensor("index_total2", [P, T], F32)]
    top = extra.tensor("index_top", [P, 16], F32)
    summing = [extra.tensor(f"summing{i}", [P, 16 + T], F32) for i in range(2)]
    pool_weights = extra.tensor("pool_weights", [P, 4, P], F32)
    pool_weights_ready = core.load("pool_weights_arrived", pool_weights[:, :, :], dram["pool_w"], act)
    background = select_keys(core, keep, index_q, index_k, weight, weight_ready, bias, index_total, relus, top, index_ready)

    def between():
        next(background, None)
        next(background, None)

    summed = project(core, stream, 6, 2, BANK, (h_high, h_low), h_ready, True, range(4), between)
    for t in range(TT):
        core.bank_read[t] = z_a_ready = copy_out(core, act, z_a[:, t, :], core.bank[t][:, :], [summed[t]], func=ACT.Silu)
    summed = project(core, stream, 8, 2, BANK, (h_high, h_low), h_ready, False, range(4), between)
    for buffer in summing:
        zeroed = dve.mark(v.memset(buffer[:, 0:16], 0.0))
    pooled_ready = []
    for g, window in enumerate(POOL_WINDOWS):
        now, other = summing
        dve.wait(dve.latest())
        act.wait(summed[g], dve.latest())
        core.bank_read[g] = copied = act.mark(act.engine.activation(now[:, 16:16 + T], core.bank[g][:, :], ACT.Copy))
        act.wait(copied)
        plain = act.mark(act.engine.activation(pooled[:, g, :], now[:, 16:16 + T], ACT.Copy))
        dve.wait(copied, plain, *tables)
        step = 1
        while step < window:
            dve.wait(dve.mark(v.tensor_tensor(other[:, 16:16 + T], now[:, 16:16 + T], now[:, 16 - step:16 + T - step], ALU.add)))
            now, other = other, now
            step *= 2
        dve.wait(dve.mark(v.tensor_tensor(now[:, 16:16 + 16], now[:, 16:16 + 16], pool_start[:, 16 * g:16 * g + 16], ALU.mult)))
        dve.mark(v.tensor_tensor(pooled[:, g, 0:16], now[:, 16:16 + 16], pooled[:, g, 0:16], ALU.subtract))
        pooled_ready.append(dve.mark(v.scalar_tensor_tensor(
            out=pooled[:, g, 16:T], in0=now[:, 32:16 + T], scalar=1.0 / window, in1=pooled[:, g, 16:T],
            op0=ALU.mult, op1=ALU.subtract)))
    summed = project(core, stream, 10, 2, BANK, (h_high, h_low), h_ready, False, range(4), between)
    for g in range(4):
        core.bank_read[g] = z_b_ready = copy_out(core, act, mixed[:, g, :], core.bank[g][:, :], [summed[g]], func=ACT.Silu)
    for _ in background:
        pass
    for g in range(4):
        pe.wait(core.bank_read[g], pooled_ready[g], pool_weights_ready)
        multiplied = pe.mark(pe.engine.matmul(core.bank[g][:, :], pool_weights[:, g, :], pooled[:, g, :], start=True, stop=True))
        dve.wait(multiplied, z_b_ready, *tables)
        core.bank_read[g] = mixed_ready = dve.mark(v.scalar_tensor_tensor(
            out=mixed[:, g, :], in0=core.bank[g][:, :], scalar=pool_scale[:, g:g + 1], in1=mixed[:, g, :],
            op0=ALU.mult, op1=ALU.mult))

    core.meet()
    buffers = Region(nc, shared_at)
    weights = [buffers.tensor(f"weights{i}", [P, T], F32) for i in range(2)]
    turned_weights = [buffers.tensor(f"turned{i}", [P, T], F32) for i in range(2)]
    attended = buffers.tensor("attended", [P, TT, T], F32)
    highest = small[:, 0, 0:32]
    total = small[:, 1, 0:32]
    items = [(t, h) for t in range(TT) for h in range(A_HEADS)]
    powered, turned_of, applied = {}, {}, {}
    attended_ready = []

    def score(i):
        t, h = items[i]
        n = (t + 1) * P
        b = i % 2
        pe.wait(core.bank_read[b], *keys_ready, *q_turned_ready)
        scored = pe.mark(pe.engine.matmul(core.bank[b][:, 0:n], q_turned[:, h // 2, t * P:t * P + P],
                                          keys[:, 2 * (h // 4) + h % 2, 0:n], start=True, stop=True))
        s = weights[i % 2][:, 0:n]
        dve.wait(scored, turned_of.get(i - 2), keep.bias_ready)
        core.bank_read[b] = dve.mark(v.tensor_tensor_reduce(
            out=s, in0=core.bank[b][:, 0:n], in1=bias[:, t, 0:n], scale=1.0, scalar=-3e38, op0=ALU.add, op1=ALU.max,
            accum_out=highest[:, i:i + 1]))
        dve.wait(core.bank_read[b])
        negated = dve.mark(v.tensor_scalar(highest[:, i:i + 1], highest[:, i:i + 1], -1.0, None, ALU.mult))
        act.wait(negated)
        powered[i] = act.mark(act.engine.activation(s, s, ACT.Exp, bias=highest[:, i:i + 1], accum_out=total[:, i:i + 1]))

    def apply(i):
        t, h = items[i]
        n = (t + 1) * P
        b = 2 + i % 2
        pe.wait(powered[i], core.bank_read[b])
        for j in range(t + 1):
            step = pe.engine.transpose(core.bank[b][:, j * P:j * P + P], weights[i % 2][:, j * P:j * P + P], ident)
        turned_of[i] = pe.mark(step)
        lane = act if i % 2 else dve
        core.bank_read[b] = copied = copy_out(core, lane, turned_weights[i % 2][:, 0:n], core.bank[b][:, 0:n],
                                              [turned_of[i], applied.get(i - 2)])
        out = 4 + t % 2
        pe.wait(copied)
        if h == 0:
            pe.wait(core.bank_read[out])
        group = h // (A_HEADS // KV_HEADS)
        for j in range(t + 1):
            step = pe.engine.matmul(core.bank[out][:, h * HEAD_DIM:(h + 1) * HEAD_DIM], turned_weights[i % 2][:, j * P:j * P + P],
                                    kvi[:, j, P + group * HEAD_DIM:P + (group + 1) * HEAD_DIM], start=(j == 0), stop=(j == t))
        applied[i] = pe.mark(step)
        if h == A_HEADS - 1:
            part = attended[:, t, :].rearrange("p (h d) -> p h d", h=A_HEADS)
            dve.wait(powered[i])
            inverse = dve.mark(v.reciprocal(total[:, t * 8:t * 8 + 8], total[:, t * 8:t * 8 + 8]))
            dve.wait(inverse, applied[i], z_a_ready)
            core.bank_read[out] = dve.mark(v.tensor_tensor(
                part, core.bank[out][:, :].rearrange("p (h d) -> p h d", h=A_HEADS),
                total[:, t * 8:t * 8 + 8].unsqueeze(2).broadcast_to([P, A_HEADS, HEAD_DIM]), ALU.mult))
            dve.wait(core.bank_read[out])
            attended_ready.append(dve.mark(v.tensor_tensor(attended[:, t, :], attended[:, t, :], z_a[:, t, :], ALU.mult)))

    for i in range(len(items) + 1):
        if i < len(items):
            score(i)
        if i:
            apply(i - 1)

    late = Region(nc, outs_at)
    skip = Region(nc, outs_at + 16384)
    a_high = late.tensor("a_high", [P, 4, T], F32R)
    a_low = late.tensor("a_low", [P, 4, T], F32R)
    assert late.at <= outs_at + 16384
    core.meet()
    a_ready = turn_to_pair(core, attended, a_high, a_low, 4, ident, attended_ready, range(4, 8))
    tail = Region(nc, outs_at + 3 * 8192)
    b_high = tail.tensor("b_high", [P, 4, T], F32R)
    b_low = tail.tensor("b_low", [P, 4, T], F32R)
    gate = [tail.tensor(f"gate_two{i}", [P, 4, T], F32) for i in range(2)]
    b_ready = split_pair(core, mixed[:, :, :], b_high[:, :, :], b_low[:, :, :], [mixed_ready])
    core.meet()
    y_high = tail.tensor("y_high", [P, KT, T], F32R)
    y_low = tail.tensor("y_low", [P, KT, T], F32R)
    chunk = 12
    combined_read = None
    y_ready = []
    for half in range(2):
        for branch in range(2):
            banks = [4 * branch + i for i in range(4)]
            summed = project(core, stream, chunk, 2, BANK, (h_high, h_low), h_ready, False, banks)
            chunk += 2
            for i, b in enumerate(banks):
                act.wait(summed[i], combined_read)
                column = branch * KT + half * 4 + i
                core.bank_read[b] = gate_ready = act.mark(act.engine.activation(
                    gate[branch][:, i, :], core.bank[b][:, :], ACT.Sigmoid, bias=merge_bias[:, column:column + 1]))
        gated = [[], []]
        for branch, (pair, ready) in enumerate((((a_high, a_low), a_ready), ((b_high, b_low), b_ready))):
            banks = [4 * branch + i for i in range(4)]
            summed = project(core, stream, chunk, 1, BANK, pair, ready, False, banks)
            chunk += 1
            for i, b in enumerate(banks):
                dve.wait(summed[i], gate_ready)
                core.bank_read[b] = dve.mark(v.tensor_tensor(gate[branch][:, i, :], core.bank[b][:, :], gate[branch][:, i, :], ALU.mult))
        for i in range(4):
            dve.wait(core.bank_read[4 + i])
            added = dve.mark(v.tensor_tensor(gate[0][:, i, :], gate[0][:, i, :], gate[1][:, i, :], ALU.add))
            k = half * 4 + i
            y_ready += split_pair(core, gate[0][:, i, :], y_high[:, k, :], y_low[:, k, :], [added])
        combined_read = y_ready[-1]
    stored = Signal(nc, "out_stored")
    for half in range(2):
        banks = [4 * half + i for i in range(4)]
        summed = project(core, stream, chunk, 2, BANK, (y_high, y_low), y_ready, True, banks)
        chunk += 2
        for t, b in enumerate(banks):
            part = x[:, t, half * BANK:(half + 1) * BANK]
            dve.wait(summed[t])
            core.bank_read[b] = written = dve.mark(v.tensor_tensor(part, part, core.bank[b][:, :], ALU.add))
            sp.wait(written)
            done = stored.after(sp.engine.dma_start(dram["out"].rearrange("(t p) d -> t p d", p=P)[t][:, half * BANK:(half + 1) * BANK], part), 16)
    sp.wait(done)


OUTPUT = "out"


def program(nc, dram):
    dram["gates"] = nc.dram_tensor("gates_scratch", [T // GATE_CHUNK, P, N_KEYS, GATE_CHUNK], F32).ap()
    dram["hidden"] = nc.dram_tensor("hidden_scratch", [N_KEYS, P, T], F32).ap()
    core = Core(nc)
    keep = Kept(core, dram)
    keep.pace = lambda j: 2
    block_one_mixing(core, dram, keep)
    peer(core, dram, keep)
    block_two(core, dram, keep)


def kernel(**inputs):
    import numpy as _np
    import concourse.bacc as _bacc
    from concourse import mybir as _mybir
    from concourse.bass_utils import run_bass_kernel_spmd as _run

    a = {name: _np.asarray(value) for name, value in inputs.items()}

    def columns(vector):
        return vector.reshape(-1, P).T

    laid = {
        "x": a["x"][0],
        "norm_mix_g": columns(a["norm_mix_g"][0]),
        "norm_ffn_g": columns(a["norm_ffn_g"][0]),
        "norm_g_2": columns(a["norm_g_2"][0]),
        "final_norm_g": a["final_norm_g"],
        "w_in": a["w_in"][0],
        "w_out": a["w_out"][0],
        "diff_lambda": a["diff_lambda"][0],
        "diff_subln_g": a["diff_subln_g"][0],
        "peer_wq": a["peer_wq"][0],
        "subkeys": a["peer_subkeys"][0].reshape(HP, N_KEYS, P).transpose(2, 0, 1),
        "peer_u": a["peer_u"][0].reshape(N_KEYS, N_KEYS, KT, P).transpose(1, 3, 2, 0),
        "peer_v": a["peer_v"][0].reshape(N_KEYS, N_KEYS, D),
        "positions": a["positions_2"].reshape(TT, P).T,
        "w_in_2": a["w_in_2"][0],
        "merge_bias": columns(a["merge_bias_2"][0].reshape(-1)),
        "q_norm_g": a["q_norm_g_2"][0],
        "k_norm_g": a["k_norm_g_2"][0],
        "pool_w": a["pool_w_2"][0].transpose(1, 0, 2),
        "pool_scale": columns(a["pool_scale_2"][0]),
        "w_branch_a": a["w_branch_a_2"][0],
        "w_branch_b": a["w_branch_b_2"][0],
        "w_out_2": a["w_out_2"][0],
    }
    laid.update(constants())
    nc = _bacc.Bacc("TRN2", target_bir_lowering=False, num_devices=1)
    arrays, dram = {}, {}
    for name, array in laid.items():
        array = _np.ascontiguousarray(array)
        arrays[f"in_{name}"] = array
        dram[name] = nc.dram_tensor(f"in_{name}", array.shape, _mybir.dt.from_np(array.dtype), kind="ExternalInput").ap()
    dram[OUTPUT] = nc.dram_tensor("result", (T, D), F32, kind="ExternalOutput").ap()
    program(nc, dram)
    result = _run(nc, [arrays], core_ids=[0]).results[0]["result"]
    return result.reshape(1, T, D)
```

```python
from concourse import mybir
import concourse.bass as bass
import numpy as np

F32 = mybir.dt.float32
F32R = mybir.dt.float32r
F16 = mybir.dt.float16
I32 = mybir.dt.int32
U32 = mybir.dt.uint32
ALU = mybir.AluOpType
ACT = mybir.ActivationFunctionType
AX_X = mybir.AxisListType.X

P = 128
T = 512
D = 1024
TT = T // P
KT = D // P
BANK = 512
RMS_EPS = 1e-6
NEG = -1e30

RET_HEADS, RET_D = 4, 128
DIFF_HEADS, DIFF_DQK, DIFF_DV = 4, 64, 128
LAMBDA_INIT = 0.8 - 0.6 * float(np.exp(-0.3 * 0))

PEER_HEADS, PEER_TOPK, N_KEYS = 8, 16, 128
HK = PEER_HEADS * PEER_TOPK
HP = PEER_HEADS * 2

A_HEADS, KV_HEADS, HEAD_DIM = 8, 2, 64
IDX_HEADS, IDX_DIM = 8, 32
K_SEL = min(256, T // 4)
ROPE_THETA = 500000.0
POOL_WINDOWS = (2, 4, 8, 16)


class Signal:

    def __init__(self, nc, name):
        self.semaphore = nc.alloc_semaphore(name)
        self.value = 0

    def after(self, instruction, amount=1):
        instruction.then_inc(self.semaphore, amount)
        self.value += amount
        return (self, self.value)


class Lane:

    def __init__(self, nc, engine, name):
        self.engine = engine
        self.finished = Signal(nc, name + "_finished")
        self.seen = {}

    def wait(self, *marks):
        for mark in marks:
            if mark is None:
                continue
            signal, value = mark
            if self.seen.get(signal, 0) < value:
                self.engine.wait_ge(signal.semaphore, value)
                self.seen[signal] = value

    def mark(self, instruction):
        return self.finished.after(instruction)

    def latest(self):
        return (self.finished, self.finished.value) if self.finished.value else None


class Region:

    def __init__(self, nc, start):
        self.nc, self.at = nc, start

    def tensor(self, name, shape, dtype):
        size = int(np.prod(shape[1:])) * mybir.dt.size(dtype)
        made = self.nc.alloc_sbuf_tensor_at(name, list(shape), dtype, offset=self.at)
        self.at += (size + 63) // 64 * 64
        return made


class Core:

    def __init__(self, nc):
        self.nc = nc
        self.pe = Lane(nc, nc.tensor, "tensor")
        self.act = Lane(nc, nc.scalar, "scalar")
        self.dve = Lane(nc, nc.vector, "vector")
        self.pool = Lane(nc, nc.gpsimd, "gpsimd")
        self.sp = Lane(nc, nc.sync, "sync")
        self.bank = [nc.alloc_psum_tensor(f"bank{i}", [P, BANK], F32) for i in range(8)]
        self.bank_read = [None] * 8
        self.stored = []

    def load(self, name, out, in_, queue=None):
        lane = queue or self.sp
        return Signal(self.nc, name).after(lane.engine.dma_start(out, in_), 16)

    def meet(self):
        lanes = (self.pe, self.act, self.dve, self.pool)
        marks = [lane.latest() for lane in lanes]
        for lane in lanes:
            lane.wait(*marks)
        return [m for m in marks if m]


def split_pair(core, source, high, low, ready, scale=None):
    act, dve = core.act, core.dve
    act.wait(*ready)
    if scale is None:
        high_ready = act.mark(act.engine.activation(high, source, ACT.Copy))
    else:
        high_ready = act.mark(act.engine.activation(high, source, ACT.Copy, scale=scale))
    dve.wait(*ready)
    dve.wait(high_ready)
    if scale is None:
        low_ready = dve.mark(dve.engine.tensor_tensor(low, source, high.bitcast(F32), ALU.subtract))
    else:
        low_ready = dve.mark(dve.engine.scalar_tensor_tensor(
            out=low, in0=source, scalar=scale, in1=high.bitcast(F32), op0=ALU.mult, op1=ALU.subtract))
    return [high_ready, low_ready]


def three_products(engine, out, left, right, first, last):
    (lh, ll), (rh, rl) = left, right
    engine.matmul(out, lh, rh, start=first, stop=False)
    engine.matmul(out, lh, rl, start=False, stop=False)
    return engine.matmul(out, ll, rh, start=False, stop=last)


class WeightStream:

    ROWS, RAW, PAIRS = 2, 3, 3
    BYTES = ROWS * BANK * 4 * (RAW + 2 * PAIRS)

    def __init__(self, core, region):
        self.core = core
        shape = [P, self.ROWS, BANK]
        self.raw = [region.tensor(f"weights_raw{i}", shape, F32) for i in range(self.RAW)]
        self.high = [region.tensor(f"weights_high{i}", shape, F32R) for i in range(self.PAIRS)]
        self.low = [region.tensor(f"weights_low{i}", shape, F32R) for i in range(self.PAIRS)]
        self.arrived = [Signal(core.nc, f"weights_arrived{i}") for i in range(self.RAW)]
        self.raw_split = [[] for _ in range(self.RAW)]
        self.pair_used = [None] * self.PAIRS
        self.queue = []
        self.loaded = 0
        self.split = 0
        self.open = 0
        self.landed = {}
        self.ready = {}
        self.next_group = 0

    def add(self, weights, columns, first_row=0):
        view = weights.rearrange("(k p) c -> p k c", p=P)[:, :, columns[0]:columns[1]]
        rows = view.shape[1]
        for k in range(0, rows, self.ROWS):
            k = (k + first_row) % rows
            self.queue.append((view[:, k:k + self.ROWS, :], columns[1] - columns[0]))

    def release(self, *free):
        self.core.sp.wait(*free)
        self.core.act.wait(*free)
        self.core.dve.wait(*free)
        self.open = len(self.queue)
        for _ in range(self.RAW - 1):
            self.load_next()

    def load_next(self):
        n = self.loaded
        if n >= self.open:
            return
        source, width = self.queue[n]
        slot = n % self.RAW
        sp = self.core.sp
        sp.wait(*self.raw_split[slot])
        out = self.raw[slot][:, :, 0:width]
        self.landed[n] = self.arrived[slot].after(sp.engine.dma_start(out, source), 16)
        self.loaded += 1

    def split_next(self):
        if self.split >= self.open:
            return
        n = self.split
        width = self.queue[n][1]
        slot, raw = n % self.PAIRS, n % self.RAW
        self.load_next()
        ready = [self.landed[n], self.pair_used[slot]]
        self.ready[n] = split_pair(self.core, self.raw[raw][:, :, 0:width],
                                   self.high[slot][:, :, 0:width], self.low[slot][:, :, 0:width], ready)
        self.raw_split[raw] = self.ready[n]
        self.split += 1

    def pair(self, n):
        return self.high[n % self.PAIRS], self.low[n % self.PAIRS]


def project(core, stream, tiles, width, data, data_ready, token_major, banks, between=None, first_row=0):
    pe = core.pe
    high, low = data
    marks = []
    chunk = stream.next_group
    n_chunks = tiles // stream.ROWS
    stream.next_group += n_chunks
    for c in range(chunk, chunk + n_chunks):
        while stream.split < min(c + 2, stream.open):
            stream.split_next()
        weight_high, weight_low = stream.pair(c)
        pe.wait(*stream.ready[c])
        for tile in range(4):
            b = banks[tile]
            if c == chunk:
                pe.wait(core.bank_read[b])
            for r in range(stream.ROWS):
                step = (c - chunk) * stream.ROWS + r
                k = (step + first_row) % tiles
                if tile == 0:
                    pe.wait(*data_ready[k])
                part = slice(tile * P, tile * P + P)
                first, last = step == 0, step == tiles - 1
                if token_major:
                    left = (high[:, k, part], low[:, k, part])
                    right = (weight_high[:, r, 0:width], weight_low[:, r, 0:width])
                    out = core.bank[b][:, 0:width]
                else:
                    left = (weight_high[:, r, part], weight_low[:, r, part])
                    right = (high[:, k, :], low[:, k, :])
                    out = core.bank[b][:, :]
                done = three_products(pe.engine, out, left, right, first, last)
            mark = pe.mark(done)
            if between is not None:
                between()
            if c == chunk + n_chunks - 1:
                marks.append(mark)
        stream.pair_used[c % stream.PAIRS] = mark
    return marks


def copy_out(core, lane, out, source, ready, **kw):
    lane.wait(*ready)
    if lane is core.act:
        return lane.mark(lane.engine.activation(out, source, kw.get("func", ACT.Copy), scale=kw.get("scale", 1.0)))
    if "scale" in kw:
        return lane.mark(lane.engine.tensor_scalar(out, source, kw["scale"], None, ALU.mult))
    return lane.mark(lane.engine.tensor_copy(out, source))


def rms_scale(core, sums, scratch, out, n, ready):
    dve, act = core.dve, core.act
    dve.wait(*ready)
    mean = dve.mark(dve.engine.tensor_scalar(scratch, sums, 1.0 / n, RMS_EPS, ALU.mult, ALU.add))
    act.wait(mean)
    root = act.mark(act.engine.activation(scratch, scratch, ACT.Sqrt))
    dve.wait(root)
    return dve.mark(dve.engine.reciprocal(out, scratch))


def token_scales(core, x, small, junks, ready):
    act, dve = core.act, core.dve
    sums, scratch, scale = (small[:, 4 * i:4 * i + 4] for i in range(3))
    summed = []
    for t in range(TT):
        lane = act if t % 2 else dve
        lane.wait(*ready[t])
        lane.wait(lane.latest())
        if lane is act:
            summed.append(act.mark(act.engine.activation(junks[0][:, :], x[:, t, :], ACT.Square, accum_out=sums[:, t:t + 1])))
        else:
            summed.append(dve.mark(dve.engine.tensor_tensor_reduce(
                out=junks[1][:, :], in0=x[:, t, :], in1=x[:, t, :], scale=1.0, scalar=0.0, op0=ALU.mult, op1=ALU.add,
                accum_out=sums[:, t:t + 1])))
    marks = []
    for pair in range(2):
        two = slice(2 * pair, 2 * pair + 2)
        mark = rms_scale(core, sums[:, two], scratch[:, two], scale[:, two], D, summed[two])
        marks += [mark, mark]
    return scale, marks


def normalise_and_turn(core, x, gain, high, low, small, normed, junks, ident, ready, banks):
    act, dve = core.act, core.dve
    scale, scaled = token_scales(core, x, small, junks, ready)
    rows = []
    for t in range(TT):
        lane = act if t % 2 else dve
        lane.wait(scaled[t])
        if lane is act:
            rows.append(act.mark(act.engine.activation(normed[:, t, :], x[:, t, :], ACT.Copy, scale=scale[:, t:t + 1])))
        else:
            rows.append(dve.mark(dve.engine.tensor_scalar(normed[:, t, :], x[:, t, :], scale[:, t:t + 1], None, ALU.mult)))
    return turn_to_pair(core, normed, high, low, range(KT), ident, rows, banks, gain)


def turn_to_pair(core, source, high, low, tiles, ident, rows, banks, gain=None):
    pe = core.pe
    ready = {}
    for n, k in enumerate(tiles):
        b = banks[n % len(banks)]
        pe.wait(core.bank_read[b])
        for t in range(TT):
            pe.wait(rows[t])
            turned = pe.engine.transpose(core.bank[b][:, t * P:t * P + P], source[:, t, k * P:k * P + P], ident)
        turned = pe.mark(turned)
        ready[k] = split_pair(core, core.bank[b][:, :], high[:, k, :], low[:, k, :], [turned],
                              scale=None if gain is None else gain[:, k:k + 1])
        core.bank_read[b] = ready[k][1]
    return ready


def constants():
    i = np.arange(P, dtype=np.float64)
    later = np.arange(T, dtype=np.float64)[None, :] - i[:, None]
    gamma = 1.0 - 2.0 ** (-5.0 - np.arange(RET_HEADS))
    decay = np.where(later[:, None, :] >= 0, gamma[None, :, None] ** np.maximum(later, 0)[:, None, :], 0.0)
    decay = decay * RET_D ** -0.5
    key = np.arange(T, dtype=np.float64)[None, :] - (T - P)
    distance = i[:, None] - key
    alibi = np.where(distance >= 0, -distance, NEG)
    chunk_end = (np.floor(i / 64) + 1)[:, None] * 64
    allowed = np.where(key < chunk_end, 0.0, NEG)
    pool_start = np.stack([1.0 / np.minimum(np.arange(16) + 1, w) for w in POOL_WINDOWS])
    freq_a = ROPE_THETA ** (-np.arange(8) / 8)
    freq_i = ROPE_THETA ** (-np.arange(4) / 4)
    return {
        "identity": np.eye(P, dtype=np.float32),
        "decay": decay.astype(np.float32).reshape(P, RET_HEADS * T),
        "alibi": alibi.astype(np.float32),
        "allowed": allowed.astype(np.float32),
        "pool_start": np.broadcast_to(pool_start.astype(np.float32).reshape(1, -1), (P, 64)).copy(),
        "frequencies": np.broadcast_to(np.concatenate([freq_a, freq_i]).astype(np.float32), (P, 12)).copy(),
        "counting": np.broadcast_to(np.arange(P, dtype=np.float32), (P, P)).copy(),
    }


def row_of(vector, n):
    return vector.rearrange("(a n) -> a n", a=1).broadcast_to([P, n])


def block_one_mixing(core, dram, keep):
    nc, pe, act, dve, stream = core.nc, core.pe, core.act, core.dve, keep.stream
    ident = keep.ident[:, :]
    x = keep.x
    region = Region(nc, keep.end)
    h_high = region.tensor("h_high", [P, KT, T], F32R)
    h_low = region.tensor("h_low", [P, KT, T], F32R)
    outs_at = region.at
    feature = {n: region.tensor(n, [P, 4, T], F32) for n in ("ret_q", "ret_k", "diff_q")}
    token = {n: region.tensor(n, [P, TT, T], F32) for n in ("ret_v", "ret_gate")}
    early_end = region.at
    feature.update({n: region.tensor(n, [P, 4, T], F32) for n in ("diff_k0", "diff_k1")})
    token["diff_v"] = region.tensor("diff_v", [P, TT, T], F32)
    mix = region.tensor("mix", [P, TT, D], F32)
    ret_weights = region.tensor("ret_weights", [P, 4, T], F32)
    scores = [region.tensor(f"diff_scores{i}", [P, 2, T], F32) for i in range(2)]
    turned_weights = [region.tensor(f"diff_turned{i}", [P, T], F32) for i in range(2)]
    junk = region.tensor("junk_head", [P, P], F32)
    lambda_rows = region.tensor("lambda_rows", [P, 4, DIFF_DQK], F32)
    lambda_sums = region.tensor("lambda_sums", [P, 4], F32)
    subln = region.tensor("subln", [P, DIFF_DV], F32)
    small = region.tensor("mix_small", [P, 64], F32)
    assert region.at <= keep.stream_at
    early = Region(nc, outs_at)
    normed = early.tensor("normed_x", [P, TT, D], F32)
    junks = [early.tensor(f"junk_x{i}", [P, D], F32) for i in range(2)]
    assert early.at <= early_end

    rows_ready = core.load("lambda_rows_in", lambda_rows[:, :, :],
                           dram["diff_lambda"].rearrange("(a q) d -> a q d", a=1).broadcast_to([P, 4, DIFF_DQK]), act)
    subln_ready = core.load("subln_in", subln[:, :], row_of(dram["diff_subln_g"], DIFF_DV), act)
    order = [("diff_q", 4), ("diff_k", 5), ("diff_v", 6), ("ret_q", 0), ("ret_k", 1), ("ret_v", 2), ("ret_gate", 3)]
    for _, g in order:
        stream.add(dram["w_in"], (g * 512, g * 512 + 512))
    for half in range(2):
        stream.add(dram["w_out"], (half * 512, half * 512 + 512), first_row=4)
    for g in range(4):
        stream.add(dram["peer_wq"], (g * 512, g * 512 + 512))
    stream.release()
    v = dve.engine
    dve.mark(v.memset(feature["diff_k0"][64:128, :, :], 0.0))
    dve.mark(v.memset(feature["diff_k1"][0:64, :, :], 0.0))
    h_ready = normalise_and_turn(core, x, keep.gains[0], h_high, h_low, small, normed, junks, ident,
                                 [[mark] for mark in keep.x_ready], range(8))

    dve.wait(rows_ready)
    for n in range(2):
        summed = dve.mark(v.tensor_tensor_reduce(
            out=lambda_rows[:, 2 * n, :], in0=lambda_rows[:, 2 * n, :], in1=lambda_rows[:, 2 * n + 1, :], scale=1.0,
            scalar=0.0, op0=ALU.mult, op1=ALU.add, accum_out=lambda_sums[:, n:n + 1]))
    act.wait(summed)
    powers = act.mark(act.engine.activation(lambda_sums[:, 2:4], lambda_sums[:, 0:2], ACT.Exp))
    lam = lambda_sums[:, 0:1]
    dve.wait(powers)
    dve.wait(dve.mark(v.tensor_tensor(lam, lambda_sums[:, 2:3], lambda_sums[:, 3:4], ALU.subtract)))
    lam_ready = dve.mark(v.tensor_scalar(lam, lam, LAMBDA_INIT, None, ALU.add))
    dve.wait(subln_ready)
    dve.mark(v.tensor_scalar(subln[:, :], subln[:, :], 1.0 - LAMBDA_INIT, None, ALU.mult))

    result = {}

    def gather(name, banks, between=None):
        token_major = name in token
        summed = project(core, stream, KT, BANK, (h_high, h_low), h_ready, token_major, banks, between)
        marks = []
        for i, b in enumerate(banks):
            source = core.bank[b][:, :]
            if name == "diff_k":
                marks.append(copy_out(core, dve, feature["diff_k0"][0:64, i, :], source[0:64, :], [summed[i]]))
                marks.append(copy_out(core, act, feature["diff_k1"][64:128, i, :], source[64:128, :], [summed[i], marks[-1]]))
            elif name == "diff_q":
                marks.append(copy_out(core, act, feature[name][:, i, :], source, [summed[i]], scale=DIFF_DQK ** -0.5))
            elif name == "ret_gate":
                marks.append(copy_out(core, act, token[name][:, i, :], source, [summed[i]], func=ACT.Silu))
            else:
                out = token[name] if token_major else feature[name]
                marks.append(copy_out(core, act if i % 2 else dve, out[:, i, :], source, [summed[i]]))
            core.bank_read[b] = marks[-1]
        result[name] = marks

    turned_all = [mark for marks in h_ready.values() for mark in marks]
    act.wait(*turned_all)
    dve.wait(*turned_all)
    gather("diff_q", range(4))
    gather("diff_k", range(4, 8))
    gather("diff_v", range(4))

    items = [(h, t) for h in range(DIFF_HEADS) for t in range(TT)]
    averaged, softmaxed, head_out, diff_mixed = {}, {}, {}, []

    def score(i):
        h, t = items[i]
        n = (t + 1) * P
        s = scores[i % 2]
        for half, key in enumerate(("diff_k0", "diff_k1")):
            b = 4 + half
            pe.wait(core.bank_read[b], *result["diff_q"], *result["diff_k"])
            scored = pe.mark(pe.engine.matmul(core.bank[b][:, 0:n], feature["diff_q"][:, h, t * P:t * P + P],
                                              feature[key][:, h, 0:n], start=True, stop=True))
            dve.wait(scored, averaged.get(i - 2))
            core.bank_read[b] = dve.mark(v.scalar_tensor_tensor(
                out=s[:, half, 0:n], in0=keep.alibi[:, T - P - t * P:T], scalar=2.0 ** (-8.0 * (h + 1) / DIFF_HEADS),
                in1=core.bank[b][:, 0:n], op0=ALU.mult, op1=ALU.add))
        base = 8 * (i % 2)
        top, total, share = (small[:, base + 2 * m:base + 2 * m + 2] for m in range(3))
        dve.wait(core.bank_read[b])
        dve.wait(dve.mark(v.tensor_reduce(top, s[:, :, 0:n], AX_X, ALU.max)))
        negated = dve.mark(v.tensor_scalar(top, top, -1.0, None, ALU.mult))
        act.wait(negated)
        for half in range(2):
            powered = act.mark(act.engine.activation(s[:, half, 0:n], s[:, half, 0:n], ACT.Exp,
                                                     bias=top[:, half:half + 1], accum_out=total[:, half:half + 1]))
        return s, n, total, share, powered

    def subtract(i, s, n, total, share, powered):
        dve.wait(powered)
        dve.wait(dve.mark(v.reciprocal(share, total)), lam_ready)
        dve.wait(dve.mark(v.tensor_scalar(share[:, 1:2], share[:, 1:2], lam, None, ALU.mult)))
        dve.wait(dve.mark(v.tensor_scalar(s[:, 1, 0:n], s[:, 1, 0:n], share[:, 1:2], None, ALU.mult)))
        softmaxed[i] = dve.mark(v.scalar_tensor_tensor(
            out=s[:, 0, 0:n], in0=s[:, 0, 0:n], scalar=share[:, 0:1], in1=s[:, 1, 0:n], op0=ALU.mult, op1=ALU.subtract))

    def weigh(i):
        h, t = items[i]
        n = (t + 1) * P
        pe.wait(softmaxed[i], core.bank_read[6])
        for j in range(t + 1):
            turned = pe.engine.transpose(core.bank[6][:, j * P:j * P + P], scores[i % 2][:, 0, j * P:j * P + P], ident)
        averaged[i] = turned = pe.mark(turned)
        copied = copy_out(core, act, turned_weights[i % 2][:, 0:n], core.bank[6][:, 0:n], [turned, head_out.get(i - 2)])
        core.bank_read[6] = copied
        return copied

    def multiply(i, copied):
        h, t = items[i]
        pe.wait(copied, *result["diff_v"])
        if t == 0:
            pe.wait(core.bank_read[7])
        for j in range(t + 1):
            step = pe.engine.matmul(core.bank[7][:, t * P:t * P + P], turned_weights[i % 2][:, j * P:j * P + P],
                                    token["diff_v"][:, j, h * P:h * P + P], start=(j == 0), stop=(j == t))
        head_out[i] = pe.mark(step)
        if t == TT - 1:
            core.bank_read[7] = copy_out(core, act, mix[:, :, h * P:h * P + P],
                                         core.bank[7][:, :].rearrange("p (t v) -> p t v", t=TT), [head_out[i]])
            diff_mixed.append(core.bank_read[7])

    rows_mixed = [None] * TT

    def norm_heads_of(first, ready, factor):
        sums, scratch, scale = (keep.head_scale[:, 32 * m + 4 * first:32 * m + 4 * first + 16] for m in range(3))
        dve.wait(*ready)
        for h in range(4):
            for t in range(TT):
                head = mix[:, t, (first + h) * P:(first + h) * P + P]
                dve.wait(dve.latest())
                summed = dve.mark(v.tensor_tensor_reduce(
                    out=junk[:, :], in0=head, in1=head, scale=1.0, scalar=0.0, op0=ALU.mult, op1=ALU.add,
                    accum_out=sums[:, 4 * t + h:4 * t + h + 1]))
            yield
        dve.wait(rms_scale(core, sums, scratch, scale, P, [summed]))
        for t in range(TT):
            for h in range(4):
                head = mix[:, t, (first + h) * P:(first + h) * P + P]
                rows_mixed[t] = dve.mark(v.scalar_tensor_tensor(
                    out=head, in0=head, scalar=scale[:, 4 * t + h:4 * t + h + 1], in1=factor(h, t), op0=ALU.mult, op1=ALU.mult))
            yield

    def attention():
        waiting, copied = {}, {}
        for i in range(len(items) + 3):
            if i < len(items):
                waiting[i] = score(i)
                yield
            if 0 <= i - 1 < len(items):
                subtract(i - 1, *waiting[i - 1])
                yield
                copied[i - 1] = weigh(i - 1)
            if 0 <= i - 2 < len(items):
                multiply(i - 2, copied[i - 2])
                yield
        yield from norm_heads_of(0, diff_mixed, lambda h, t: subln[:, :])

    background = attention()

    for name in ("ret_q", "ret_k", "ret_v"):
        gather(name, range(4), lambda: next(background, None))

    ret_used, ret_mixed = [None], []

    def retention():
        for h in range(RET_HEADS):
            for j in range(TT):
                n = (TT - j) * P
                b = 4 + j % 2
                pe.wait(core.bank_read[b], *result["ret_q"], *result["ret_k"])
                scored = pe.mark(pe.engine.matmul(core.bank[b][:, 0:n], feature["ret_k"][:, h, j * P:j * P + P],
                                                  feature["ret_q"][:, h, j * P:T], start=True, stop=True))
                dve.wait(scored, ret_used[0])
                weighted = core.bank_read[b] = dve.mark(v.tensor_tensor(
                    ret_weights[:, j, 0:n], core.bank[b][:, 0:n], keep.decay[:, h * T:h * T + n], ALU.mult))
                yield
            b = 6 + h % 2
            pe.wait(core.bank_read[b], weighted, *result["ret_v"])
            for t in range(TT):
                for j in range(t + 1):
                    step = pe.engine.matmul(core.bank[b][:, t * P:t * P + P], ret_weights[:, j, (t - j) * P:(t - j) * P + P],
                                            token["ret_v"][:, j, h * P:h * P + P], start=(j == 0), stop=(j == t))
            ret_used[0] = pe.mark(step)
            core.bank_read[b] = copy_out(core, act, mix[:, :, BANK + h * P:BANK + h * P + P],
                                         core.bank[b][:, :].rearrange("p (t v) -> p t v", t=TT), [ret_used[0]])
            ret_mixed.append(core.bank_read[b])
            yield

    for _ in background:
        pass
    background = retention()
    gather("ret_gate", range(4), lambda: (next(background, None), next(background, None)))
    for _ in background:
        pass

    late = Region(nc, keep.end)
    mix_high = late.tensor("mix_high", [P, KT, T], F32R)
    mix_low = late.tensor("mix_low", [P, KT, T], F32R)
    act.wait(*[mark for mark in (pe.latest(),)])
    dve.wait(pe.latest())
    attention_rows = list(rows_mixed)
    mix_ready = turn_to_pair(core, mix, mix_high, mix_low, range(4), ident, attention_rows, range(4, 8))
    for _ in norm_heads_of(4, ret_mixed + result["ret_gate"], lambda h, t: token["ret_gate"][:, t, h * P:h * P + P]):
        pass
    mix_ready.update(turn_to_pair(core, mix, mix_high, mix_low, range(4, 8), ident, rows_mixed, range(4, 8)))
    x_written = [None] * TT
    for g in range(2):
        banks = [g * 4 + i for i in range(4)]
        summed = project(core, stream, KT, BANK, (mix_high, mix_low), mix_ready, True, banks)
        for t, b in enumerate(banks):
            dve.wait(summed[t])
            part = x[:, t, g * BANK:g * BANK + BANK]
            core.bank_read[b] = x_written[t] = dve.mark(v.tensor_tensor(part, part, core.bank[b][:, :], ALU.add))
    keep.x_rows = [[mark] for mark in x_written]


class Kept:

    def __init__(self, core, dram):
        nc = core.nc
        region = Region(nc, (nc.sbuf_base + 63) // 64 * 64)
        self.x = region.tensor("x", [P, TT, D], F32)
        self.ident = region.tensor("ident", [P, P], F32)
        self.gains = [region.tensor(f"gain{i}", [P, KT], F32) for i in range(3)]
        self.head_scale = region.tensor("head_scale", [P, 96], F32)
        self.rows_at = region.at
        self.decay = region.tensor("decay_sb", [P, RET_HEADS * T], F32)
        self.alibi = region.tensor("alibi_sb", [P, T], F32)
        self.end = region.at
        self.stream_at = (nc.sbuf_usable_end - WeightStream.BYTES) // 64 * 64
        self.stream = WeightStream(core, Region(nc, self.stream_at))
        arrived = Signal(nc, "tables_arrived")
        act = core.act
        arrived.after(act.engine.dma_start(self.ident[:, :], dram["identity"]), 16)
        for tile, name in zip(self.gains, ("norm_mix_g", "norm_ffn_g", "norm_g_2")):
            arrived.after(act.engine.dma_start(tile[:, :], dram[name]), 16)
        arrived.after(act.engine.dma_start(self.decay[:, :], dram["decay"]), 16)
        tables = arrived.after(act.engine.dma_start(self.alibi[:, :], dram["alibi"]), 16)
        self.x_ready = [core.load(f"x_arrived{t}", self.x[:, t, :], dram["x"].rearrange("(t p) d -> p t d", p=P)[:, t, :])
                        for t in range(TT)]
        for lane in (core.pe, core.act, core.dve):
            lane.wait(tables)
        self.x_rows = None


EARLY_BANKS = (0, 1, 2, 3)
GATE_BANKS = (4, 5, 6, 7)
GATE_CHUNK = 64
HOT = 16
GATE_SCALE = 2.0 ** 15
BATCH = 4
GROUP = 4


def peer_scores(core, dram, keep, xn_high, xn_low, region, scores, prologue):
    pe, act, dve, stream = core.pe, core.act, core.dve, keep.stream
    small = region.tensor("ffn_small", [P, 16], F32)
    subkeys = region.tensor("subkeys", [P, HP, N_KEYS], F32)
    query = region.tensor("query", [P, HP, T], F32)
    normed = region.tensor("normed_ffn", [P, TT, D], F32)
    junks = [region.tensor(f"junk_ffn{i}", [P, D], F32) for i in range(2)]
    assert region.at <= keep.u_raw_at
    subkeys_ready = core.load("subkeys_arrived", subkeys[:, :, :], dram["subkeys"])
    xn_ready = normalise_and_turn(core, keep.x, keep.gains[1], xn_high, xn_low, small, normed, junks,
                                  keep.ident[:, :], keep.x_rows, range(8))
    query_ready = []
    for g in range(4):
        banks = [(g % 2) * 4 + i for i in range(4)]
        summed = project(core, stream, KT, BANK, (xn_high, xn_low), xn_ready, False, banks)
        for i, b in enumerate(banks):
            lane = act if i % 2 else dve
            core.bank_read[b] = copy_out(core, lane, query[:, 4 * g + i, :], core.bank[b][:, :], [summed[i]])
            query_ready.append(core.bank_read[b])
    next(prologue)
    marks = []
    for t in range(TT):
        for g in range(4):
            b = (4 * t + g) % 8
            pe.wait(core.bank_read[b], subkeys_ready, *query_ready[4 * g:4 * g + 4])
            for i in range(4):
                scored = pe.engine.matmul(core.bank[b][:, i * P:i * P + P], query[:, 4 * g + i, t * P:t * P + P],
                                          subkeys[:, 4 * g + i, :], start=True, stop=True)
            lane = act if g % 2 else dve
            core.bank_read[b] = copy_out(core, lane, scores[:, t, 4 * g:4 * g + 4, :],
                                         core.bank[b][:, :].rearrange("p (a k) -> p a k", a=4), [pe.mark(scored)])
            marks.append(core.bank_read[b])
    return marks


def top_sixteen(core, pairs):
    dve = core.dve
    v = dve.engine
    first = [dve.mark(v.max(top[:, 0:8], values)) for values, work, top, places in pairs]
    for n, (values, work, top, places) in enumerate(pairs):
        dve.wait(first[n])
        dve.mark(v.max_index(places[:, 0:8], top[:, 0:8], values))
    rest = [dve.mark(v.match_replace(work, top[:, 0:8], values, -3e38)) for values, work, top, places in pairs]
    for n, (values, work, top, places) in enumerate(pairs):
        dve.wait(rest[n])
        first[n] = dve.mark(v.max(top[:, 8:16], work))
    for n, (values, work, top, places) in enumerate(pairs):
        dve.wait(first[n])
        done = dve.mark(v.max_index(places[:, 8:16], top[:, 8:16], work))
    return done


def choose_experts(core, dram, keep, scores, scores_ready, chosen, region):
    pe, act, dve = core.pe, core.act, core.dve
    work = [region.tensor(f"top_work{i}", [P, 2 * N_KEYS], F32) for i in range(2)]
    cand = [region.tensor(f"candidates{i}", [P, PEER_TOPK, PEER_TOPK], F32) for i in range(2)]
    top = region.tensor("top", [P, HP, PEER_TOPK], F32)
    places = region.tensor("places", [P, HP, PEER_TOPK], U32)
    keys = region.tensor("top_keys", [P, HP, PEER_TOPK], F32)
    best = region.tensor("best", [P, PEER_HEADS, PEER_TOPK], F32)
    best_at = region.tensor("best_at", [P, PEER_HEADS, PEER_TOPK], U32)
    digit = region.tensor("digit", [P, 2, PEER_HEADS, PEER_TOPK], U32)
    digit_value = region.tensor("digit_value", [P, 2, PEER_HEADS, PEER_TOPK], F32)
    match = region.tensor("match", [P, PEER_HEADS * PEER_TOPK, PEER_TOPK], F32)
    picked = region.tensor("picked", [P, 3, HK], F32)
    total = region.tensor("gate_total", [P, 2, PEER_HEADS], F32)
    v = dve.engine
    turned = None
    dve.wait(*scores_ready)
    act.wait(*scores_ready)
    yield
    for t in range(TT):
        for hp in range(0, HP, 2):
            done = top_sixteen(core, [(scores[:, t, hp + i, :], work[i][:, 0:N_KEYS], top[:, hp + i, :], places[:, hp + i, :])
                                      for i in range(2)])
            yield
        dve.wait(done)
        keys_ready = dve.mark(v.tensor_copy(keys[:, :, :], places[:, :, :]))
        for h in range(0, PEER_HEADS, 2):
            rows = []
            for i in range(2):
                a = top[:, 2 * (h + i), :].unsqueeze(2).broadcast_to([P, PEER_TOPK, PEER_TOPK])
                b = top[:, 2 * (h + i) + 1, :].unsqueeze(1).broadcast_to([P, PEER_TOPK, PEER_TOPK])
                summed = dve.mark(v.tensor_tensor(cand[i][:, :, :], a, b, ALU.add))
                rows.append((cand[i][:, :, :].rearrange("p a b -> p (a b)"), work[i][:, :], best[:, h + i, :], best_at[:, h + i, :]))
            dve.wait(summed)
            done = top_sixteen(core, rows)
            yield
        gate = picked[:, 2, :].rearrange("p (h k) -> p h k", h=PEER_HEADS)
        dve.wait(done, turned)
        shifted = dve.mark(v.tensor_tensor(gate, best[:, :, :], best[:, :, 0:1].broadcast_to([P, PEER_HEADS, PEER_TOPK]), ALU.subtract))
        act.wait(shifted)
        powered = act.mark(act.engine.activation(picked[:, 2, :], picked[:, 2, :], ACT.Exp))
        dve.mark(v.tensor_scalar(digit[:, 0, :, :], best_at[:, :, :], 4, None, ALU.logical_shift_right))
        split = dve.mark(v.tensor_scalar(digit[:, 1, :, :], best_at[:, :, :], 15, None, ALU.bitwise_and))
        dve.wait(split)
        digits = dve.mark(v.tensor_copy(digit_value[:, :, :, :], digit[:, :, :, :]))
        dve.wait(powered)
        summed = dve.mark(v.tensor_reduce(total[:, 0, :], gate, AX_X, ALU.add))
        dve.wait(summed)
        inverse = dve.mark(v.reciprocal(total[:, 1, :], total[:, 0, :]))
        dve.wait(inverse, digits, keys_ready)
        gated = dve.mark(v.tensor_tensor(gate, gate, total[:, 1, :].unsqueeze(2).broadcast_to([P, PEER_HEADS, PEER_TOPK]), ALU.mult))
        yield
        for half in range(2):
            wide = [P, HK, PEER_TOPK]
            ranks = keep.counting[:, 0:PEER_TOPK].unsqueeze(1).broadcast_to(wide)
            chosen_rank = digit_value[:, half, :, :].rearrange("p h k -> p (h k)").unsqueeze(2).broadcast_to(wide)
            compared = dve.mark(v.tensor_tensor(match[:, :, :], chosen_rank, ranks, ALU.is_equal))
            dve.wait(compared)
            yield
            for h in range(PEER_HEADS):
                part = match[:, h * PEER_TOPK:(h + 1) * PEER_TOPK, :]
                of_rank = keys[:, 2 * h + half, :].unsqueeze(1).broadcast_to([P, PEER_TOPK, PEER_TOPK])
                marked = dve.mark(v.tensor_tensor(part, part, of_rank, ALU.mult))
            dve.wait(marked)
            yield
            picked_ready = dve.mark(v.tensor_reduce(picked[:, half, :], match[:, :, :], AX_X, ALU.add))
            dve.wait(picked_ready)
        b = GATE_BANKS[t % 4]
        pe.wait(picked_ready, gated, core.bank_read[b])
        for i in range(3):
            step = pe.engine.transpose(core.bank[b][:, i * P:i * P + P], picked[:, i, :], keep.ident[:, :])
        turned = pe.mark(step)
        for i in range(3):
            moved = copy_out(core, act, chosen[i][:, t * P:t * P + P], core.bank[b][:, i * P:i * P + P], [turned])
        core.bank_read[b] = moved
        yield
    keep.chosen_ready = moved


def build_gates(core, dram, keep, chosen, region):
    pe, act, dve = core.pe, core.act, core.dve
    key1, key2, gate = chosen
    stages = [region.tensor(f"gate_stage{i}", [P, N_KEYS, GATE_CHUNK], F32) for i in range(2)]
    every_key = region.tensor("every_key", [P, N_KEYS, HOT], F16)
    parts = [region.tensor(f"gate_part{i}", [P, T], F16) for i in range(2)]
    ring = 2
    hot1 = [region.tensor(f"hot1_{i}", [P, N_KEYS, HOT], F16) for i in range(ring)]
    hot2 = region.tensor("hot2", [P, N_KEYS, HOT], F16)
    weighed = [[region.tensor(f"hot2_part{p}_{i}", [P, N_KEYS, HOT], F16) for p in range(2)] for i in range(ring)]
    stored_signal = [Signal(core.nc, f"gates_stored{i}") for i in range(2)]
    v = dve.engine
    shape = [P, N_KEYS, HOT]
    dve.wait(keep.chosen_ready)
    dve.mark(v.tensor_copy(every_key[:, :, :], keep.counting[:, :].unsqueeze(2).broadcast_to(shape)))
    first = dve.mark(v.tensor_scalar(parts[0][:, :], gate[:, :], GATE_SCALE, None, ALU.mult))
    dve.wait(first)
    dve.wait(dve.mark(v.scalar_tensor_tensor(out=parts[1][:, :], in0=gate[:, :], scalar=GATE_SCALE, in1=parts[0][:, :],
                                             op0=ALU.mult, op1=ALU.subtract)))
    yield
    used, hot_ready = [None] * ring, {}
    stored = [None, None]
    blocks = T // HOT

    def make_hot(n):
        part = slice(n * HOT, (n + 1) * HOT)
        dve.wait(used[n % ring])
        dve.mark(v.tensor_tensor(hot1[n % ring][:, :, :], every_key[:, :, :],
                                 key1[:, part].unsqueeze(1).broadcast_to(shape), ALU.is_equal))
        yield
        dve.wait(hot_ready.get(n - 1))
        second = dve.mark(v.tensor_tensor(hot2[:, :, :], every_key[:, :, :],
                                          key2[:, part].unsqueeze(1).broadcast_to(shape), ALU.is_equal))
        dve.wait(second)
        yield
        for p in range(2):
            hot_ready[n] = dve.mark(v.tensor_tensor(weighed[n % ring][p][:, :, :], hot2[:, :, :],
                                                    parts[p][:, part].unsqueeze(1).broadcast_to(shape), ALU.mult))
            yield

    for _ in make_hot(0):
        yield
    for n in range(blocks):
        following = make_hot(n + 1) if n + 1 < blocks else iter(())
        for q in range(HOT // BATCH):
            b = GATE_BANKS[q % 4]
            pe.wait(hot_ready[n], core.bank_read[b])
            for i in range(BATCH):
                for p in range(2):
                    t = q * BATCH + i
                    step = pe.engine.matmul(core.bank[b][:, i * P:i * P + P], hot1[n % ring][:, :, t],
                                            weighed[n % ring][p][:, :, t], start=(p == 0), stop=(p == 1))
            used[n % ring] = built = pe.mark(step)
            at = n * HOT + q * BATCH
            chunk, within = at // GATE_CHUNK, at % GATE_CHUNK
            act.wait(built, stored[chunk % 2])
            core.bank_read[b] = act.mark(act.engine.activation(
                stages[chunk % 2][:, :, within:within + BATCH],
                core.bank[b][:, :].rearrange("p (t k) -> p k t", t=BATCH), ACT.Copy, scale=1.0 / GATE_SCALE))
            if within == GATE_CHUNK - BATCH:
                act.wait(core.bank_read[b])
                stored[chunk % 2] = stored_signal[chunk % 2].after(
                    act.engine.dma_start(dram["gates"][chunk], stages[chunk % 2][:, :, :]), 16)
                keep.gates_stored = list(stored)
            next(following, None)
            yield
        for _ in following:
            yield


def hidden_units(core, dram, keep, xn_high, xn_low, background, following):
    pe, act, dve, sp = core.pe, core.act, core.dve, core.sp
    RAW, PAIR, OUT = 3, 2, 3
    at_raw, at_pairs = Region(core.nc, keep.u_raw_at), Region(core.nc, keep.stream_at)
    raw = [at_raw.tensor(f"u_raw{i}", [P, KT, P], F32) for i in range(RAW)]
    assert at_raw.at <= keep.stream_at
    high = [at_pairs.tensor(f"u_high{i}", [P, KT, P], F32R) for i in range(PAIR)]
    low = [at_pairs.tensor(f"u_low{i}", [P, KT, P], F32R) for i in range(PAIR)]
    out = [at_pairs.tensor(f"hidden{i}", [P, T], F32) for i in range(OUT)]
    arrived = [Signal(core.nc, f"u_arrived{i}") for i in range(RAW)]
    stored = [Signal(core.nc, f"hidden_stored{i}") for i in range(OUT)]
    stored_at = [None] * OUT
    split_of, landed, product_of = {}, {}, {}

    def load(j):
        sp.wait(*split_of.get(j - RAW, []))
        landed[j] = arrived[j % RAW].after(sp.engine.dma_start(raw[j % RAW][:, :, :], dram["peer_u"][j]), 16)

    def split(j):
        split_of[j] = split_pair(core, raw[j % RAW][:, :, :], high[j % PAIR][:, :, :], low[j % PAIR][:, :, :],
                                 [landed[j], product_of.get(j - PAIR)])

    for j in range(RAW):
        load(j)
    act.wait(core.pe.latest())
    dve.wait(core.pe.latest())
    split(0)
    yield
    for j in range(N_KEYS):
        if j + 1 < N_KEYS:
            split(j + 1)
        b = EARLY_BANKS[j % 4]
        pe.wait(*split_of[j], core.bank_read[b])
        for k in range(KT):
            step = three_products(pe.engine, core.bank[b][:, :], (high[j % PAIR][:, k, :], low[j % PAIR][:, k, :]),
                                  (xn_high[:, k, :], xn_low[:, k, :]), k == 0, k == KT - 1)
        product_of[j] = pe.mark(step)
        for _ in range(pace(j)):
            next(background, None)
        if j + RAW < N_KEYS:
            load(j + RAW)
        act.wait(product_of[j], stored_at[j % OUT])
        core.bank_read[b] = act.mark(act.engine.activation(out[j % OUT][:, :], core.bank[b][:, :], ACT.Gelu))
        sp.wait(core.bank_read[b])
        stored_at[j % OUT] = stored[j % OUT].after(sp.engine.dma_start(dram["hidden"][j], out[j % OUT][:, :]), 16)
        if (j + 1) % GROUP == 0:
            keep.hidden_stored[j // GROUP] = [stored_at[m % OUT] for m in range(max(0, j - OUT + 1), j + 1)]
        if j == N_KEYS - 4:
            for _ in background:
                pass
            next(following)


def combine(core, dram, keep, region):
    pe, act, dve, sp, pool = core.pe, core.act, core.dve, core.sp, core.pool
    chunks = T // GATE_CHUNK
    gate = [region.tensor(f"gate_in{i}", [P, chunks, GROUP, GATE_CHUNK], F32) for i in range(2)]
    hidden = [region.tensor(f"hidden_in{i}", [P, GROUP, T], F32) for i in range(2)]
    value = [region.tensor(f"v_raw{i}", [P, GROUP, BANK], F32) for i in range(2)]
    keep.values_at = region.at
    value_pair = [[region.tensor(f"v_{n}{i}", [P, GROUP, BANK], F32R) for n in ("high", "low")] for i in range(2)]
    early = [region.tensor(f"w_{n}0", [P, GROUP, T], F32R) for n in ("high", "low")]
    assert region.at <= keep.u_raw_at
    after_xn = Region(core.nc, keep.rows_at)
    late = [after_xn.tensor(f"w_{n}1", [P, GROUP, T], F32R) for n in ("high", "low")]
    weight_pair = [early, late]
    arrived = {n: [Signal(core.nc, f"{n}_arrived{i}") for i in range(2)] for n in ("gate", "hid", "v")}
    groups = N_KEYS // GROUP
    split_of, landed, half_done, multiplied, weight_ready = {}, {}, {}, {}, {}

    def load_weights(g):
        s = g % 2
        sp.wait(*keep.gates_stored, *keep.hidden_stored[g], *weight_ready.get(g - 2, []))
        for c in range(chunks):
            mark = arrived["gate"][s].after(sp.engine.dma_start(
                gate[s][:, c, :, :], dram["gates"][c][:, g * GROUP:(g + 1) * GROUP, :]), 16)
        landed["w", g] = [mark, arrived["hid"][s].after(sp.engine.dma_start(
            hidden[s][:, :, :], dram["hidden"][g * GROUP:(g + 1) * GROUP].rearrange("j p t -> p j t")), 16)]

    def load_values(n):
        g, half = n // 2, n % 2
        sp.wait(*split_of.get(n - 2, []))
        landed["v", n] = arrived["v"][n % 2].after(sp.engine.dma_start(
            value[n % 2][:, :, :], dram["peer_v"][:, g * GROUP:(g + 1) * GROUP, half * BANK:(half + 1) * BANK]), 16)

    def prepare_values(n):
        high, low = value_pair[n % 2]
        split_of[n] = split_pair(core, value[n % 2][:, :, :], high[:, :, :], low[:, :, :],
                                 [landed["v", n], half_done.get(n - 2)])

    def prepare_weights(g):
        s = g % 2
        product = hidden[s][:, :, :].rearrange("p j (c t) -> p j c t", c=chunks)
        dve.wait(*landed["w", g])
        for j in range(GROUP):
            step = dve.engine.tensor_tensor(product[:, j, :, :], product[:, j, :, :], gate[s][:, :, j, :], ALU.mult)
        multiplied[g] = dve.mark(step)
        high, low = weight_pair[s]
        weight_ready[g] = split_pair(core, hidden[s][:, :, :], high[:, :, :], low[:, :, :],
                                     [multiplied[g], half_done.get(2 * (g - 2) + 1)])

    built = [core.pe.latest(), core.act.latest(), core.dve.latest(), *keep.gates_stored]
    for lane in (sp, act, dve):
        lane.wait(*built)
    load_weights(0)
    load_values(0)
    load_values(1)
    load_weights(1)
    prepare_weights(0)
    prepare_values(0)
    yield
    act.wait(pe.latest())
    dve.wait(pe.latest())
    keep.x_rows = x_rows = [[None, None] for _ in range(TT)]
    for n in range(2 * groups):
        g, half = n // 2, n % 2
        if n + 1 < 2 * groups:
            prepare_values(n + 1)
        if n + 2 < 2 * groups:
            load_values(n + 2)
        if half == 0 and g + 1 < groups:
            prepare_weights(g + 1)
            if g + 2 < groups:
                load_weights(g + 2)
        if n == 2 * groups - 2:
            yield
        value_high, value_low = value_pair[n % 2]
        weight_high, weight_low = weight_pair[g % 2]
        pe.wait(*split_of[n], *weight_ready[g])
        for t in range(TT):
            b = 4 * half + t
            pe.wait(core.bank_read[b])
            for j in range(GROUP):
                part = slice(t * P, t * P + P)
                step = three_products(pe.engine, core.bank[b][:, :], (weight_high[:, j, part], weight_low[:, j, part]),
                                      (value_high[:, j, :], value_low[:, j, :]), j == 0, j == GROUP - 1)
            half_done[n] = pe.mark(step)
            out = keep.x[:, t, half * BANK:(half + 1) * BANK]
            dve.wait(half_done[n])
            core.bank_read[b] = x_rows[t][half] = dve.mark(dve.engine.tensor_tensor(out, out, core.bank[b][:, :], ALU.add))
            if n == 2 * groups - 1:
                yield


def pace(j):
    return 1 if j < 66 else 3


def peer(core, dram, keep):
    nc = core.nc
    core.sp.wait(*core.meet())
    region = Region(nc, keep.rows_at)
    xn_high = region.tensor("xn_high", [P, KT, T], F32R)
    xn_low = region.tensor("xn_low", [P, KT, T], F32R)
    keep.counting = region.tensor("counting_sb", [P, P], F32)
    chosen = [region.tensor(n, [P, T], dtype) for n, dtype in (("key1", F16), ("key2", F16), ("gate", F32))]
    scores_at = keep.scores_at = region.at
    scores = region.tensor("scores", [P, TT, HP, N_KEYS], F32)
    after_scores = region.at
    keep.hidden_stored = {}
    keep.u_raw_at = keep.stream_at - 3 * KT * P * 4

    def background():
        yield from choose_experts(core, dram, keep, scores, scores_ready, chosen, Region(nc, after_scores))
        core.act.wait(core.dve.latest(), core.pe.latest())
        core.dve.wait(core.act.latest(), core.pe.latest())
        yield from build_gates(core, dram, keep, chosen, Region(nc, scores_at))

    core.dve.wait(core.load("counting_arrived", keep.counting[:, :], dram["counting"], core.act))
    combining = combine(core, dram, keep, Region(nc, scores_at))
    hidden = hidden_units(core, dram, keep, xn_high, xn_low, background(), combining)
    scores_ready = peer_scores(core, dram, keep, xn_high, xn_low, Region(nc, after_scores), scores, hidden)
    for _ in hidden:
        pass
    keep.first_stage_done = [core.pe.latest(), core.act.latest(), core.dve.latest(), *keep.gates_stored,
                             *keep.hidden_stored[N_KEYS // GROUP - 1]]
    next(combining)
    return combining


TWO_PI = 2.0 * float(np.pi)
TURN = (6.28125, float(np.float32(1.9350051879882812e-03)), 0.0)
TURN = (TURN[0], TURN[1], TWO_PI - TURN[0] - TURN[1])
ROUND = 1.5 * 2.0 ** 23
PI_BELOW = 3.1415925
FREQS = 12


def rotary_tables(core, dram, region):
    act, dve = core.act, core.dve
    v = dve.engine
    position = region.tensor("position", [P, TT], I32)
    position_value = region.tensor("position_value", [P, TT], F32)
    frequency = region.tensor("frequency", [P, FREQS], F32)
    angle = region.tensor("angle", [P, TT, FREQS], F32)
    turns = region.tensor("turns", [P, TT, FREQS], F32)
    tables = [region.tensor(n, [P, TT, FREQS], F32) for n in ("cosine", "sine")]
    loaded = [core.load("position_arrived", position[:, :], dram["positions"], act),
              core.load("frequency_arrived", frequency[:, :], dram["frequencies"], act)]
    dve.wait(*loaded)
    dve.wait(dve.mark(v.tensor_copy(position_value[:, :], position[:, :])))
    shape = [P, TT, FREQS]
    dve.wait(dve.mark(v.tensor_tensor(angle[:, :, :], position_value[:, :].unsqueeze(2).broadcast_to(shape),
                                      frequency[:, :].unsqueeze(1).broadcast_to(shape), ALU.mult)))
    ready = []
    for table, quarter in zip(tables, (0.25, 0.0)):
        dve.wait(dve.mark(v.tensor_scalar(turns[:, :, :], angle[:, :, :], 1.0 / TWO_PI, quarter, ALU.mult, ALU.add)))
        dve.wait(dve.mark(v.tensor_scalar(turns[:, :, :], turns[:, :, :], ROUND, None, ALU.add)))
        dve.wait(dve.mark(v.tensor_scalar(turns[:, :, :], turns[:, :, :], ROUND, None, ALU.subtract)))
        source = angle
        for part in TURN:
            dve.wait(dve.mark(v.scalar_tensor_tensor(out=table[:, :, :], in0=turns[:, :, :], scalar=-part,
                                                     in1=source[:, :, :], op0=ALU.mult, op1=ALU.add)))
            source = table
        dve.wait(dve.mark(v.tensor_scalar(table[:, :, :], table[:, :, :], quarter * TWO_PI, PI_BELOW, ALU.add, ALU.min)))
        reduced = dve.mark(v.tensor_scalar(table[:, :, :], table[:, :, :], -PI_BELOW, None, ALU.max))
        dve.wait(reduced)
        act.wait(reduced)
        ready.append(act.mark(act.engine.activation(table[:, :, :], table[:, :, :], ACT.Sin)))
    return tables, ready


def rotate(core, tensor, heads, width, pairs, cosine, sine, at, scratch):
    dve = core.dve
    v = dve.engine
    view = tensor.rearrange("p t (h d) -> p t h d", h=heads)
    one, two = view[:, :, :, 0:pairs], view[:, :, :, pairs:2 * pairs]
    shape = [P, TT, heads, pairs]
    c = cosine[:, :, at:at + pairs].unsqueeze(2).broadcast_to(shape)
    s = sine[:, :, at:at + pairs].unsqueeze(2).broadcast_to(shape)
    size = TT * heads * pairs
    parts = [scratch[:, i, 0:size].rearrange("p (t h d) -> p t h d", t=TT, h=heads) for i in range(4)]
    for out, a, b in ((parts[0], one, c), (parts[1], two, s), (parts[2], one, s), (parts[3], two, c)):
        product = dve.mark(v.tensor_tensor(out, a, b, ALU.mult))
    dve.wait(product)
    dve.mark(v.tensor_tensor(one, parts[0], parts[1], ALU.subtract))
    done = dve.mark(v.tensor_tensor(two, parts[2], parts[3], ALU.add))
    dve.wait(done)
    return done


def norm_heads(core, tensor, heads, gain, square, small, ready):
    dve = core.dve
    v = dve.engine
    view = tensor.rearrange("p t (h d) -> p t h d", h=heads)
    squared = square[:, 0:TT * heads * HEAD_DIM].rearrange("p (t h d) -> p t h d", t=TT, h=heads)
    sums, scratch, scale = (small[:, i, 0:TT * heads] for i in range(3))
    dve.wait(*ready)
    dve.wait(dve.mark(v.tensor_tensor(squared, view, view, ALU.mult)))
    yield
    summed = dve.mark(v.tensor_reduce(sums, square[:, 0:TT * heads * HEAD_DIM].rearrange("p (a d) -> p a d", d=HEAD_DIM),
                                      AX_X, ALU.add))
    yield
    scaled = rms_scale(core, sums, scratch, scale, HEAD_DIM, [summed])
    dve.wait(scaled)
    shape = [P, TT, heads, HEAD_DIM]
    dve.wait(dve.mark(v.tensor_tensor(view, view, scale.rearrange("p (t h) -> p t h", t=TT).unsqueeze(3).broadcast_to(shape), ALU.mult)))
    yield
    for t in range(TT):
        done = dve.mark(v.tensor_tensor(view[:, t, :, :], view[:, t, :, :],
                                        gain.unsqueeze(1).broadcast_to([P, heads, HEAD_DIM]), ALU.mult))
    dve.wait(done)
    yield


def select_keys(core, t, allowed, index_q, index_k, weight, bias, totals, relus, used, top, banks, ready, bias_ready):
    pe, act, dve = core.pe, core.act, core.dve
    v = dve.engine
    n = (t + 1) * P
    low = allowed[:, T - n:T]
    total, other = totals[0][:, 0:n], totals[1][:, 0:n]
    for h in range(IDX_HEADS):
        b = banks[h % len(banks)]
        pe.wait(core.bank_read[b], *ready)
        scored = pe.mark(pe.engine.matmul(core.bank[b][:, 0:n], index_q[:, h // 4, t * P:t * P + P],
                                          index_k[:, h % 4, 0:n], start=True, stop=True))
        relu = relus[h % 2][:, 0:n]
        act.wait(scored, used[h % 2])
        core.bank_read[b] = act.mark(act.engine.activation(relu, core.bank[b][:, 0:n], ACT.Relu))
        dve.wait(core.bank_read[b], dve.latest())
        used[h % 2] = dve.mark(v.scalar_tensor_tensor(
            out=total, in0=relu, scalar=weight[:, t, h:h + 1], in1=low if h == 0 else total,
            op0=ALU.mult, op1=ALU.add))
        yield
    now = total
    for r in range(K_SEL // 8):
        best = top[:, 8 * (r % 2):8 * (r % 2) + 8]
        dve.wait(dve.latest())
        dve.wait(dve.mark(v.max(best, now)))
        after = other if now is total else total
        dve.mark(v.match_replace(after, best, now, -3e38))
        now = after
        if r % 2:
            yield
    dve.wait(dve.latest())
    dve.wait(dve.mark(v.tensor_scalar(now, now, -2e38, NEG, ALU.is_gt, ALU.mult)))
    bias_ready[t] = dve.mark(v.tensor_tensor(bias[:, t, 0:n], now, low, ALU.add))
    dve.wait(bias_ready[t])
    yield


def block_two(core, dram, keep, combining):
    nc, pe, act, dve, sp, stream = core.nc, core.pe, core.act, core.dve, core.sp, keep.stream
    v = dve.engine
    x, ident = keep.x, keep.ident[:, :]

    outs = Region(nc, keep.rows_at)
    z_a = outs.tensor("z_a", [P, TT, T], F32)
    mixed = outs.tensor("z_b", [P, 4, T], F32)
    assert outs.at <= keep.rows_at + 16384
    allowed = outs.tensor("allowed_sb", [P, T], F32)
    final_gain = outs.tensor("final_gain", [P, D], F32)
    relus = [outs.tensor(f"relu{i}", [P, T], F32) for i in range(2)]
    totals = [outs.tensor(f"index_total{i}", [P, T], F32) for i in range(2)]
    small = outs.tensor("small_two", [P, 4, 64], F32)
    pool_start = outs.tensor("pool_start_sb", [P, 64], F32)
    pool_scale = outs.tensor("pool_scale_sb", [P, 4], F32)
    merge_bias = outs.tensor("merge_bias_sb", [P, 16], F32)
    head_gain = outs.tensor("head_gain", [P, 2, HEAD_DIM], F32)
    top = outs.tensor("index_top", [P, 16], F32)
    pool_weights = outs.tensor("pool_weights", [P, 4, P], F32)
    rotary = outs
    rows = Region(nc, keep.scores_at)
    pooled = rows.tensor("pooled", [P, 4, T], F32)
    kvi = rows.tensor("k_v_qi", [P, TT, T], F32)
    q_turned = rows.tensor("q_turned", [P, 4, T], F32)
    keys = rows.tensor("keys", [P, 4, T], F32)
    q = rows.tensor("q", [P, TT, T], F32)
    bias = rows.tensor("bias", [P, TT, T], F32)
    assert rows.at == keep.values_at
    h_high = rows.tensor("h2_high", [P, KT, T], F32R)
    h_low = rows.tensor("h2_low", [P, KT, T], F32R)
    work_at = rows.at
    gate = [rows.tensor(f"gate_two{i}", [P, 4, T], F32) for i in range(2)]
    index_q = rows.tensor("index_q", [P, 2, T], F32)
    index_at = rows.at
    index_k = rows.tensor("index_k", [P, 4, T], F32)
    kiw = rows.tensor("ki_wi", [P, TT, IDX_DIM + IDX_HEADS], F32)
    summing = [rows.tensor(f"summing{i}", [P, 16 + T], F32) for i in range(2)]
    index_k_four = rows.tensor("index_k_four", [P, TT, 4, IDX_DIM], F32)
    assert rows.at <= keep.stream_at
    early = Region(nc, keep.scores_at)
    normed = early.tensor("normed_two", [P, TT, D], F32)
    junk = early.tensor("junk_two", [P, D], F32)
    work = Region(nc, work_at)
    square = work.tensor("square", [P, TT * T], F32)
    rotary_work = work.tensor("rotary_work", [P, 4, 256], F32)
    keys_twice = work.tensor("keys_twice", [P, TT, 4, HEAD_DIM], F32)
    assert work.at <= work_at + 16384

    act.wait(*keep.first_stage_done)
    tables = [core.load(n + "_arrived", tile, source, act) for n, tile, source in (
        ("final_gain", final_gain[:, :], row_of(dram["final_norm_g"], D)),
        ("allowed", allowed[:, :], dram["allowed"]), ("pool_start", pool_start[:, :], dram["pool_start"]),
        ("pool_scale", pool_scale[:, :], dram["pool_scale"]), ("merge_bias", merge_bias[:, :], dram["merge_bias"]),
        ("q_gain", head_gain[:, 0, :], row_of(dram["q_norm_g"], HEAD_DIM)),
        ("k_gain", head_gain[:, 1, :], row_of(dram["k_norm_g"], HEAD_DIM)),
        ("pool_weights", pool_weights[:, :, :], dram["pool_w"]))]
    w = dram["w_in_2"]
    for columns in ((512, 1024), (1024, 1064), (0, 512), (1064, 1576), (1576, 2088), (2088, 2600)):
        stream.add(w, columns)
    for half in range(2):
        for branch in range(2):
            stream.add(w, (2600 + 1024 * branch + 512 * half, 2600 + 1024 * branch + 512 * half + 512))
        stream.add(dram["w_branch_b"], (half * 512, half * 512 + 512))
        stream.add(dram["w_branch_a"], (half * 512, half * 512 + 512))
    for half in range(2):
        stream.add(dram["w_out_2"], (half * 512, half * 512 + 512))
    stream.release(*keep.first_stage_done)
    dve.wait(*keep.first_stage_done)
    stream.split_next()
    stream.split_next()
    (cosine, sine), rotary_ready = rotary_tables(core, dram, rotary)
    assert rotary.at <= keep.scores_at
    dve.wait(*tables, *rotary_ready)
    gains_ready = dve.mark(v.tensor_scalar(head_gain[:, 0, :], head_gain[:, 0, :], HEAD_DIM ** -0.5, None, ALU.mult))

    sums = [small[:, i, 0:TT] for i in range(2)]
    scratch, last_scale, both, mean = (small[:, 2, TT * i:TT * i + TT] for i in range(4))
    squared = [None] * TT
    for t in range(TT):
        next(combining)
        act.wait(*keep.x_rows[t], act.latest())
        dve.wait(*keep.x_rows[t])
        first = act.mark(act.engine.activation(junk[:, :], x[:, t, :], ACT.Square, accum_out=sums[0][:, t:t + 1]))
        dve.wait(first)
        gained = dve.mark(v.tensor_tensor(x[:, t, :], x[:, t, :], final_gain[:, :], ALU.mult))
        act.wait(gained)
        squared[t] = act.mark(act.engine.activation(junk[:, :], x[:, t, :], ACT.Square, accum_out=sums[1][:, t:t + 1]))
    for _ in combining:
        pass
    rows_ready, x_scaled = [], []
    for pair in range(2):
        two = slice(2 * pair, 2 * pair + 2)
        dve.wait(rms_scale(core, sums[0][:, two], scratch[:, two], last_scale[:, two], D, squared[two]))
        dve.wait(dve.mark(v.tensor_tensor(mean[:, two], sums[1][:, two], last_scale[:, two], ALU.mult)))
        meant = dve.mark(v.tensor_tensor(mean[:, two], mean[:, two], last_scale[:, two], ALU.mult))
        dve.wait(rms_scale(core, mean[:, two], scratch[:, two], both[:, two], D, [meant]))
        scaled = dve.mark(v.tensor_tensor(both[:, two], both[:, two], last_scale[:, two], ALU.mult))
        for t in range(2 * pair, 2 * pair + 2):
            lane = act if t % 2 else dve
            lane.wait(scaled)
            if lane is act:
                rows_ready.append(act.mark(act.engine.activation(normed[:, t, :], x[:, t, :], ACT.Copy, scale=both[:, t:t + 1])))
            else:
                rows_ready.append(dve.mark(v.tensor_scalar(normed[:, t, :], x[:, t, :], both[:, t:t + 1], None, ALU.mult)))
    h_ready = turn_to_pair(core, normed, h_high, h_low, range(KT), ident, rows_ready, range(8), keep.gains[2])

    turned_all = [mark for marks in h_ready.values() for mark in marks]
    act.wait(*turned_all)
    dve.wait(*turned_all)
    for t in range(TT):
        x_scaled = dve.mark(v.tensor_scalar(x[:, t, :], x[:, t, :], last_scale[:, t:t + 1], None, ALU.mult))
    dve.mark(v.memset(keys[:, :, :], 0.0))
    cleared = dve.mark(v.memset(index_k[:, :, :], 0.0))

    made = {}

    def gather(name, tensor, width, token_major, between, func=ACT.Copy):
        summed = project(core, stream, KT, width, (h_high, h_low), h_ready, token_major, range(4), between)
        made[name] = []
        for t in range(4):
            core.bank_read[t] = copy_out(core, act, tensor[:, t, 0:width], core.bank[t][:, 0:width], [summed[t]], func=func)
            made[name].append(core.bank_read[t])

    turns = [0]

    def turn_out(source, evacuate, ready):
        b = 4 + turns[0] % 4
        turns[0] += 1
        pe.wait(core.bank_read[b], *ready)
        for t in range(TT):
            step = pe.engine.transpose(core.bank[b][:, t * P:t * P + P], source(t), ident)
        core.bank_read[b] = evacuate(core.bank[b], pe.mark(step))
        return core.bank_read[b]

    def spread(out, parts):
        size = P // parts

        def evacuate(bank, turned):
            act.wait(turned, cleared)
            for j in range(parts):
                part = slice(size * j, size * j + size)
                step = act.mark(act.engine.activation(out[part, j, :], bank[part, :], ACT.Copy))
            return step
        return evacuate

    keys_ready, index_ready, q_turned_ready = [], [], []
    weight = kiw[:, :, IDX_DIM:IDX_DIM + IDX_HEADS]

    def keys_and_index():
        yield from norm_heads(core, kvi[:, :, 0:128], KV_HEADS, head_gain[:, 1, :], square, small, made["kvi"])
        rotated = rotate(core, kvi[:, :, 0:128], KV_HEADS, HEAD_DIM, 8, cosine, sine, 0, rotary_work)
        act.wait(rotated)
        for g in range(KV_HEADS):
            for again in range(2):
                twice = act.mark(act.engine.activation(keys_twice[:, :, 2 * g + again, :], kvi[:, :, g * 64:g * 64 + 64], ACT.Copy))
        yield
        for g in range(KV_HEADS):
            keys_ready.append(turn_out(lambda t: keys_twice[:, t, 2 * g:2 * g + 2, :].rearrange("p a d -> p (a d)"),
                                       spread(keys[:, 2 * g:2 * g + 2, :], 2), [twice]))
            yield
        rotated = rotate(core, kvi[:, :, 256:512], IDX_HEADS, IDX_DIM, 4, cosine, sine, 8, rotary_work)
        yield
        for c in range(2):
            index_ready.append(turn_out(lambda t: kvi[:, t, 256 + c * P:256 + c * P + P],
                                        lambda bank, turned: copy_out(core, act, index_q[:, c, :], bank[:, :], [turned]),
                                        [rotated]))
            yield
        dve.wait(*made["kiw"])
        rotated = rotate(core, kiw[:, :, 0:IDX_DIM], 1, IDX_DIM, 4, cosine, sine, 8, rotary_work)
        index_ready.append(dve.mark(v.tensor_scalar(weight, weight, IDX_DIM ** -0.5 * IDX_HEADS ** -0.5, None, ALU.mult)))
        act.wait(rotated)
        for again in range(4):
            four = act.mark(act.engine.activation(index_k_four[:, :, again, :], kiw[:, :, 0:IDX_DIM], ACT.Copy))
        yield
        index_ready.append(turn_out(lambda t: index_k_four[:, t, :, :].rearrange("p a d -> p (a d)"),
                                    spread(index_k, 4), [four]))

    gather("kvi", kvi, BANK, True, None)
    background = keys_and_index()
    gather("kiw", kiw, IDX_DIM + IDX_HEADS, True, None)
    gather("q", q, BANK, True, lambda: next(background, None))
    for _ in background:
        pass

    over_index = Region(nc, index_at)
    weights = [over_index.tensor(f"weights{i}", [P, T], F32) for i in range(2)]
    turned_weights = [over_index.tensor(f"turned{i}", [P, T], F32) for i in range(2)]
    attended = q
    highest = small[:, 3, 0:32]
    items = [(t, h) for t in range(TT) for h in range(A_HEADS)]
    powered, turned_of, applied, bias_ready = {}, {}, {}, {}
    attended_ready, index_used = [], [None, None]
    total = keep.head_scale[:, 0:len(items)]

    def score(i):
        t, h = items[i]
        n = (t + 1) * P
        b = 4
        pe.wait(core.bank_read[b], *keys_ready, *q_turned_ready)
        scored = pe.mark(pe.engine.matmul(core.bank[b][:, 0:n], q_turned[:, h // 2, t * P:t * P + P],
                                          keys[:, 2 * (h // 4) + h % 2, 0:n], start=True, stop=True))
        s = weights[i % 2][:, 0:n]
        dve.wait(scored, turned_of.get(i - 2), bias_ready[t])
        core.bank_read[b] = dve.mark(v.tensor_tensor_reduce(
            out=s, in0=core.bank[b][:, 0:n], in1=bias[:, t, 0:n], scale=1.0, scalar=-3e38, op0=ALU.add, op1=ALU.max,
            accum_out=highest[:, i:i + 1]))
        dve.wait(core.bank_read[b])
        negated = dve.mark(v.tensor_scalar(highest[:, i:i + 1], highest[:, i:i + 1], -1.0, None, ALU.mult))
        act.wait(negated)
        powered[i] = act.mark(act.engine.activation(s, s, ACT.Exp, bias=highest[:, i:i + 1], accum_out=total[:, i:i + 1]))

    def apply(i):
        t, h = items[i]
        n = (t + 1) * P
        b = 6
        pe.wait(powered[i], core.bank_read[b])
        for j in range(t + 1):
            step = pe.engine.transpose(core.bank[b][:, j * P:j * P + P], weights[i % 2][:, j * P:j * P + P], ident)
        turned_of[i] = pe.mark(step)
        core.bank_read[b] = copied = copy_out(core, act, turned_weights[i % 2][:, 0:n], core.bank[b][:, 0:n],
                                              [turned_of[i], applied.get(i - 2)])
        return copied

    def multiply(i, copied):
        t, h = items[i]
        out = 7
        pe.wait(copied)
        if h == 0:
            pe.wait(core.bank_read[out])
        group = h // (A_HEADS // KV_HEADS)
        for j in range(t + 1):
            step = pe.engine.matmul(core.bank[out][:, h * HEAD_DIM:(h + 1) * HEAD_DIM], turned_weights[i % 2][:, j * P:j * P + P],
                                    kvi[:, j, P + group * HEAD_DIM:P + (group + 1) * HEAD_DIM], start=(j == 0), stop=(j == t))
        applied[i] = pe.mark(step)
        if h == A_HEADS - 1:
            part = attended[:, t, :].rearrange("p (h d) -> p h d", h=A_HEADS)
            dve.wait(powered[i])
            inverse = dve.mark(v.reciprocal(total[:, t * 8:t * 8 + 8], total[:, t * 8:t * 8 + 8]))
            dve.wait(inverse, applied[i], *made["z_a"])
            core.bank_read[out] = dve.mark(v.tensor_tensor(
                part, core.bank[out][:, :].rearrange("p (h d) -> p h d", h=A_HEADS),
                total[:, t * 8:t * 8 + 8].unsqueeze(2).broadcast_to([P, A_HEADS, HEAD_DIM]), ALU.mult))
            dve.wait(core.bank_read[out])
            attended_ready.append(dve.mark(v.tensor_tensor(attended[:, t, :], attended[:, t, :], z_a[:, t, :], ALU.mult)))

    def attention():
        yield from norm_heads(core, q[:, :, :], A_HEADS, head_gain[:, 0, :], square, small, made["q"] + [gains_ready])
        rotated = rotate(core, q[:, :, :], A_HEADS, HEAD_DIM, 8, cosine, sine, 0, rotary_work)
        yield
        for c in range(4):
            q_turned_ready.append(turn_out(lambda t: q[:, t, c * P:c * P + P],
                                           lambda bank, turned: copy_out(core, act, q_turned[:, c, :], bank[:, :], [turned]),
                                           [rotated]))
            yield
        assert K_SEL >= P
        bias_ready[0] = dve.mark(v.tensor_copy(bias[:, 0, 0:P], allowed[:, T - P:T]))
        for t in range(1, TT):
            yield from select_keys(core, t, allowed, index_q, index_k, weight, bias, totals, relus, index_used, top, (4, 5),
                                   index_ready, bias_ready)
        dve.wait(pe.latest())
        act.wait(pe.latest())
        copied = {}
        for i in range(len(items) + 2):
            if i < len(items):
                score(i)
                yield
            if 0 <= i - 1 < len(items):
                copied[i - 1] = apply(i - 1)
                yield
            if 0 <= i - 2 < len(items):
                multiply(i - 2, copied[i - 2])

    pooled_ready = []

    def pooling():
        for buffer in summing:
            dve.mark(v.memset(buffer[:, 0:16], 0.0))
        for g, window in enumerate(POOL_WINDOWS):
            now, other = summing
            act.wait(dve.latest())
            copied = act.mark(act.engine.activation(now[:, 16:16 + T], pooled[:, g, :], ACT.Copy))
            dve.wait(copied, dve.latest())
            yield
            step = 1
            while step < window:
                dve.wait(dve.mark(v.tensor_tensor(other[:, 16:16 + T], now[:, 16:16 + T], now[:, 16 - step:16 + T - step], ALU.add)))
                now, other = other, now
                step *= 2
            yield
            dve.wait(dve.mark(v.tensor_tensor(now[:, 16:16 + 16], now[:, 16:16 + 16], pool_start[:, 16 * g:16 * g + 16], ALU.mult)))
            dve.mark(v.tensor_tensor(pooled[:, g, 0:16], now[:, 16:16 + 16], pooled[:, g, 0:16], ALU.subtract))
            pooled_ready.append(dve.mark(v.scalar_tensor_tensor(
                out=pooled[:, g, 16:T], in0=now[:, 32:16 + T], scalar=1.0 / window, in1=pooled[:, g, 16:T],
                op0=ALU.mult, op1=ALU.subtract)))
            yield

    attending, pools = attention(), pooling()

    def between(count):
        def pieces():
            for _ in range(count):
                next(attending, None)
        return pieces

    gather("z_a", z_a, BANK, True, between(1), ACT.Silu)
    gather("u_b", pooled, BANK, False, between(1))
    gather("z_b", mixed, BANK, False, lambda: (next(pools, None), next(attending, None)), ACT.Silu)
    for _ in pools:
        pass
    for g in range(4):
        pe.wait(core.bank_read[g], pooled_ready[g])
        multiplied = pe.mark(pe.engine.matmul(core.bank[g][:, :], pool_weights[:, g, :], pooled[:, g, :], start=True, stop=True))
        dve.wait(multiplied, *made["z_b"])
        core.bank_read[g] = mixed_ready = dve.mark(v.scalar_tensor_tensor(
            out=mixed[:, g, :], in0=core.bank[g][:, :], scalar=pool_scale[:, g:g + 1], in1=mixed[:, g, :],
            op0=ALU.mult, op1=ALU.mult))

    late = Region(nc, keep.scores_at)
    a_high = late.tensor("a_high", [P, 4, T], F32R)
    a_low = late.tensor("a_low", [P, 4, T], F32R)
    b_high = late.tensor("b_high", [P, 4, T], F32R)
    b_low = late.tensor("b_low", [P, 4, T], F32R)
    y_low = late.tensor("y_low", [P, KT, T], F32R)
    assert late.at == keep.values_at
    y_high = Region(nc, keep.rows_at).tensor("y_high", [P, KT, T], F32R)
    y_ready, combined_read = {}, None
    for half in range(2):
        for branch in range(2):
            banks = range(4)
            summed = project(core, stream, KT, BANK, (h_high, h_low), h_ready, False, banks, between(2))
            for i, b in enumerate(banks):
                act.wait(summed[i], combined_read)
                column = branch * KT + half * 4 + i
                core.bank_read[b] = gate_ready = act.mark(act.engine.activation(
                    gate[branch][:, i, :], core.bank[b][:, :], ACT.Sigmoid, bias=merge_bias[:, column:column + 1]))
        if half == 0:
            for _ in attending:
                pass
            act.wait(pe.latest())
            dve.wait(pe.latest(), mixed_ready)
            b_ready = {}
            for k in range(4):
                b_ready[k] = split_pair(core, mixed[:, k, :], b_high[:, k, :], b_low[:, k, :], [mixed_ready])

        def branch_out(branch, pair, ready, banks):
            summed = project(core, stream, 4, BANK, pair, ready, False, banks)
            for i, b in enumerate(banks):
                dve.wait(summed[i], gate_ready)
                core.bank_read[b] = dve.mark(v.tensor_tensor(gate[branch][:, i, :], core.bank[b][:, :], gate[branch][:, i, :], ALU.mult))

        branch_out(1, (b_high, b_low), b_ready, range(4))
        if half == 0:
            a_ready = turn_to_pair(core, attended, a_high, a_low, range(4), ident, attended_ready, range(4, 8))
            read = [mark for marks in (*a_ready.values(), *b_ready.values()) for mark in marks]
            act.wait(*read)
            dve.wait(*read)
        branch_out(0, (a_high, a_low), a_ready, range(4, 8))
        for i in range(4):
            dve.wait(core.bank_read[4 + i])
            added = dve.mark(v.tensor_tensor(gate[0][:, i, :], gate[0][:, i, :], gate[1][:, i, :], ALU.add))
            k = half * 4 + i
            y_ready[k] = split_pair(core, gate[0][:, i, :], y_high[:, k, :], y_low[:, k, :], [added])
        combined_read = y_ready[k][1]
    stored = Signal(nc, "out_stored")
    for half in range(2):
        banks = [4 * half + i for i in range(4)]
        summed = project(core, stream, KT, BANK, (y_high, y_low), y_ready, True, banks)
        for t, b in enumerate(banks):
            part = x[:, t, half * BANK:(half + 1) * BANK]
            dve.wait(summed[t])
            core.bank_read[b] = written = dve.mark(v.tensor_tensor(part, part, core.bank[b][:, :], ALU.add))
            sp.wait(written)
            done = stored.after(sp.engine.dma_start(dram["out"].rearrange("(t p) d -> t p d", p=P)[t][:, half * BANK:(half + 1) * BANK], part), 16)
    sp.wait(done)


OUTPUT = "out"


def program(nc, dram):
    dram["gates"] = nc.dram_tensor("gates_scratch", [T // GATE_CHUNK, P, N_KEYS, GATE_CHUNK], F32).ap()
    dram["hidden"] = nc.dram_tensor("hidden_scratch", [N_KEYS, P, T], F32).ap()
    core = Core(nc)
    keep = Kept(core, dram)
    block_one_mixing(core, dram, keep)
    block_two(core, dram, keep, peer(core, dram, keep))


def kernel(**inputs):
    import numpy as _np
    import concourse.bacc as _bacc
    from concourse import mybir as _mybir
    from concourse.bass_utils import run_bass_kernel_spmd as _run

    a = {name: _np.asarray(value) for name, value in inputs.items()}

    def columns(vector):
        return vector.reshape(-1, P).T

    laid = {
        "x": a["x"][0],
        "norm_mix_g": columns(a["norm_mix_g"][0]),
        "norm_ffn_g": columns(a["norm_ffn_g"][0]),
        "norm_g_2": columns(a["norm_g_2"][0]),
        "final_norm_g": a["final_norm_g"],
        "w_in": a["w_in"][0],
        "w_out": a["w_out"][0],
        "diff_lambda": a["diff_lambda"][0],
        "diff_subln_g": a["diff_subln_g"][0],
        "peer_wq": a["peer_wq"][0],
        "subkeys": a["peer_subkeys"][0].reshape(HP, N_KEYS, P).transpose(2, 0, 1),
        "peer_u": a["peer_u"][0].reshape(N_KEYS, N_KEYS, KT, P).transpose(1, 3, 2, 0),
        "peer_v": a["peer_v"][0].reshape(N_KEYS, N_KEYS, D),
        "positions": a["positions_2"].reshape(TT, P).T,
        "w_in_2": a["w_in_2"][0],
        "merge_bias": columns(a["merge_bias_2"][0].reshape(-1)),
        "q_norm_g": a["q_norm_g_2"][0],
        "k_norm_g": a["k_norm_g_2"][0],
        "pool_w": a["pool_w_2"][0].transpose(1, 0, 2),
        "pool_scale": columns(a["pool_scale_2"][0]),
        "w_branch_a": a["w_branch_a_2"][0],
        "w_branch_b": a["w_branch_b_2"][0],
        "w_out_2": a["w_out_2"][0],
    }
    laid.update(constants())
    nc = _bacc.Bacc("TRN2", target_bir_lowering=False, num_devices=1)
    arrays, dram = {}, {}
    for name, array in laid.items():
        array = _np.ascontiguousarray(array)
        arrays[f"in_{name}"] = array
        dram[name] = nc.dram_tensor(f"in_{name}", array.shape, _mybir.dt.from_np(array.dtype), kind="ExternalInput").ap()
    dram[OUTPUT] = nc.dram_tensor("result", (T, D), F32, kind="ExternalOutput").ap()
    program(nc, dram)
    result = _run(nc, [arrays], core_ids=[0]).results[0]["result"]
    return result.reshape(1, T, D)
```

```python
from concourse import mybir
import concourse.bass as bass
import numpy as np

F32 = mybir.dt.float32
F32R = mybir.dt.float32r
F16 = mybir.dt.float16
I32 = mybir.dt.int32
U32 = mybir.dt.uint32
ALU = mybir.AluOpType
ACT = mybir.ActivationFunctionType
AX_X = mybir.AxisListType.X

P = 128
T = 512
D = 1024
TT = T // P
KT = D // P
BANK = 512
RMS_EPS = 1e-6
NEG = -1e30

RET_HEADS, RET_D = 4, 128
DIFF_HEADS, DIFF_DQK, DIFF_DV = 4, 64, 128
LAMBDA_INIT = 0.8 - 0.6 * float(np.exp(-0.3 * 0))

PEER_HEADS, PEER_TOPK, N_KEYS = 8, 16, 128
HK = PEER_HEADS * PEER_TOPK
HP = PEER_HEADS * 2

A_HEADS, KV_HEADS, HEAD_DIM = 8, 2, 64
IDX_HEADS, IDX_DIM = 8, 32
K_SEL = min(256, T // 4)
ROPE_THETA = 500000.0
POOL_WINDOWS = (2, 4, 8, 16)


class Signal:

    def __init__(self, nc, name):
        self.semaphore = nc.alloc_semaphore(name)
        self.value = 0

    def after(self, instruction, amount=1):
        instruction.then_inc(self.semaphore, amount)
        self.value += amount
        return (self, self.value)


class Lane:

    def __init__(self, nc, engine, name):
        self.engine = engine
        self.finished = Signal(nc, name + "_finished")
        self.seen = {}

    def wait(self, *marks):
        for mark in marks:
            if mark is None:
                continue
            signal, value = mark
            if self.seen.get(signal, 0) < value:
                self.engine.wait_ge(signal.semaphore, value)
                self.seen[signal] = value

    def mark(self, instruction):
        return self.finished.after(instruction)

    def latest(self):
        return (self.finished, self.finished.value) if self.finished.value else None


class Region:

    def __init__(self, nc, start):
        self.nc, self.at = nc, start

    def tensor(self, name, shape, dtype):
        size = int(np.prod(shape[1:])) * mybir.dt.size(dtype)
        made = self.nc.alloc_sbuf_tensor_at(name, list(shape), dtype, offset=self.at)
        self.at += (size + 63) // 64 * 64
        return made


class Core:

    def __init__(self, nc):
        self.nc = nc
        self.pe = Lane(nc, nc.tensor, "tensor")
        self.act = Lane(nc, nc.scalar, "scalar")
        self.dve = Lane(nc, nc.vector, "vector")
        self.pool = Lane(nc, nc.gpsimd, "gpsimd")
        self.sp = Lane(nc, nc.sync, "sync")
        self.bank = [nc.alloc_psum_tensor(f"bank{i}", [P, BANK], F32) for i in range(8)]
        self.bank_read = [None] * 8
        self.stored = []

    def load(self, name, out, in_, queue=None):
        lane = queue or self.sp
        return Signal(self.nc, name).after(lane.engine.dma_start(out, in_), 16)

    def meet(self):
        lanes = (self.pe, self.act, self.dve, self.pool)
        marks = [lane.latest() for lane in lanes]
        for lane in lanes:
            lane.wait(*marks)
        return [m for m in marks if m]


def split_pair(core, source, high, low, ready, scale=None):
    act, dve = core.act, core.dve
    act.wait(*ready)
    if scale is None:
        high_ready = act.mark(act.engine.activation(high, source, ACT.Copy))
    else:
        high_ready = act.mark(act.engine.activation(high, source, ACT.Copy, scale=scale))
    dve.wait(*ready)
    dve.wait(high_ready)
    if scale is None:
        low_ready = dve.mark(dve.engine.tensor_tensor(low, source, high.bitcast(F32), ALU.subtract))
    else:
        low_ready = dve.mark(dve.engine.scalar_tensor_tensor(
            out=low, in0=source, scalar=scale, in1=high.bitcast(F32), op0=ALU.mult, op1=ALU.subtract))
    return [high_ready, low_ready]


def three_products(engine, out, left, right, first, last):
    (lh, ll), (rh, rl) = left, right
    engine.matmul(out, lh, rh, start=first, stop=False)
    engine.matmul(out, lh, rl, start=False, stop=False)
    return engine.matmul(out, ll, rh, start=False, stop=last)


class WeightStream:

    ROWS, RAW, PAIRS = 2, 3, 3
    BYTES = ROWS * BANK * 4 * (RAW + 2 * PAIRS)

    def __init__(self, core, region):
        self.core = core
        shape = [P, self.ROWS * BANK]
        self.raw = [region.tensor(f"weights_raw{i}", shape, F32) for i in range(self.RAW)]
        self.high = [region.tensor(f"weights_high{i}", shape, F32R) for i in range(self.PAIRS)]
        self.low = [region.tensor(f"weights_low{i}", shape, F32R) for i in range(self.PAIRS)]
        self.arrived = [Signal(core.nc, f"weights_arrived{i}") for i in range(self.RAW)]
        self.raw_split = [[] for _ in range(self.RAW)]
        self.pair_used = [None] * self.PAIRS
        self.queue = []
        self.loaded = 0
        self.split = 0
        self.open = 0
        self.landed = {}
        self.ready = {}
        self.next_group = 0

    def add(self, weights, columns, first_row=0):
        view = weights.rearrange("(k p) c -> p k c", p=P)[:, :, columns[0]:columns[1]]
        rows, width = view.shape[1], columns[1] - columns[0]
        in_chunk = min(rows, self.ROWS * BANK // width)
        for k in range(0, rows, in_chunk):
            k = (k + first_row) % rows
            self.queue.append((view[:, k:k + in_chunk, :], in_chunk, width))

    def part(self, buffer, n):
        _, rows, width = self.queue[n]
        return buffer[:, 0:rows * width].rearrange("p (k c) -> p k c", k=rows)

    def release(self, *free):
        self.core.sp.wait(*free)
        self.core.act.wait(*free)
        self.core.dve.wait(*free)
        self.open = len(self.queue)
        for _ in range(self.RAW - 1):
            self.load_next()

    def load_next(self):
        n = self.loaded
        if n >= self.open:
            return
        slot = n % self.RAW
        sp = self.core.sp
        sp.wait(*self.raw_split[slot])
        out = self.part(self.raw[slot], n)
        self.landed[n] = self.arrived[slot].after(sp.engine.dma_start(out, self.queue[n][0]), 16)
        self.loaded += 1

    def split_next(self):
        if self.split >= self.open:
            return
        n = self.split
        slot, raw = n % self.PAIRS, n % self.RAW
        self.load_next()
        ready = [self.landed[n], self.pair_used[slot]]
        self.ready[n] = split_pair(self.core, self.part(self.raw[raw], n),
                                   self.part(self.high[slot], n), self.part(self.low[slot], n), ready)
        self.raw_split[raw] = self.ready[n]
        self.split += 1

    def pair(self, n):
        return self.part(self.high[n % self.PAIRS], n), self.part(self.low[n % self.PAIRS], n)


def project(core, stream, tiles, width, data, data_ready, token_major, banks, between=None, first_row=0):
    pe = core.pe
    high, low = data
    marks = []
    chunk = stream.next_group
    rows = stream.queue[chunk][1]
    n_chunks = tiles // rows
    stream.next_group += n_chunks
    for c in range(chunk, chunk + n_chunks):
        while stream.split < min(c + 3, stream.open):
            stream.split_next()
        weight_high, weight_low = stream.pair(c)
        pe.wait(*stream.ready[c])
        for tile, b in enumerate(banks):
            if c == chunk:
                pe.wait(core.bank_read[b])
            for r in range(rows):
                step = (c - chunk) * rows + r
                k = (step + first_row) % tiles
                if tile == 0:
                    pe.wait(*data_ready[k])
                part = slice(tile * P, tile * P + P if token_major else min(tile * P + P, width))
                first, last = step == 0, step == tiles - 1
                if token_major:
                    left = (high[:, k, part], low[:, k, part])
                    right = (weight_high[:, r, 0:width], weight_low[:, r, 0:width])
                    out = core.bank[b][:, 0:width]
                else:
                    left = (weight_high[:, r, part], weight_low[:, r, part])
                    right = (high[:, k, :], low[:, k, :])
                    out = core.bank[b][0:part.stop - part.start, :]
                done = three_products(pe.engine, out, left, right, first, last)
            mark = pe.mark(done)
            if between is not None:
                between()
            if c == chunk + n_chunks - 1:
                marks.append(mark)
        stream.pair_used[c % stream.PAIRS] = mark
    return marks


def copy_out(core, lane, out, source, ready, **kw):
    lane.wait(*ready)
    if lane is core.act:
        return lane.mark(lane.engine.activation(out, source, kw.get("func", ACT.Copy), scale=kw.get("scale", 1.0)))
    if "scale" in kw:
        return lane.mark(lane.engine.tensor_scalar(out, source, kw["scale"], None, ALU.mult))
    return lane.mark(lane.engine.tensor_copy(out, source))


def rms_scale(core, sums, scratch, out, n, ready):
    dve, act = core.dve, core.act
    dve.wait(*ready)
    mean = dve.mark(dve.engine.tensor_scalar(scratch, sums, 1.0 / n, RMS_EPS, ALU.mult, ALU.add))
    act.wait(mean)
    root = act.mark(act.engine.activation(scratch, scratch, ACT.Sqrt))
    dve.wait(root)
    return dve.mark(dve.engine.reciprocal(out, scratch))


def half_of(half):
    return slice(half * BANK, (half + 1) * BANK)


def square_half(core, lane, source, junk, total, ready):
    lane.wait(*ready, lane.latest())
    if lane is core.act:
        return lane.mark(lane.engine.activation(junk, source, ACT.Square, accum_out=total))
    return lane.mark(lane.engine.tensor_tensor_reduce(
        out=junk, in0=source, in1=source, scale=1.0, scalar=0.0, op0=ALU.mult, op1=ALU.add, accum_out=total))


def pair_scale(core, halves, total, scratch, out, ready):
    dve = core.dve
    dve.wait(*ready)
    sums = halves.rearrange("p (t h) -> p t h", h=2)
    summed = dve.mark(dve.engine.tensor_tensor(total, sums[:, :, 0], sums[:, :, 1], ALU.add))
    return rms_scale(core, total, scratch, out, D, [summed])


def scale_rows(core, out, source, scale, ready):
    act, dve = core.act, core.dve
    act.wait(*ready)
    dve.wait(*ready)
    return [act.mark(act.engine.activation(out[:, half_of(0)], source[:, half_of(0)], ACT.Copy, scale=scale)),
            dve.mark(dve.engine.tensor_scalar(out[:, half_of(1)], source[:, half_of(1)], scale, None, ALU.mult))]


def small_columns(small):
    return small[:, 0:2 * TT], small[:, 2 * TT:3 * TT], small[:, 3 * TT:4 * TT], small[:, 4 * TT:5 * TT]


def normalise_and_turn(core, x, gain, high, low, small, normed, ident, squared, banks, before_turns=None):
    halves, total, scratch, scale = small_columns(small)
    rows = []
    for pair in range(0, TT, 2):
        two = slice(pair, pair + 2)
        scaled = pair_scale(core, halves[:, 2 * pair:2 * pair + 4], total[:, two], scratch[:, two], scale[:, two],
                            squared(pair) + squared(pair + 1))
        for t in (pair, pair + 1):
            rows.append(scale_rows(core, normed[:, t, :], x[:, t, :], scale[:, t:t + 1], [scaled]))
    if before_turns is not None:
        before_turns()
    return turn_to_pair(core, normed, high, low, range(KT), ident, rows, banks, gain)


def turn_to_pair(core, source, high, low, tiles, ident, rows, banks, gain=None):
    pe = core.pe
    ready = {}
    for n, k in enumerate(tiles):
        b = banks[n % len(banks)]
        pe.wait(core.bank_read[b])
        for t in range(TT):
            pe.wait(*rows[t])
            turned = pe.engine.transpose(core.bank[b][:, t * P:t * P + P], source[:, t, k * P:k * P + P], ident)
        turned = pe.mark(turned)
        ready[k] = split_pair(core, core.bank[b][:, :], high[:, k, :], low[:, k, :], [turned],
                              scale=None if gain is None else gain[:, k:k + 1])
        core.bank_read[b] = ready[k][1]
    return ready


def constants():
    i = np.arange(P, dtype=np.float64)
    later = np.arange(T, dtype=np.float64)[None, :] - i[:, None]
    gamma = 1.0 - 2.0 ** (-5.0 - np.arange(RET_HEADS))
    decay = np.where(later[:, None, :] >= 0, gamma[None, :, None] ** np.maximum(later, 0)[:, None, :], 0.0)
    decay = decay * RET_D ** -0.5
    key = np.arange(T, dtype=np.float64)[None, :] - (T - P)
    distance = i[:, None] - key
    alibi = np.where(distance >= 0, -distance, NEG)
    chunk_end = (np.floor(i / 64) + 1)[:, None] * 64
    allowed = np.where(key < chunk_end, 0.0, NEG)
    pool_start = np.stack([1.0 / np.minimum(np.arange(16) + 1, w) for w in POOL_WINDOWS])
    freq_a = ROPE_THETA ** (-np.arange(8) / 8)
    freq_i = ROPE_THETA ** (-np.arange(4) / 4)
    return {
        "identity": np.eye(P, dtype=np.float32),
        "decay": decay.astype(np.float32).reshape(P, RET_HEADS * T),
        "alibi": alibi.astype(np.float32),
        "allowed": allowed.astype(np.float32),
        "pool_start": np.broadcast_to(pool_start.astype(np.float32).reshape(1, -1), (P, 64)).copy(),
        "frequencies": np.broadcast_to(np.concatenate([freq_a, freq_i]).astype(np.float32), (P, 12)).copy(),
        "counting": np.broadcast_to(np.arange(P, dtype=np.float32), (P, P)).copy(),
    }


def row_of(vector, n):
    return vector.rearrange("(a n) -> a n", a=1).broadcast_to([P, n])


def block_one_mixing(core, dram, keep):
    nc, pe, act, dve, stream = core.nc, core.pe, core.act, core.dve, keep.stream
    ident = keep.ident[:, :]
    x = keep.x
    region = Region(nc, keep.end)
    h_high = region.tensor("h_high", [P, KT, T], F32R)
    h_low = region.tensor("h_low", [P, KT, T], F32R)
    outs_at = region.at
    feature = {n: region.tensor(n, [P, 4, T], F32) for n in ("ret_q", "ret_k", "diff_q")}
    token = {n: region.tensor(n, [P, TT, T], F32) for n in ("ret_v", "ret_gate")}
    early_end = region.at
    feature.update({n: region.tensor(n, [P, 4, T], F32) for n in ("diff_k0", "diff_k1")})
    token["diff_v"] = region.tensor("diff_v", [P, TT, T], F32)
    mix = region.tensor("mix", [P, TT, D], F32)
    ret_weights_at = region.at
    ret_weights = region.tensor("ret_weights", [P, 4, T], F32)
    scores = [region.tensor(f"diff_scores{i}", [P, 2, T], F32) for i in range(2)]
    scores.append(Region(nc, ret_weights_at).tensor("diff_scores2", [P, 2, T], F32))
    turned_weights = [region.tensor(f"diff_turned{i}", [P, T], F32) for i in range(2)]
    junk = region.tensor("junk_head", [P, P], F32)
    lambda_rows = region.tensor("lambda_rows", [P, 4, DIFF_DQK], F32)
    lambda_sums = region.tensor("lambda_sums", [P, 4], F32)
    subln = region.tensor("subln", [P, DIFF_DV], F32)
    small = region.tensor("mix_small", [P, 64], F32)
    assert region.at <= keep.stream_at
    early = Region(nc, outs_at)
    normed = early.tensor("normed_x", [P, TT, D], F32)
    junks = [early.tensor(f"junk_x{i}", [P, BANK], F32) for i in range(2)]
    assert early.at <= early_end

    rows_ready = core.load("lambda_rows_in", lambda_rows[:, :, :],
                           dram["diff_lambda"].rearrange("(a q) d -> a q d", a=1).broadcast_to([P, 4, DIFF_DQK]), act)
    subln_ready = core.load("subln_in", subln[:, :], row_of(dram["diff_subln_g"], DIFF_DV), act)
    order = [("diff_q", 4), ("diff_k", 5), ("diff_v", 6), ("ret_q", 0), ("ret_k", 1), ("ret_v", 2), ("ret_gate", 3)]
    for _, g in order:
        stream.add(dram["w_in"], (g * 512, g * 512 + 512))
    for half in range(2):
        stream.add(dram["w_out"], (half * 512, half * 512 + 512), first_row=4)
    for g in range(4):
        stream.add(dram["peer_wq"], (g * 512, g * 512 + 512))
    core.sp.wait(*keep.x_ready[0:TT - 1])
    stream.release()
    v = dve.engine
    dve.mark(v.memset(feature["diff_k0"][64:128, :, :], 0.0))
    dve.mark(v.memset(feature["diff_k1"][0:64, :, :], 0.0))
    halves = small_columns(small)[0]

    def squared(t):
        return [square_half(core, lane, x[:, t, half_of(half)], junks[half][:, :], halves[:, 2 * t + half:2 * t + half + 1],
                            [keep.x_ready[t]]) for half, lane in enumerate((act, dve))]

    h_ready = normalise_and_turn(core, x, keep.gains[0], h_high, h_low, small, normed, ident, squared, range(8),
                                 stream.split_next)
    tables_ready = [core.load("alibi_arrived", keep.alibi[:, :], dram["alibi"], act),
                    core.load("decay_arrived", keep.decay[:, :], dram["decay"], act)]

    result = {}

    def gather(name, banks, between=None):
        token_major = name in token
        summed = project(core, stream, KT, BANK, (h_high, h_low), h_ready, token_major, banks, between)
        marks = []
        for i, b in enumerate(banks):
            source = core.bank[b][:, :]
            if name == "diff_k":
                marks.append(copy_out(core, dve, feature["diff_k0"][0:64, i, :], source[0:64, :], [summed[i]]))
                marks.append(copy_out(core, act, feature["diff_k1"][64:128, i, :], source[64:128, :], [summed[i], marks[-1]]))
            elif name == "diff_q":
                marks.append(copy_out(core, act, feature[name][:, i, :], source, [summed[i]], scale=DIFF_DQK ** -0.5))
            elif name == "ret_gate":
                marks.append(copy_out(core, act, token[name][:, i, :], source, [summed[i]], func=ACT.Silu))
            else:
                out = token[name] if token_major else feature[name]
                marks.append(copy_out(core, act if i % 2 else dve, out[:, i, :], source, [summed[i]]))
            core.bank_read[b] = marks[-1]
        result[name] = marks

    turned_all = [mark for marks in h_ready.values() for mark in marks]
    act.wait(*turned_all)
    dve.wait(*turned_all)
    gather("diff_q", range(4))
    gather("diff_k", range(4, 8))
    gather("diff_v", range(4))

    dve.wait(rows_ready)
    for n in range(2):
        summed = dve.mark(v.tensor_tensor_reduce(
            out=lambda_rows[:, 2 * n, :], in0=lambda_rows[:, 2 * n, :], in1=lambda_rows[:, 2 * n + 1, :], scale=1.0,
            scalar=0.0, op0=ALU.mult, op1=ALU.add, accum_out=lambda_sums[:, n:n + 1]))
    act.wait(summed)
    powers = act.mark(act.engine.activation(lambda_sums[:, 2:4], lambda_sums[:, 0:2], ACT.Exp))
    lam = lambda_sums[:, 0:1]
    dve.wait(powers)
    dve.wait(dve.mark(v.tensor_tensor(lam, lambda_sums[:, 2:3], lambda_sums[:, 3:4], ALU.subtract)))
    lam_ready = dve.mark(v.tensor_scalar(lam, lam, LAMBDA_INIT, None, ALU.add))
    dve.wait(subln_ready)
    dve.mark(v.tensor_scalar(subln[:, :], subln[:, :], 1.0 - LAMBDA_INIT, None, ALU.mult))


    items = [(h, t) for h in range(DIFF_HEADS) for t in range(TT)]
    averaged, softmaxed, head_out, diff_mixed = {}, {}, {}, []

    def score(i):
        h, t = items[i]
        n = (t + 1) * P
        s = scores[i % 3]
        for half, key in enumerate(("diff_k0", "diff_k1")):
            b = 4 + half
            pe.wait(core.bank_read[b], *result["diff_q"], *result["diff_k"])
            scored = pe.mark(pe.engine.matmul(core.bank[b][:, 0:n], feature["diff_q"][:, h, t * P:t * P + P],
                                              feature[key][:, h, 0:n], start=True, stop=True))
            dve.wait(scored, averaged.get(i - 3), tables_ready[0])
            core.bank_read[b] = dve.mark(v.scalar_tensor_tensor(
                out=s[:, half, 0:n], in0=keep.alibi[:, T - P - t * P:T], scalar=2.0 ** (-8.0 * (h + 1) / DIFF_HEADS),
                in1=core.bank[b][:, 0:n], op0=ALU.mult, op1=ALU.add))
        base = 32 + 8 * (i % 3)
        top, total, share = (small[:, base + 2 * m:base + 2 * m + 2] for m in range(3))
        dve.wait(core.bank_read[b])
        dve.wait(dve.mark(v.tensor_reduce(top, s[:, :, 0:n], AX_X, ALU.max)))
        negated = dve.mark(v.tensor_scalar(top, top, -1.0, None, ALU.mult))
        act.wait(negated)
        for half in range(2):
            powered = act.mark(act.engine.activation(s[:, half, 0:n], s[:, half, 0:n], ACT.Exp,
                                                     bias=top[:, half:half + 1], accum_out=total[:, half:half + 1]))
        return s, n, total, share, powered

    def subtract(i, s, n, total, share, powered):
        dve.wait(powered)
        dve.wait(dve.mark(v.reciprocal(share, total)), lam_ready)
        dve.wait(dve.mark(v.tensor_scalar(share[:, 1:2], share[:, 1:2], lam, None, ALU.mult)))
        dve.wait(dve.mark(v.tensor_scalar(s[:, 1, 0:n], s[:, 1, 0:n], share[:, 1:2], None, ALU.mult)))
        softmaxed[i] = dve.mark(v.scalar_tensor_tensor(
            out=s[:, 0, 0:n], in0=s[:, 0, 0:n], scalar=share[:, 0:1], in1=s[:, 1, 0:n], op0=ALU.mult, op1=ALU.subtract))

    def weigh(i):
        h, t = items[i]
        n = (t + 1) * P
        pe.wait(softmaxed[i], core.bank_read[6])
        for j in range(t + 1):
            turned = pe.engine.transpose(core.bank[6][:, j * P:j * P + P], scores[i % 3][:, 0, j * P:j * P + P], ident)
        averaged[i] = turned = pe.mark(turned)
        copied = copy_out(core, act, turned_weights[i % 2][:, 0:n], core.bank[6][:, 0:n], [turned, head_out.get(i - 2)])
        core.bank_read[6] = copied
        return copied

    def multiply(i, copied):
        h, t = items[i]
        pe.wait(copied, *result["diff_v"])
        if t == 0:
            pe.wait(core.bank_read[7])
        for j in range(t + 1):
            step = pe.engine.matmul(core.bank[7][:, t * P:t * P + P], turned_weights[i % 2][:, j * P:j * P + P],
                                    token["diff_v"][:, j, h * P:h * P + P], start=(j == 0), stop=(j == t))
        head_out[i] = pe.mark(step)
        if t == TT - 1:
            core.bank_read[7] = copy_out(core, act, mix[:, :, h * P:h * P + P],
                                         core.bank[7][:, :].rearrange("p (t v) -> p t v", t=TT), [head_out[i]])
            diff_mixed.append(core.bank_read[7])

    rows_mixed = [None] * TT

    def head_squares(first, h):
        sums = keep.head_scale[:, 4 * first:4 * first + 16]
        for t in range(TT):
            head = mix[:, t, (first + h) * P:(first + h) * P + P]
            act.wait(act.latest())
            summed = act.mark(act.engine.activation(junk[:, :], head, ACT.Square, accum_out=sums[:, 4 * t + h:4 * t + h + 1]))
        return summed

    def scale_heads(first, summed, factor):
        sums, scratch, scale = (keep.head_scale[:, 32 * m + 4 * first:32 * m + 4 * first + 16] for m in range(3))
        dve.wait(rms_scale(core, sums, scratch, scale, P, [summed]))
        for t in range(TT):
            for h in range(4):
                head = mix[:, t, (first + h) * P:(first + h) * P + P]
                rows_mixed[t] = dve.mark(v.scalar_tensor_tensor(
                    out=head, in0=head, scalar=scale[:, 4 * t + h:4 * t + h + 1], in1=factor(h, t), op0=ALU.mult, op1=ALU.mult))
            yield

    def attention():
        waiting, copied = {}, {}
        for i in range(len(items) + 3):
            if i < len(items):
                waiting[i] = score(i)
                yield
            if 0 <= i - 3 < len(items):
                multiply(i - 3, copied[i - 3])
            if 0 <= i - 2 < len(items):
                copied[i - 2] = weigh(i - 2)
                yield
            if 0 <= i - 1 < len(items):
                subtract(i - 1, *waiting[i - 1])
                yield
        for h in range(DIFF_HEADS):
            summed = head_squares(0, h)
            yield
        yield from scale_heads(0, summed, lambda h, t: subln[:, :])

    attending = attention()

    for name in ("ret_q", "ret_k", "ret_v"):
        gather(name, range(4), lambda: next(attending, None))

    ret_used, ret_mixed = [None], []

    def retention():
        dve.wait(pe.latest())
        for h in range(RET_HEADS):
            for j in range(TT):
                n = (TT - j) * P
                b = 4 + j % 2
                pe.wait(core.bank_read[b], *result["ret_q"], *result["ret_k"])
                scored = pe.mark(pe.engine.matmul(core.bank[b][:, 0:n], feature["ret_k"][:, h, j * P:j * P + P],
                                                  feature["ret_q"][:, h, j * P:T], start=True, stop=True))
                dve.wait(scored, ret_used[0], tables_ready[1])
                weighted = core.bank_read[b] = dve.mark(v.tensor_tensor(
                    ret_weights[:, j, 0:n], core.bank[b][:, 0:n], keep.decay[:, h * T:h * T + n], ALU.mult))
                yield
            b = 6 + h % 2
            pe.wait(core.bank_read[b], weighted, *result["ret_v"])
            for t in range(TT):
                for j in range(t + 1):
                    step = pe.engine.matmul(core.bank[b][:, t * P:t * P + P], ret_weights[:, j, (t - j) * P:(t - j) * P + P],
                                            token["ret_v"][:, j, h * P:h * P + P], start=(j == 0), stop=(j == t))
            ret_used[0] = pe.mark(step)
            core.bank_read[b] = copy_out(core, act, mix[:, :, BANK + h * P:BANK + h * P + P],
                                         core.bank[b][:, :].rearrange("p (t v) -> p t v", t=TT), [ret_used[0]])
            ret_mixed.append(core.bank_read[b])
            yield
            ret_summed.append(head_squares(4, h))

    def attention_then_retention():
        while not diff_mixed[DIFF_HEADS - 1:]:
            next(attending)
            yield
        retaining = retention()
        for _ in retaining:
            yield
            next(attending, None)
        for _ in attending:
            pass
        attention_rows.extend(rows_mixed)

    attention_rows, ret_summed = [], []
    background = attention_then_retention()
    gather("ret_gate", range(4), lambda: (next(background, None), next(background, None)))
    for _ in background:
        pass

    late = Region(nc, keep.end)
    mix_high = late.tensor("mix_high", [P, KT, T], F32R)
    mix_low = late.tensor("mix_low", [P, KT, T], F32R)
    act.wait(*[mark for mark in (pe.latest(),)])
    dve.wait(pe.latest())
    mix_ready = turn_to_pair(core, mix, mix_high, mix_low, range(4), ident, [[mark] for mark in attention_rows], range(4, 8))

    def retention_rows():
        dve.wait(*result["ret_gate"])
        yield from scale_heads(4, ret_summed[-1], lambda h, t: token["ret_gate"][:, t, h * P:h * P + P])
        for k in range(4, 8):
            mix_ready.update(turn_to_pair(core, mix, mix_high, mix_low, [k], ident, [[mark] for mark in rows_mixed], [k]))
            yield

    background = retention_rows()
    halves = small_columns(keep.norm_small)[0]
    keep.x_squared = [[None, None] for _ in range(TT)]
    for g in range(2):
        banks = [g * 4 + i for i in range(4)]
        summed = project(core, stream, KT, BANK, (mix_high, mix_low), mix_ready, True, banks, lambda: next(background, None))
        for t, b in enumerate(banks):
            dve.wait(summed[t])
            part = x[:, t, half_of(g)]
            core.bank_read[b] = added = dve.mark(v.tensor_tensor(part, part, core.bank[b][:, :], ALU.add))
            keep.x_squared[t][g] = square_half(core, act, part, ret_weights[:, 0, :], halves[:, 2 * t + g:2 * t + g + 1], [added])


class Kept:

    def __init__(self, core, dram):
        nc = core.nc
        region = Region(nc, (nc.sbuf_base + 63) // 64 * 64)
        self.x = region.tensor("x", [P, TT, D], F32)
        self.ident = region.tensor("ident", [P, P], F32)
        self.gains = [region.tensor(f"gain{i}", [P, KT], F32) for i in range(3)]
        self.head_scale = region.tensor("head_scale", [P, 96], F32)
        self.counting = region.tensor("counting_sb", [P, P], F32)
        self.norm_small = region.tensor("norm_small", [P, 64], F32)
        self.rows_at = region.at
        self.decay = region.tensor("decay_sb", [P, RET_HEADS * T], F32)
        self.alibi = region.tensor("alibi_sb", [P, T], F32)
        self.end = region.at
        self.stream_at = (nc.sbuf_usable_end - WeightStream.BYTES) // 64 * 64
        self.stream = WeightStream(core, Region(nc, self.stream_at))
        arrived = Signal(nc, "tables_arrived")
        act = core.act
        arrived.after(act.engine.dma_start(self.ident[:, :], dram["identity"]), 16)
        arrived.after(act.engine.dma_start(self.counting[:, :], dram["counting"]), 16)
        for tile, name in zip(self.gains, ("norm_mix_g", "norm_ffn_g", "norm_g_2")):
            arrived.after(act.engine.dma_start(tile[:, :], dram[name]), 16)
        tables = (arrived, arrived.value)
        self.x_ready = [core.load(f"x_arrived{t}", self.x[:, t, :], dram["x"].rearrange("(t p) d -> p t d", p=P)[:, t, :],
                                  act if t % 2 else None) for t in range(TT)]
        for lane in (core.pe, core.act, core.dve):
            lane.wait(tables)



EARLY_BANKS = (0, 1, 2, 3)
GATE_BANKS = (4, 5, 6, 7)
GATE_CHUNK = 64
HOT = 16
GATE_SCALE = 2.0 ** 15
BATCH = 4
U_RAW = 4
GROUP = 4


def peer_scores(core, dram, keep, xn_high, xn_low, region, scores, prologue):
    pe, act, dve, stream = core.pe, core.act, core.dve, keep.stream
    subkeys = region.tensor("subkeys", [P, HP, N_KEYS], F32)
    query = region.tensor("query", [P, HP, T], F32)
    normed = region.tensor("normed_ffn", [P, TT, D], F32)
    assert region.at <= keep.u_raw_at
    subkeys_ready = core.load("subkeys_arrived", subkeys[:, :, :], dram["subkeys"])
    xn_ready = normalise_and_turn(core, keep.x, keep.gains[1], xn_high, xn_low, keep.norm_small, normed, keep.ident[:, :],
                                  lambda t: keep.x_squared[t], range(8))
    query_ready = []
    for g in range(4):
        banks = [(g % 2) * 4 + i for i in range(4)]
        summed = project(core, stream, KT, BANK, (xn_high, xn_low), xn_ready, False, banks)
        for i, b in enumerate(banks):
            lane = act if i % 2 else dve
            core.bank_read[b] = copy_out(core, lane, query[:, 4 * g + i, :], core.bank[b][:, :], [summed[i]])
            query_ready.append(core.bank_read[b])
    next(prologue)
    marks = []
    for t in range(TT):
        for g in range(4):
            b = (4 * t + g) % 8
            pe.wait(core.bank_read[b], subkeys_ready, *query_ready[4 * g:4 * g + 4])
            for i in range(4):
                scored = pe.engine.matmul(core.bank[b][:, i * P:i * P + P], query[:, 4 * g + i, t * P:t * P + P],
                                          subkeys[:, 4 * g + i, :], start=True, stop=True)
            lane = act if g % 2 else dve
            core.bank_read[b] = copy_out(core, lane, scores[:, t, 4 * g:4 * g + 4, :],
                                         core.bank[b][:, :].rearrange("p (a k) -> p a k", a=4), [pe.mark(scored)])
            marks.append(core.bank_read[b])
    return marks


def top_sixteen(core, pairs):
    dve = core.dve
    v = dve.engine
    first = [dve.mark(v.max(top[:, 0:8], values)) for values, work, top, places in pairs]
    for n, (values, work, top, places) in enumerate(pairs):
        dve.wait(first[n])
        dve.mark(v.max_index(places[:, 0:8], top[:, 0:8], values))
    rest = [dve.mark(v.match_replace(work, top[:, 0:8], values, -3e38)) for values, work, top, places in pairs]
    for n, (values, work, top, places) in enumerate(pairs):
        dve.wait(rest[n])
        first[n] = dve.mark(v.max(top[:, 8:16], work))
    for n, (values, work, top, places) in enumerate(pairs):
        dve.wait(first[n])
        done = dve.mark(v.max_index(places[:, 8:16], top[:, 8:16], work))
    return done


def choose_experts(core, dram, keep, scores, scores_ready, chosen, region):
    pe, act, dve = core.pe, core.act, core.dve
    work = [region.tensor(f"top_work{i}", [P, 2 * N_KEYS], F32) for i in range(2)]
    cand = [region.tensor(f"candidates{i}", [P, PEER_TOPK, PEER_TOPK], F32) for i in range(2)]
    top = region.tensor("top", [P, HP, PEER_TOPK], F32)
    places = region.tensor("places", [P, HP, PEER_TOPK], U32)
    keys = region.tensor("top_keys", [P, HP, PEER_TOPK], F32)
    best = region.tensor("best", [P, PEER_HEADS, PEER_TOPK], F32)
    best_at = region.tensor("best_at", [P, PEER_HEADS, PEER_TOPK], U32)
    digit = region.tensor("digit", [P, 2, PEER_HEADS, PEER_TOPK], U32)
    digit_value = region.tensor("digit_value", [P, 2, PEER_HEADS, PEER_TOPK], F32)
    match = region.tensor("match", [P, PEER_HEADS * PEER_TOPK, PEER_TOPK], F32)
    picked = region.tensor("picked", [P, 3, HK], F32)
    total = region.tensor("gate_total", [P, 2, PEER_HEADS], F32)
    v = dve.engine
    turned = None
    dve.wait(*scores_ready)
    act.wait(*scores_ready)
    yield
    for t in range(TT):
        for hp in range(0, HP, 2):
            done = top_sixteen(core, [(scores[:, t, hp + i, :], work[i][:, 0:N_KEYS], top[:, hp + i, :], places[:, hp + i, :])
                                      for i in range(2)])
            yield
        dve.wait(done)
        keys_ready = dve.mark(v.tensor_copy(keys[:, :, :], places[:, :, :]))
        for h in range(0, PEER_HEADS, 2):
            rows = []
            for i in range(2):
                a = top[:, 2 * (h + i), :].unsqueeze(2).broadcast_to([P, PEER_TOPK, PEER_TOPK])
                b = top[:, 2 * (h + i) + 1, :].unsqueeze(1).broadcast_to([P, PEER_TOPK, PEER_TOPK])
                summed = dve.mark(v.tensor_tensor(cand[i][:, :, :], a, b, ALU.add))
                rows.append((cand[i][:, :, :].rearrange("p a b -> p (a b)"), work[i][:, :], best[:, h + i, :], best_at[:, h + i, :]))
            dve.wait(summed)
            done = top_sixteen(core, rows)
            yield
        gate = picked[:, 2, :].rearrange("p (h k) -> p h k", h=PEER_HEADS)
        dve.wait(done, turned)
        shifted = dve.mark(v.tensor_tensor(gate, best[:, :, :], best[:, :, 0:1].broadcast_to([P, PEER_HEADS, PEER_TOPK]), ALU.subtract))
        act.wait(shifted)
        powered = act.mark(act.engine.activation(picked[:, 2, :], picked[:, 2, :], ACT.Exp))
        dve.mark(v.tensor_scalar(digit[:, 0, :, :], best_at[:, :, :], 4, None, ALU.logical_shift_right))
        split = dve.mark(v.tensor_scalar(digit[:, 1, :, :], best_at[:, :, :], 15, None, ALU.bitwise_and))
        dve.wait(split)
        digits = dve.mark(v.tensor_copy(digit_value[:, :, :, :], digit[:, :, :, :]))
        dve.wait(powered)
        summed = dve.mark(v.tensor_reduce(total[:, 0, :], gate, AX_X, ALU.add))
        dve.wait(summed)
        inverse = dve.mark(v.reciprocal(total[:, 1, :], total[:, 0, :]))
        dve.wait(inverse, digits, keys_ready)
        gated = dve.mark(v.tensor_tensor(gate, gate, total[:, 1, :].unsqueeze(2).broadcast_to([P, PEER_HEADS, PEER_TOPK]), ALU.mult))
        yield
        for half in range(2):
            wide = [P, HK, PEER_TOPK]
            ranks = keep.counting[:, 0:PEER_TOPK].unsqueeze(1).broadcast_to(wide)
            chosen_rank = digit_value[:, half, :, :].rearrange("p h k -> p (h k)").unsqueeze(2).broadcast_to(wide)
            compared = dve.mark(v.tensor_tensor(match[:, :, :], chosen_rank, ranks, ALU.is_equal))
            dve.wait(compared)
            yield
            for h in range(PEER_HEADS):
                part = match[:, h * PEER_TOPK:(h + 1) * PEER_TOPK, :]
                of_rank = keys[:, 2 * h + half, :].unsqueeze(1).broadcast_to([P, PEER_TOPK, PEER_TOPK])
                marked = dve.mark(v.tensor_tensor(part, part, of_rank, ALU.mult))
            dve.wait(marked)
            yield
            picked_ready = dve.mark(v.tensor_reduce(picked[:, half, :], match[:, :, :], AX_X, ALU.add))
            dve.wait(picked_ready)
        yield
        b = GATE_BANKS[t % 4]
        pe.wait(picked_ready, gated, core.bank_read[b])
        for i in range(3):
            step = pe.engine.transpose(core.bank[b][:, i * P:i * P + P], picked[:, i, :], keep.ident[:, :])
        turned = pe.mark(step)
        for i in range(3):
            moved = copy_out(core, act, chosen[i][:, t * P:t * P + P], core.bank[b][:, i * P:i * P + P], [turned])
        core.bank_read[b] = moved
        yield
    keep.chosen_ready = moved


def build_gates(core, dram, keep, chosen, region):
    pe, act, dve = core.pe, core.act, core.dve
    key1, key2, gate = chosen
    stages = [region.tensor(f"gate_stage{i}", [P, N_KEYS, GATE_CHUNK], F32) for i in range(2)]
    every_key = region.tensor("every_key", [P, N_KEYS, HOT], F16)
    parts = [region.tensor(f"gate_part{i}", [P, T], F16) for i in range(2)]
    ring = 2
    hot1 = [region.tensor(f"hot1_{i}", [P, N_KEYS, HOT], F16) for i in range(ring)]
    hot2 = region.tensor("hot2", [P, N_KEYS, HOT], F16)
    weighed = [[region.tensor(f"hot2_part{p}_{i}", [P, N_KEYS, HOT], F16) for p in range(2)] for i in range(ring)]
    stored_signal = [Signal(core.nc, f"gates_stored{i}") for i in range(2)]
    v = dve.engine
    shape = [P, N_KEYS, HOT]
    dve.wait(keep.chosen_ready)
    dve.mark(v.tensor_copy(every_key[:, :, :], keep.counting[:, :].unsqueeze(2).broadcast_to(shape)))
    first = dve.mark(v.tensor_scalar(parts[0][:, :], gate[:, :], GATE_SCALE, None, ALU.mult))
    dve.wait(first)
    dve.wait(dve.mark(v.scalar_tensor_tensor(out=parts[1][:, :], in0=gate[:, :], scalar=GATE_SCALE, in1=parts[0][:, :],
                                             op0=ALU.mult, op1=ALU.subtract)))
    yield
    used, hot_ready = [None] * ring, {}
    stored = [None, None]
    blocks = T // HOT

    def make_hot(n):
        part = slice(n * HOT, (n + 1) * HOT)
        dve.wait(used[n % ring])
        dve.mark(v.tensor_tensor(hot1[n % ring][:, :, :], every_key[:, :, :],
                                 key1[:, part].unsqueeze(1).broadcast_to(shape), ALU.is_equal))
        yield
        dve.wait(hot_ready.get(n - 1))
        second = dve.mark(v.tensor_tensor(hot2[:, :, :], every_key[:, :, :],
                                          key2[:, part].unsqueeze(1).broadcast_to(shape), ALU.is_equal))
        dve.wait(second)
        yield
        for p in range(2):
            hot_ready[n] = dve.mark(v.tensor_tensor(weighed[n % ring][p][:, :, :], hot2[:, :, :],
                                                    parts[p][:, part].unsqueeze(1).broadcast_to(shape), ALU.mult))
            yield

    for _ in make_hot(0):
        yield
    for _ in range(3):
        yield
    for n in range(blocks):
        following = make_hot(n + 1) if n + 1 < blocks else iter(())
        for q in range(HOT // BATCH):
            b = GATE_BANKS[q % 4]
            pe.wait(hot_ready[n], core.bank_read[b])
            for i in range(BATCH):
                for p in range(2):
                    t = q * BATCH + i
                    step = pe.engine.matmul(core.bank[b][:, i * P:i * P + P], hot1[n % ring][:, :, t],
                                            weighed[n % ring][p][:, :, t], start=(p == 0), stop=(p == 1))
            used[n % ring] = built = pe.mark(step)
            at = n * HOT + q * BATCH
            chunk, within = at // GATE_CHUNK, at % GATE_CHUNK
            act.wait(built, stored[chunk % 2])
            core.bank_read[b] = act.mark(act.engine.activation(
                stages[chunk % 2][:, :, within:within + BATCH],
                core.bank[b][:, :].rearrange("p (t k) -> p k t", t=BATCH), ACT.Copy, scale=1.0 / GATE_SCALE))
            if within == GATE_CHUNK - BATCH:
                act.wait(core.bank_read[b])
                stored[chunk % 2] = stored_signal[chunk % 2].after(
                    act.engine.dma_start(dram["gates"][chunk], stages[chunk % 2][:, :, :]), 16)
                keep.gates_stored = list(stored)
            next(following, None)
            yield
        for _ in following:
            yield


def hidden_units(core, dram, keep, xn_high, xn_low, background, following):
    pe, act, dve, sp = core.pe, core.act, core.dve, core.sp
    RAW, PAIR, OUT = U_RAW, 3, 3
    at_raw, at_pairs = Region(core.nc, keep.u_raw_at), Region(core.nc, keep.stream_at)
    raw = [at_raw.tensor(f"u_raw{i}", [P, KT, P], F32) for i in range(RAW)]
    assert at_raw.at <= keep.stream_at
    high = [at_pairs.tensor(f"u_high{i}", [P, KT, P], F32R) for i in range(PAIR)]
    low = [at_pairs.tensor(f"u_low{i}", [P, KT, P], F32R) for i in range(PAIR)]
    out = [at_pairs.tensor(f"hidden{i}", [P, T], F32) for i in range(OUT)]
    assert at_pairs.at <= keep.stream_at + WeightStream.BYTES
    arrived = [Signal(core.nc, f"u_arrived{i}") for i in range(RAW)]
    stored = [Signal(core.nc, f"hidden_stored{i}") for i in range(OUT)]
    stored_at = [None] * OUT
    split_of, landed, product_of = {}, {}, {}

    def load(j):
        sp.wait(*split_of.get(j - RAW, []))
        landed[j] = arrived[j % RAW].after(sp.engine.dma_start(raw[j % RAW][:, :, :], dram["peer_u"][j]), 16)

    def split(j):
        split_of[j] = split_pair(core, raw[j % RAW][:, :, :], high[j % PAIR][:, :, :], low[j % PAIR][:, :, :],
                                 [landed[j], product_of.get(j - PAIR)])

    for j in range(RAW):
        load(j)
    act.wait(core.pe.latest())
    dve.wait(core.pe.latest())
    split(0)
    split(1)
    yield
    for j in range(N_KEYS):
        if j + 2 < N_KEYS:
            split(j + 2)
        b = EARLY_BANKS[j % 4]
        pe.wait(*split_of[j], core.bank_read[b])
        for k in range(KT):
            step = three_products(pe.engine, core.bank[b][:, :], (high[j % PAIR][:, k, :], low[j % PAIR][:, k, :]),
                                  (xn_high[:, k, :], xn_low[:, k, :]), k == 0, k == KT - 1)
        product_of[j] = pe.mark(step)
        for _ in range(pace(j)):
            next(background, None)
        if j + RAW < N_KEYS:
            load(j + RAW)
        act.wait(product_of[j], stored_at[j % OUT])
        core.bank_read[b] = act.mark(act.engine.activation(out[j % OUT][:, :], core.bank[b][:, :], ACT.Gelu))
        sp.wait(core.bank_read[b])
        stored_at[j % OUT] = stored[j % OUT].after(sp.engine.dma_start(dram["hidden"][j], out[j % OUT][:, :]), 16)
        if (j + 1) % GROUP == 0:
            keep.hidden_stored[j // GROUP] = [stored_at[m % OUT] for m in range(max(0, j - OUT + 1), j + 1)]
        if j == N_KEYS - 12:
            for _ in background:
                pass
        if j in (N_KEYS - 12, N_KEYS - 9, N_KEYS - 7, N_KEYS - 5, N_KEYS - 3, N_KEYS - 2):
            next(following)


def combine(core, dram, keep, region):
    pe, act, dve, sp = core.pe, core.act, core.dve, core.sp
    chunks = T // GATE_CHUNK
    gate = [region.tensor(f"gate_in{i}", [P, chunks, GROUP, GATE_CHUNK], F32) for i in range(2)]
    hidden = [region.tensor(f"hidden_in{i}", [P, GROUP, T], F32) for i in range(2)]
    value = [region.tensor(f"v_raw{i}", [P, GROUP, BANK], F32) for i in range(2)]
    keep.values_at = region.at
    value_pair = [[region.tensor(f"v_{n}{i}", [P, GROUP, BANK], F32R) for n in ("high", "low")] for i in range(2)]
    early = [region.tensor(f"w_{n}0", [P, GROUP, T], F32R) for n in ("high", "low")]
    assert region.at <= keep.u_raw_at
    after_xn = Region(core.nc, keep.rows_at)
    late = [after_xn.tensor(f"w_{n}1", [P, GROUP, T], F32R) for n in ("high", "low")]
    weight_pair = [early, late]
    arrived = {n: [Signal(core.nc, f"{n}_arrived{i}") for i in range(2)] for n in ("gate", "hid", "v")}
    groups = N_KEYS // GROUP
    split_of, landed, half_done, multiplied, weight_ready = {}, {}, {}, {}, {}

    def load_weights(g):
        s = g % 2
        sp.wait(*keep.gates_stored, *keep.hidden_stored[g], *weight_ready.get(g - 2, []))
        for c in range(chunks):
            mark = arrived["gate"][s].after(sp.engine.dma_start(
                gate[s][:, c, :, :], dram["gates"][c][:, g * GROUP:(g + 1) * GROUP, :]), 16)
        landed["w", g] = [mark, arrived["hid"][s].after(sp.engine.dma_start(
            hidden[s][:, :, :], dram["hidden"][g * GROUP:(g + 1) * GROUP].rearrange("j p t -> p j t")), 16)]

    def load_values(n):
        g, half = n // 2, n % 2
        sp.wait(*split_of.get(n - 2, []))
        landed["v", n] = arrived["v"][n % 2].after(sp.engine.dma_start(
            value[n % 2][:, :, :], dram["peer_v"][:, g * GROUP:(g + 1) * GROUP, half * BANK:(half + 1) * BANK]), 16)

    def prepare_values(n):
        high, low = value_pair[n % 2]
        split_of[n] = split_pair(core, value[n % 2][:, :, :], high[:, :, :], low[:, :, :],
                                 [landed["v", n], half_done.get(n - 2)])

    def multiply_weights(g):
        s = g % 2
        product = hidden[s][:, :, :].rearrange("p j (c t) -> p j c t", c=chunks)
        dve.wait(*landed["w", g])
        for j in range(GROUP):
            step = dve.engine.tensor_tensor(product[:, j, :, :], product[:, j, :, :], gate[s][:, :, j, :], ALU.mult)
        multiplied[g] = dve.mark(step)

    def split_weights(g):
        s = g % 2
        high, low = weight_pair[s]
        weight_ready[g] = split_pair(core, hidden[s][:, :, :], high[:, :, :], low[:, :, :],
                                     [multiplied[g], half_done.get(2 * (g - 2) + 1)])

    built = [core.pe.latest(), core.act.latest(), core.dve.latest(), *keep.gates_stored]
    for lane in (sp, act, dve):
        lane.wait(*built)
    load_weights(0)
    yield
    load_values(0)
    yield
    load_values(1)
    yield
    multiply_weights(0)
    yield
    split_weights(0)
    yield
    prepare_values(0)
    yield
    load_weights(1)
    act.wait(pe.latest())
    dve.wait(pe.latest())
    keep.x_rows = x_rows = [[None, None] for _ in range(TT)]
    for n in range(2 * groups):
        g, half = n // 2, n % 2
        if n + 1 < 2 * groups:
            prepare_values(n + 1)
        if n + 2 < 2 * groups:
            load_values(n + 2)
        if half == 0 and g + 1 < groups:
            multiply_weights(g + 1)
            split_weights(g + 1)
            if g + 2 < groups:
                load_weights(g + 2)
        if n in (2 * groups - 6, 2 * groups - 4):
            yield
        value_high, value_low = value_pair[n % 2]
        weight_high, weight_low = weight_pair[g % 2]
        pe.wait(*split_of[n], *weight_ready[g])
        for t in range(TT):
            b = 4 * half + t
            pe.wait(core.bank_read[b])
            for j in range(GROUP):
                part = slice(t * P, t * P + P)
                step = three_products(pe.engine, core.bank[b][:, :], (weight_high[:, j, part], weight_low[:, j, part]),
                                      (value_high[:, j, :], value_low[:, j, :]), j == 0, j == GROUP - 1)
            half_done[n] = pe.mark(step)
            out = keep.x[:, t, half * BANK:(half + 1) * BANK]
            dve.wait(half_done[n])
            core.bank_read[b] = x_rows[t][half] = dve.mark(dve.engine.tensor_tensor(out, out, core.bank[b][:, :], ALU.add))
            if g == groups - 1:
                yield


def pace(j):
    return 1 + (j % 4 == 3) if j < 64 else 3


def peer(core, dram, keep):
    nc = core.nc
    core.sp.wait(*core.meet())
    region = Region(nc, keep.rows_at)
    xn_high = region.tensor("xn_high", [P, KT, T], F32R)
    xn_low = region.tensor("xn_low", [P, KT, T], F32R)
    chosen = [region.tensor(n, [P, T], dtype) for n, dtype in (("key1", F16), ("key2", F16), ("gate", F32))]
    scores_at = keep.scores_at = region.at
    scores = region.tensor("scores", [P, TT, HP, N_KEYS], F32)
    after_scores = region.at
    keep.hidden_stored = {}
    keep.u_raw_at = keep.stream_at - U_RAW * KT * P * 4

    def background():
        yield from choose_experts(core, dram, keep, scores, scores_ready, chosen, Region(nc, after_scores))
        core.act.wait(core.dve.latest(), core.pe.latest())
        core.dve.wait(core.act.latest(), core.pe.latest())
        yield from build_gates(core, dram, keep, chosen, Region(nc, scores_at))

    combining = combine(core, dram, keep, Region(nc, scores_at))
    hidden = hidden_units(core, dram, keep, xn_high, xn_low, background(), combining)
    scores_ready = peer_scores(core, dram, keep, xn_high, xn_low, Region(nc, after_scores), scores, hidden)
    for _ in hidden:
        pass
    keep.first_stage_done = [core.pe.latest(), core.act.latest(), core.dve.latest(), *keep.gates_stored,
                             *keep.hidden_stored[N_KEYS // GROUP - 1]]
    next(combining)
    return combining


TWO_PI = 2.0 * float(np.pi)
TURN = (6.28125, float(np.float32(1.9350051879882812e-03)), 0.0)
TURN = (TURN[0], TURN[1], TWO_PI - TURN[0] - TURN[1])
ROUND = 1.5 * 2.0 ** 23
PI_BELOW = 3.1415925
SPARE = 1.2
FREQS = 12


def rotary_tables(core, dram, region):
    act, dve = core.act, core.dve
    v = dve.engine
    position = region.tensor("position", [P, TT], I32)
    position_value = region.tensor("position_value", [P, TT], F32)
    frequency = region.tensor("frequency", [P, FREQS], F32)
    angle = region.tensor("angle", [P, TT, FREQS], F32)
    turns = region.tensor("turns", [P, TT, FREQS], F32)
    tables = [region.tensor(n, [P, TT, FREQS], F32) for n in ("cosine", "sine")]
    loaded = [core.load("position_arrived", position[:, :], dram["positions"], act),
              core.load("frequency_arrived", frequency[:, :], dram["frequencies"], act)]
    dve.wait(*loaded)
    dve.wait(dve.mark(v.tensor_copy(position_value[:, :], position[:, :])))
    shape = [P, TT, FREQS]
    dve.wait(dve.mark(v.tensor_tensor(angle[:, :, :], position_value[:, :].unsqueeze(2).broadcast_to(shape),
                                      frequency[:, :].unsqueeze(1).broadcast_to(shape), ALU.mult)))
    ready = []
    for table, quarter in zip(tables, (0.25, 0.0)):
        dve.wait(dve.mark(v.tensor_scalar(turns[:, :, :], angle[:, :, :], 1.0 / TWO_PI, quarter, ALU.mult, ALU.add)))
        dve.wait(dve.mark(v.tensor_scalar(turns[:, :, :], turns[:, :, :], ROUND, None, ALU.add)))
        dve.wait(dve.mark(v.tensor_scalar(turns[:, :, :], turns[:, :, :], ROUND, None, ALU.subtract)))
        source = angle
        for part in TURN:
            dve.wait(dve.mark(v.scalar_tensor_tensor(out=table[:, :, :], in0=turns[:, :, :], scalar=-part,
                                                     in1=source[:, :, :], op0=ALU.mult, op1=ALU.add)))
            source = table
        dve.wait(dve.mark(v.tensor_scalar(table[:, :, :], table[:, :, :], quarter * TWO_PI, PI_BELOW, ALU.add, ALU.min)))
        reduced = dve.mark(v.tensor_scalar(table[:, :, :], table[:, :, :], -PI_BELOW, None, ALU.max))
        dve.wait(reduced)
        act.wait(reduced)
        ready.append(act.mark(act.engine.activation(table[:, :, :], table[:, :, :], ACT.Sin)))
    return tables, ready


def rotate(core, tensor, heads, width, pairs, cosine, sine, at, scratch):
    dve = core.dve
    v = dve.engine
    view = tensor.rearrange("p t (h d) -> p t h d", h=heads)
    one, two = view[:, :, :, 0:pairs], view[:, :, :, pairs:2 * pairs]
    shape = [P, TT, heads, pairs]
    c = cosine[:, :, at:at + pairs].unsqueeze(2).broadcast_to(shape)
    s = sine[:, :, at:at + pairs].unsqueeze(2).broadcast_to(shape)
    size = TT * heads * pairs
    parts = [scratch[:, i, 0:size].rearrange("p (t h d) -> p t h d", t=TT, h=heads) for i in range(4)]
    for out, a, b in ((parts[0], one, c), (parts[1], two, s), (parts[2], one, s), (parts[3], two, c)):
        product = dve.mark(v.tensor_tensor(out, a, b, ALU.mult))
    dve.wait(product)
    dve.mark(v.tensor_tensor(one, parts[0], parts[1], ALU.subtract))
    done = dve.mark(v.tensor_tensor(two, parts[2], parts[3], ALU.add))
    dve.wait(done)
    return done


def norm_heads(core, tensor, heads, gain, square, small, ready):
    act, dve = core.act, core.dve
    v = dve.engine
    view = tensor.rearrange("p t (h d) -> p t h d", h=heads)
    squared = square[:, 0:TT * heads * HEAD_DIM].rearrange("p (t h d) -> p t h d", t=TT, h=heads)
    sums, scratch, scale = (small[:, i, 0:TT * heads] for i in range(3))
    act.wait(*ready, dve.latest())
    squares = act.mark(act.engine.activation(squared, view, ACT.Square))
    dve.wait(*ready, squares)
    size = TT * heads * HEAD_DIM / 1000
    yield 0.3 + size / 2
    summed = dve.mark(v.tensor_reduce(sums, square[:, 0:TT * heads * HEAD_DIM].rearrange("p (a d) -> p a d", d=HEAD_DIM),
                                      AX_X, ALU.add))
    yield size
    scaled = rms_scale(core, sums, scratch, scale, HEAD_DIM, [summed])
    dve.wait(scaled)
    shape = [P, TT, heads, HEAD_DIM]
    dve.wait(dve.mark(v.tensor_tensor(view, view, scale.rearrange("p (t h) -> p t h", t=TT).unsqueeze(3).broadcast_to(shape), ALU.mult)))
    yield 1 + size
    for t in range(TT):
        done = dve.mark(v.tensor_tensor(view[:, t, :, :], view[:, t, :, :],
                                        gain.unsqueeze(1).broadcast_to([P, heads, HEAD_DIM]), ALU.mult))
    dve.wait(done)
    yield size


def index_scores(core, t, allowed, index_q, index_k, weight, total, relus, used, bank, ready):
    pe, act, dve = core.pe, core.act, core.dve
    n = (t + 1) * P
    for h in range(IDX_HEADS):
        pe.wait(core.bank_read[bank], *ready)
        scored = pe.mark(pe.engine.matmul(core.bank[bank][:, 0:n], index_q[:, h // 4, t * P:t * P + P],
                                          index_k[:, h % 4, 0:n], start=True, stop=True))
        relu = relus[h % 2][:, 0:n]
        act.wait(scored, used[h % 2])
        core.bank_read[bank] = act.mark(act.engine.activation(relu, core.bank[bank][:, 0:n], ACT.Relu))
        dve.wait(core.bank_read[bank], dve.latest())
        used[h % 2] = dve.mark(dve.engine.scalar_tensor_tensor(
            out=total, in0=relu, scalar=weight[:, t, h:h + 1], in1=allowed[:, T - n:T] if h == 0 else total,
            op0=ALU.mult, op1=ALU.add))
        yield 0.2 + n / 1000


def choose_keys(core, t, allowed, scores, works, top, bias_ready):
    dve = core.dve
    v = dve.engine
    n = (t + 1) * P
    now = scores
    for r in range(K_SEL // 8):
        best = top[:, 8 * (r % 2):8 * (r % 2) + 8]
        dve.wait(dve.latest())
        dve.wait(dve.mark(v.max(best, now)))
        after = works[r % 2][:, 0:n]
        dve.mark(v.match_replace(after, best, now, -3e38))
        now = after
        yield 0.3 + n / 430
    dve.wait(dve.latest())
    dve.wait(dve.mark(v.tensor_scalar(now, now, -2e38, NEG, ALU.is_gt, ALU.mult)))
    bias_ready[t] = dve.mark(v.tensor_tensor(scores, now, allowed[:, T - n:T], ALU.add))
    yield 0.3 + n / 500


def block_two(core, dram, keep, combining):
    nc, pe, act, dve, sp, stream = core.nc, core.pe, core.act, core.dve, core.sp, keep.stream
    v = dve.engine
    x, ident = keep.x, keep.ident[:, :]

    outs = Region(nc, keep.rows_at)
    z_a = outs.tensor("z_a", [P, TT, T], F32)
    mixed = outs.tensor("z_b", [P, 4, T], F32)
    assert outs.at <= keep.rows_at + 16384
    allowed = outs.tensor("allowed_sb", [P, T], F32)
    final_gain_at = outs.at
    final_gain = outs.tensor("final_gain", [P, D], F32)
    final_gain_end = outs.at
    relus = [outs.tensor(f"relu{i}", [P, T], F32) for i in range(2)]
    totals = [outs.tensor(f"index_total{i}", [P, T], F32) for i in range(2)]
    small = outs.tensor("small_two", [P, 4, 64], F32)
    pool_start = outs.tensor("pool_start_sb", [P, 64], F32)
    pool_scale = outs.tensor("pool_scale_sb", [P, 4], F32)
    merge_bias = outs.tensor("merge_bias_sb", [P, 16], F32)
    head_gain = outs.tensor("head_gain", [P, 2, HEAD_DIM], F32)
    top = outs.tensor("index_top", [P, 16], F32)
    pool_weights = outs.tensor("pool_weights", [P, 4, P], F32)
    rotary = outs
    rows = Region(nc, keep.scores_at)
    pooled = rows.tensor("pooled", [P, 4, T], F32)
    kvi = rows.tensor("k_v_qi", [P, TT, T], F32)
    q_turned = rows.tensor("q_turned", [P, 4, T], F32)
    keys = rows.tensor("keys", [P, 4, T], F32)
    q = rows.tensor("q", [P, TT, T], F32)
    bias = rows.tensor("bias", [P, TT, T], F32)
    assert rows.at == keep.values_at
    h_high = rows.tensor("h2_high", [P, KT, T], F32R)
    h_low = rows.tensor("h2_low", [P, KT, T], F32R)
    work_at = rows.at
    gate = [rows.tensor(f"gate_two{i}", [P, 4, T], F32) for i in range(2)]
    index_at = rows.at
    index_q = rows.tensor("index_q", [P, 2, T], F32)
    index_k = rows.tensor("index_k", [P, 4, T], F32)
    kiw = rows.tensor("ki_wi", [P, TT, IDX_DIM + IDX_HEADS], F32)
    summing = [rows.tensor(f"summing{i}", [P, 16 + T], F32) for i in range(2)]
    turned_at = rows.at
    index_k_four = rows.tensor("index_k_four", [P, TT, 4, IDX_DIM], F32)
    turned_region, weights_region = Region(nc, turned_at), Region(nc, final_gain_at)
    turned_weights = [turned_region.tensor(f"turned{i}", [P, T], F32) for i in range(2)]
    assert turned_region.at <= keep.stream_at
    weights = [weights_region.tensor(f"weights{i}", [P, T], F32) for i in range(2)]
    assert weights_region.at <= final_gain_end
    early = Region(nc, keep.scores_at)
    normed = early.tensor("normed_two", [P, TT, D], F32)
    junk = early.tensor("junk_two", [P, BANK], F32)
    work = Region(nc, work_at)
    square = work.tensor("square", [P, TT * T], F32)
    rotary_work = work.tensor("rotary_work", [P, 4, 256], F32)
    keys_twice = work.tensor("keys_twice", [P, TT, 4, HEAD_DIM], F32)
    assert work.at <= work_at + 16384

    act.wait(*keep.first_stage_done)
    tables = [core.load(n + "_arrived", tile, source, act) for n, tile, source in (
        ("final_gain", final_gain[:, :], row_of(dram["final_norm_g"], D)),
        ("allowed", allowed[:, :], dram["allowed"]), ("pool_start", pool_start[:, :], dram["pool_start"]),
        ("pool_scale", pool_scale[:, :], dram["pool_scale"]), ("merge_bias", merge_bias[:, :], dram["merge_bias"]),
        ("q_gain", head_gain[:, 0, :], row_of(dram["q_norm_g"], HEAD_DIM)),
        ("k_gain", head_gain[:, 1, :], row_of(dram["k_norm_g"], HEAD_DIM)),
        ("pool_weights", pool_weights[:, :, :], dram["pool_w"]))]
    w = dram["w_in_2"]
    for columns in ((1024, 1064), (512, 1024), (1576, 2088), (2088, 2600), (1064, 1576), (0, 512)):
        stream.add(w, columns)
    for half in range(2):
        for branch in range(2):
            stream.add(w, (2600 + 1024 * branch + 512 * half, 2600 + 1024 * branch + 512 * half + 512))
        stream.add(dram["w_branch_b"], (half * 512, half * 512 + 512))
        stream.add(dram["w_branch_a"], (half * 512, half * 512 + 512))
    for half in range(2):
        stream.add(dram["w_out_2"], (half * 512, half * 512 + 512))
    stream.release(*keep.first_stage_done)
    dve.wait(*keep.first_stage_done)
    next(combining)
    stream.split_next()
    stream.split_next()
    (cosine, sine), rotary_ready = rotary_tables(core, dram, rotary)
    assert rotary.at <= keep.scores_at
    dve.wait(*tables, *rotary_ready)
    gains_ready = dve.mark(v.tensor_scalar(head_gain[:, 0, :], head_gain[:, 0, :], HEAD_DIM ** -0.5, None, ALU.mult))

    act.wait(gains_ready)
    act.mark(act.engine.activation(small[:, 2, 0:1], keep.ident[:, 0:1], ACT.Sqrt))

    halves, both_total, both_scratch, both = small_columns(keep.norm_small)
    last_halves, last_total, last_scratch, last_scale = small_columns(keep.norm_small[:, 5 * TT:10 * TT])
    squared = [[] for _ in range(TT)]
    for half in range(2):
        for t in range(TT):
            next(combining)
            at = slice(2 * t + half, 2 * t + half + 1)
            part, gained_part = x[:, t, half_of(half)], normed[:, t, half_of(half)]
            squared[t].append(square_half(core, act, part, junk[:, :], last_halves[:, at], [keep.x_rows[t][half]]))
            dve.wait(keep.x_rows[t][half])
            gained = dve.mark(v.tensor_tensor(gained_part, part, final_gain[:, half_of(half)], ALU.mult))
            squared[t].append(square_half(core, act, gained_part, junk[:, :], halves[:, at], [gained]))
    for _ in combining:
        pass
    rows_ready = []
    for pair in range(0, TT, 2):
        two, four = slice(pair, pair + 2), slice(2 * pair, 2 * pair + 4)
        dve.wait(pair_scale(core, last_halves[:, four], last_total[:, two], last_scratch[:, two], last_scale[:, two],
                            squared[pair] + squared[pair + 1]))
        sums = halves[:, four].rearrange("p (t h) -> p t h", h=2)
        dve.wait(dve.mark(v.tensor_tensor(both_total[:, two], sums[:, :, 0], sums[:, :, 1], ALU.add)))
        for _ in range(2):
            meant = dve.mark(v.tensor_tensor(both_total[:, two], both_total[:, two], last_scale[:, two], ALU.mult))
            dve.wait(meant)
        dve.wait(rms_scale(core, both_total[:, two], both_scratch[:, two], both[:, two], D, [meant]))
        scaled = dve.mark(v.tensor_tensor(both[:, two], both[:, two], last_scale[:, two], ALU.mult))
        for t in (pair, pair + 1):
            rows_ready.append(scale_rows(core, normed[:, t, :], normed[:, t, :], both[:, t:t + 1], [scaled]))
    h_ready = turn_to_pair(core, normed, h_high, h_low, range(KT), ident, rows_ready, range(8), keep.gains[2])

    turned_all = [mark for marks in h_ready.values() for mark in marks]
    act.wait(*turned_all)
    dve.wait(*turned_all)
    core.pool.wait(*turned_all)
    core.pool.mark(core.pool.engine.memset(keys[:, :, :], 0.0))
    cleared = core.pool.mark(core.pool.engine.memset(index_k[:, :, :], 0.0))

    def residual():
        for t in range(TT):
            dve.mark(v.scalar_tensor_tensor(out=x[:, t, :], in0=x[:, t, :], scalar=last_scale[:, t:t + 1], in1=final_gain[:, :],
                                            op0=ALU.mult, op1=ALU.mult))
            yield

    made = {}

    def gather(name, tensor, width, token_major, between, func=ACT.Copy):
        summed = project(core, stream, KT, width, (h_high, h_low), h_ready, token_major, range(4), between)
        made[name] = []
        for t in range(4):
            core.bank_read[t] = copy_out(core, act, tensor[:, t, 0:width], core.bank[t][:, 0:width], [summed[t]], func=func)
            made[name].append(core.bank_read[t])

    turns = [0]

    def turn_out(source, evacuate, ready):
        b = 4 + turns[0] % 4
        turns[0] += 1
        pe.wait(core.bank_read[b], *ready)
        for t in range(TT):
            step = pe.engine.transpose(core.bank[b][:, t * P:t * P + P], source(t), ident)
        core.bank_read[b] = evacuate(core.bank[b], pe.mark(step))
        return core.bank_read[b]

    def spread(out, parts):
        size = P // parts

        def evacuate(bank, turned):
            act.wait(turned, cleared)
            for j in range(parts):
                part = slice(size * j, size * j + size)
                step = act.mark(act.engine.activation(out[part, j, :], bank[part, :], ACT.Copy))
            return step
        return evacuate

    keys_ready, index_ready, q_turned_ready = [], [], []
    weight = kiw[:, :, IDX_DIM:IDX_DIM + IDX_HEADS]

    def keys_and_index():
        yield from norm_heads(core, kvi[:, :, 0:128], KV_HEADS, head_gain[:, 1, :], square, small, made["kvi"])
        rotated = rotate(core, kvi[:, :, 0:128], KV_HEADS, HEAD_DIM, 8, cosine, sine, 0, rotary_work)
        act.wait(rotated)
        for g in range(KV_HEADS):
            for again in range(2):
                twice = act.mark(act.engine.activation(keys_twice[:, :, 2 * g + again, :], kvi[:, :, g * 64:g * 64 + 64], ACT.Copy))
        yield 4.5
        for g in range(KV_HEADS):
            keys_ready.append(turn_out(lambda t: keys_twice[:, t, 2 * g:2 * g + 2, :].rearrange("p a d -> p (a d)"),
                                       spread(keys[:, 2 * g:2 * g + 2, :], 2), [twice]))
            yield 0.1
        rotated = rotate(core, kvi[:, :, 256:512], IDX_HEADS, IDX_DIM, 4, cosine, sine, 8, rotary_work)
        yield 2.0
        for c in range(2):
            index_ready.append(turn_out(lambda t: kvi[:, t, 256 + c * P:256 + c * P + P],
                                        lambda bank, turned: copy_out(core, act, index_q[:, c, :], bank[:, :], [turned]),
                                        [rotated]))
            yield 0.1
        dve.wait(*made["kiw"])
        rotated = rotate(core, kiw[:, :, 0:IDX_DIM], 1, IDX_DIM, 4, cosine, sine, 8, rotary_work)
        index_ready.append(dve.mark(v.tensor_scalar(weight, weight, IDX_DIM ** -0.5 * IDX_HEADS ** -0.5, None, ALU.mult)))
        act.wait(rotated)
        for again in range(4):
            four = act.mark(act.engine.activation(index_k_four[:, :, again, :], kiw[:, :, 0:IDX_DIM], ACT.Copy))
        yield 2.5
        index_ready.append(turn_out(lambda t: index_k_four[:, t, :, :].rearrange("p a d -> p (a d)"),
                                    spread(index_k, 4), [four]))

    scaling = residual()
    columns = IDX_DIM + IDX_HEADS
    summed = project(core, stream, KT, columns, (h_high, h_low), h_ready, False, [0])
    kiw_turned = relus[0][0:columns, :]
    core.bank_read[0] = copied = copy_out(core, act, kiw_turned, core.bank[0][0:columns, :], summed)
    gather("kvi", kvi, BANK, True, lambda: next(scaling, None))
    pe.wait(copied, core.bank_read[4])
    for t in range(TT):
        step = pe.engine.transpose(core.bank[4][:, t * columns:(t + 1) * columns], kiw_turned[:, t * P:t * P + P],
                                   ident[0:columns, 0:columns])
    core.bank_read[4] = copy_out(core, act, kiw[:, :, :], core.bank[4][:, 0:TT * columns].rearrange("p (t c) -> p t c", t=TT),
                                 [pe.mark(step)])
    made["kiw"] = [core.bank_read[4]]

    attended = q
    highest = small[:, 3, 0:32]
    items = [(t, h) for t in range(TT) for h in range(A_HEADS)]
    powered, turned_of, applied, bias_ready = {}, {}, {}, {}
    attended_ready, index_used = [], [None, None]
    total = keep.head_scale[:, 0:len(items)]

    def score(i):
        t, h = items[i]
        n = (t + 1) * P
        b = 4 + i % 2
        pe.wait(core.bank_read[b], *keys_ready, *q_turned_ready)
        scored = pe.mark(pe.engine.matmul(core.bank[b][:, 0:n], q_turned[:, h // 2, t * P:t * P + P],
                                          keys[:, 2 * (h // 4) + h % 2, 0:n], start=True, stop=True))
        s = weights[i % 2][:, 0:n]
        dve.wait(scored, turned_of.get(i - 2), bias_ready[t])
        core.bank_read[b] = dve.mark(v.tensor_tensor_reduce(
            out=s, in0=core.bank[b][:, 0:n], in1=bias[:, t, 0:n], scale=1.0, scalar=-3e38, op0=ALU.add, op1=ALU.max,
            accum_out=highest[:, i:i + 1]))
        dve.wait(core.bank_read[b])
        negated = dve.mark(v.tensor_scalar(highest[:, i:i + 1], highest[:, i:i + 1], -1.0, None, ALU.mult))
        act.wait(negated)
        powered[i] = act.mark(act.engine.activation(s, s, ACT.Exp, bias=highest[:, i:i + 1], accum_out=total[:, i:i + 1]))

    def apply(i):
        t, h = items[i]
        n = (t + 1) * P
        b = 6
        pe.wait(powered[i], core.bank_read[b])
        for j in range(t + 1):
            step = pe.engine.transpose(core.bank[b][:, j * P:j * P + P], weights[i % 2][:, j * P:j * P + P], ident)
        turned_of[i] = pe.mark(step)
        core.bank_read[b] = copied = copy_out(core, act, turned_weights[i % 2][:, 0:n], core.bank[b][:, 0:n],
                                              [turned_of[i], applied.get(i - 2)])
        return copied

    def multiply(i, copied):
        t, h = items[i]
        out = 7
        pe.wait(copied)
        if h == 0:
            pe.wait(core.bank_read[out])
        group = h // (A_HEADS // KV_HEADS)
        for j in range(t + 1):
            step = pe.engine.matmul(core.bank[out][:, h * HEAD_DIM:(h + 1) * HEAD_DIM], turned_weights[i % 2][:, j * P:j * P + P],
                                    kvi[:, j, P + group * HEAD_DIM:P + (group + 1) * HEAD_DIM], start=(j == 0), stop=(j == t))
        applied[i] = pe.mark(step)
        if h == A_HEADS - 1:
            part = attended[:, t, :].rearrange("p (h d) -> p h d", h=A_HEADS)
            dve.wait(powered[i])
            inverse = dve.mark(v.reciprocal(total[:, t * 8:t * 8 + 8], total[:, t * 8:t * 8 + 8]))
            dve.wait(inverse, applied[i], *made["z_a"])
            core.bank_read[out] = dve.mark(v.tensor_tensor(
                part, core.bank[out][:, :].rearrange("p (h d) -> p h d", h=A_HEADS),
                total[:, t * 8:t * 8 + 8].unsqueeze(2).broadcast_to([P, A_HEADS, HEAD_DIM]), ALU.mult))
            dve.wait(core.bank_read[out])
            attended_ready.append([dve.mark(v.tensor_tensor(attended[:, t, :], attended[:, t, :], z_a[:, t, :], ALU.mult))])

    def choices():
        yield from keys_and_index()
        assert K_SEL >= P
        bias_ready[0] = dve.mark(v.tensor_copy(bias[:, 0, 0:P], allowed[:, T - P:T]))
        scores = {t: bias[:, t, 0:(t + 1) * P] for t in range(1, TT)}

        def scoring():
            for t in range(1, TT):
                yield from index_scores(core, t, allowed, index_q, index_k, weight, scores[t], relus, index_used, 6, index_ready)

        following = scoring()
        for _ in range(IDX_HEADS):
            yield next(following)
        for t in range(1, TT):
            for n, cost in enumerate(choose_keys(core, t, allowed, scores[t], totals, top, bias_ready)):
                if n % 2:
                    cost += next(following, 0)
                yield cost

    def attention():
        yield from norm_heads(core, q[:, :, :], A_HEADS, head_gain[:, 0, :], square, small, made["q"] + [gains_ready])
        rotated = rotate(core, q[:, :, :], A_HEADS, HEAD_DIM, 8, cosine, sine, 0, rotary_work)
        yield 5.5
        for c in range(4):
            q_turned_ready.append(turn_out(lambda t: q[:, t, c * P:c * P + P],
                                           lambda bank, turned: copy_out(core, act, q_turned[:, c, :], bank[:, :], [turned]),
                                           [rotated]))
            yield 0.1

        copied = {}
        for i in range(len(items) + 2):
            if i < len(items):
                while items[i][0] not in bias_ready:
                    yield next(choosing)
                score(i)
                yield 0.3 + (items[i][0] + 1) * P / 1000
            if 0 <= i - 1 < len(items):
                copied[i - 1] = apply(i - 1)
                yield 0.2
            if 0 <= i - 2 < len(items):
                multiply(i - 2, copied[i - 2])

    pooled_ready = []

    def pooling():
        for buffer in summing:
            dve.mark(v.memset(buffer[:, 0:16], 0.0))
        for g, window in enumerate(POOL_WINDOWS):
            now, other = summing
            act.wait(dve.latest())
            copied = act.mark(act.engine.activation(now[:, 16:16 + T], pooled[:, g, :], ACT.Copy))
            dve.wait(copied, dve.latest())
            yield 0.1
            step = 1
            while step < window:
                dve.wait(dve.mark(v.tensor_tensor(other[:, 16:16 + T], now[:, 16:16 + T], now[:, 16 - step:16 + T - step], ALU.add)))
                now, other = other, now
                step *= 2
            yield 0.65 * (g + 1)
            dve.wait(dve.mark(v.tensor_tensor(now[:, 16:16 + 16], now[:, 16:16 + 16], pool_start[:, 16 * g:16 * g + 16], ALU.mult)))
            dve.mark(v.tensor_tensor(pooled[:, g, 0:16], now[:, 16:16 + 16], pooled[:, g, 0:16], ALU.subtract))
            pooled_ready.append(dve.mark(v.scalar_tensor_tensor(
                out=pooled[:, g, 16:T], in0=now[:, 32:16 + T], scalar=1.0 / window, in1=pooled[:, g, 16:T],
                op0=ALU.mult, op1=ALU.subtract)))
            yield 1.0

    mixed_ready = []

    def mixing():
        yield from pools
        b = 6
        for g in range(4):
            pe.wait(core.bank_read[b], pooled_ready[g])
            multiplied = pe.mark(pe.engine.matmul(core.bank[b][:, :], pool_weights[:, g, :], pooled[:, g, :], start=True, stop=True))
            dve.wait(multiplied, *made["z_b"])
            core.bank_read[b] = dve.mark(v.scalar_tensor_tensor(
                out=mixed[:, g, :], in0=core.bank[b][:, :], scalar=pool_scale[:, g:g + 1], in1=mixed[:, g, :],
                op0=ALU.mult, op1=ALU.mult))
            mixed_ready.append(core.bank_read[b])
            yield 0.7

    choosing, attending, pools, mixes = choices(), attention(), pooling(), mixing()

    spare = [0.0]

    def between(*works):
        def pieces():
            spare[0] = min(spare[0] + SPARE, SPARE)
            for work in works:
                if spare[0] > 0:
                    spare[0] -= next(work, 0)
        return pieces

    gather("u_b", pooled, BANK, False, between(choosing, choosing, choosing))
    gather("z_b", mixed, BANK, False, between(pools, choosing), ACT.Silu)
    gather("z_a", z_a, BANK, True, between(pools, choosing), ACT.Silu)
    gather("q", q, BANK, True, between(mixes, choosing))

    late = Region(nc, keep.scores_at)
    a_high = late.tensor("a_high", [P, 4, T], F32R)
    a_low = late.tensor("a_low", [P, 4, T], F32R)
    late.at = keep.scores_at + 4 * 8192
    y_low = late.tensor("y_low", [P, KT, T], F32R)
    assert late.at == keep.values_at
    over_index = Region(nc, index_at)
    b_high = over_index.tensor("b_high", [P, 4, T], F32R)
    b_low = over_index.tensor("b_low", [P, 4, T], F32R)
    assert over_index.at <= turned_at
    y_high = Region(nc, keep.rows_at).tensor("y_high", [P, KT, T], F32R)
    y_ready, combined_read = {}, None

    def open_gate(branch, i, half, source, ready):
        column = branch * KT + half * 4 + i
        act.wait(*ready)
        return act.mark(act.engine.activation(gate[branch][:, i, :], source, ACT.Sigmoid,
                                              bias=merge_bias[:, column:column + 1]))

    for half in range(2):
        for branch in range(2):
            summed = project(core, stream, KT, BANK, (h_high, h_low), h_ready, False, range(4),
                             between(mixes, attending, choosing, attending))
            for i in range(4):
                if half == 0:
                    core.bank_read[i] = moved = copy_out(core, act, gate[branch][:, i, :], core.bank[i][:, :], [summed[i]])
                else:
                    core.bank_read[i] = gate_ready = open_gate(branch, i, half, core.bank[i][:, :], [summed[i], combined_read])
        if half == 0:
            for work in (choosing, mixes):
                for _ in work:
                    pass
            act.wait(*mixed_ready, pe.latest())
            dve.wait(*mixed_ready, pe.latest())
            b_ready = {}
            for k in range(4):
                b_ready[k] = split_pair(core, mixed[:, k, :], b_high[:, k, :], b_low[:, k, :], [mixed_ready[k]])
        summed_b = project(core, stream, 4, BANK, (b_high, b_low), b_ready, False, range(4), between(attending, attending, attending))
        if half == 0:
            for _ in attending:
                pass
            act.wait(pe.latest())
            dve.wait(pe.latest())
            a_ready = turn_to_pair(core, attended, a_high, a_low, range(4), ident, attended_ready, range(4, 8))
            read = [mark for marks in (*a_ready.values(), *b_ready.values()) for mark in marks]
            act.wait(*read)
            dve.wait(*read)
            for branch in (1, 0):
                for i in range(4):
                    gate_ready = open_gate(branch, i, half, gate[branch][:, i, :], [moved])
        for i in range(4):
            dve.wait(summed_b[i], gate_ready)
            core.bank_read[i] = dve.mark(v.tensor_tensor(gate[1][:, i, :], core.bank[i][:, :], gate[1][:, i, :], ALU.mult))
        summed = project(core, stream, 4, BANK, (a_high, a_low), a_ready, False, range(4, 8))
        for i in range(4):
            b, k = 4 + i, half * 4 + i
            dve.wait(summed[i], gate_ready)
            core.bank_read[b] = dve.mark(v.tensor_tensor(gate[0][:, i, :], core.bank[b][:, :], gate[0][:, i, :], ALU.mult))
            dve.wait(core.bank_read[b])
            added = dve.mark(v.tensor_tensor(gate[0][:, i, :], gate[0][:, i, :], gate[1][:, i, :], ALU.add))
            y_ready[k] = split_pair(core, gate[0][:, i, :], y_high[:, k, :], y_low[:, k, :], [added])
        combined_read = y_ready[k][1]
    stored = Signal(nc, "out_stored")
    for half in range(2):
        banks = [4 * half + i for i in range(4)]
        summed = project(core, stream, KT, BANK, (y_high, y_low), y_ready, True, banks)
        for t, b in enumerate(banks):
            part = x[:, t, half * BANK:(half + 1) * BANK]
            dve.wait(summed[t])
            core.bank_read[b] = written = dve.mark(v.tensor_tensor(part, part, core.bank[b][:, :], ALU.add))
            sp.wait(written)
            done = stored.after(sp.engine.dma_start(dram["out"].rearrange("(t p) d -> t p d", p=P)[t][:, half * BANK:(half + 1) * BANK], part), 16)
    sp.wait(done)


OUTPUT = "out"


def program(nc, dram):
    dram["gates"] = nc.dram_tensor("gates_scratch", [T // GATE_CHUNK, P, N_KEYS, GATE_CHUNK], F32).ap()
    dram["hidden"] = nc.dram_tensor("hidden_scratch", [N_KEYS, P, T], F32).ap()
    core = Core(nc)
    keep = Kept(core, dram)
    block_one_mixing(core, dram, keep)
    block_two(core, dram, keep, peer(core, dram, keep))


def kernel(**inputs):
    import numpy as _np
    import concourse.bacc as _bacc
    from concourse import mybir as _mybir
    from concourse.bass_utils import run_bass_kernel_spmd as _run

    a = {name: _np.asarray(value) for name, value in inputs.items()}

    def columns(vector):
        return vector.reshape(-1, P).T

    laid = {
        "x": a["x"][0],
        "norm_mix_g": columns(a["norm_mix_g"][0]),
        "norm_ffn_g": columns(a["norm_ffn_g"][0]),
        "norm_g_2": columns(a["norm_g_2"][0]),
        "final_norm_g": a["final_norm_g"],
        "w_in": a["w_in"][0],
        "w_out": a["w_out"][0],
        "diff_lambda": a["diff_lambda"][0],
        "diff_subln_g": a["diff_subln_g"][0],
        "peer_wq": a["peer_wq"][0],
        "subkeys": a["peer_subkeys"][0].reshape(HP, N_KEYS, P).transpose(2, 0, 1),
        "peer_u": a["peer_u"][0].reshape(N_KEYS, N_KEYS, KT, P).transpose(1, 3, 2, 0),
        "peer_v": a["peer_v"][0].reshape(N_KEYS, N_KEYS, D),
        "positions": a["positions_2"].reshape(TT, P).T,
        "w_in_2": a["w_in_2"][0],
        "merge_bias": columns(a["merge_bias_2"][0].reshape(-1)),
        "q_norm_g": a["q_norm_g_2"][0],
        "k_norm_g": a["k_norm_g_2"][0],
        "pool_w": a["pool_w_2"][0].transpose(1, 0, 2),
        "pool_scale": columns(a["pool_scale_2"][0]),
        "w_branch_a": a["w_branch_a_2"][0],
        "w_branch_b": a["w_branch_b_2"][0],
        "w_out_2": a["w_out_2"][0],
    }
    laid.update(constants())
    nc = _bacc.Bacc("TRN2", target_bir_lowering=False, num_devices=1)
    arrays, dram = {}, {}
    for name, array in laid.items():
        array = _np.ascontiguousarray(array)
        arrays[f"in_{name}"] = array
        dram[name] = nc.dram_tensor(f"in_{name}", array.shape, _mybir.dt.from_np(array.dtype), kind="ExternalInput").ap()
    dram[OUTPUT] = nc.dram_tensor("result", (T, D), F32, kind="ExternalOutput").ap()
    program(nc, dram)
    result = _run(nc, [arrays], core_ids=[0]).results[0]["result"]
    return result.reshape(1, T, D)
```
